# Optimizing a Trainium2 kernel written in Bass

```python
import jax, jax.numpy as jnp
from jax import lax
import numpy as np

D_MODEL = 1024
BATCH = 1
SEQ = 1024
DEPTH = 1

CHUNK = 64
RET_HEADS = 4
RET_DK = 128
RET_DV = 128
D_RET_QK = RET_HEADS * RET_DK
D_RET = RET_HEADS * RET_DV
MLSTM_HEADS = 4
MLSTM_D = 128
D_MLSTM = MLSTM_HEADS * MLSTM_D
D_MIX = D_RET + D_MLSTM
CONV_W = 4
ROPE_BASE = 10000.0
PEER_HEADS = 8
PEER_NKEYS = 128
PEER_TOPK = 16
PEER_DKEY = 256
PEER_N = PEER_NKEYS * PEER_NKEYS
PEER_BLOCK = 128
EPS = 1e-6
PROJ_SIZES = (D_RET_QK, D_RET_QK, D_RET, D_RET, D_MLSTM, D_MLSTM, D_MLSTM, MLSTM_HEADS, MLSTM_HEADS)
D_IN_PROJ = sum(PROJ_SIZES)

kernel_name = "retention_mlstm_peer_hybrid"

def rms_norm(x, g):
    xf = x.astype(jnp.float32)
    y = xf * lax.rsqrt(jnp.mean(xf * xf, axis=-1, keepdims=True) + EPS)
    return (y * g.astype(jnp.float32)).astype(x.dtype)

def head_group_norm(h, g):
    mu = jnp.mean(h, axis=-1, keepdims=True)
    var = jnp.mean(jnp.square(h - mu), axis=-1, keepdims=True)
    return (h - mu) * lax.rsqrt(var + EPS) * g.astype(jnp.float32)

def rotary(t, pos):
    half = t.shape[-1] // 2
    inv = ROPE_BASE ** (-jnp.arange(half, dtype=jnp.float32) / half)
    ang = pos.astype(jnp.float32)[:, None] * inv[None, :]
    cos = jnp.cos(ang)[None, :, None, :]
    sin = jnp.sin(ang)[None, :, None, :]
    t1, t2 = t[..., :half], t[..., half:]
    return jnp.concatenate([t1 * cos - t2 * sin, t1 * sin + t2 * cos], axis=-1)

def to_chunks(t):
    b, s, h, d = t.shape
    return t.reshape(b, s // CHUNK, CHUNK, h, d).transpose(1, 0, 3, 2, 4)

def from_chunks(t):
    nc, b, h, l, d = t.shape
    return t.transpose(1, 0, 3, 2, 4).reshape(b, nc * l, h, d)

def causal_dwconv(x, w, b):
    s = x.shape[1]
    xp = jnp.pad(x, ((0, 0), (CONV_W - 1, 0), (0, 0)))
    y = b + xp[:, 0:s] * w[0]
    for j in range(1, CONV_W):
        y = y + xp[:, j:j + s] * w[j]
    return y

def retention(q, k, v):
    b, _, h, dk = q.shape
    dv = v.shape[-1]
    log_g = jnp.log(1.0 - 2.0 ** (-5.0 - jnp.arange(h, dtype=jnp.float32)))
    l = jnp.arange(CHUNK, dtype=jnp.float32)
    intra_decay = jnp.exp(log_g[:, None, None] * jnp.abs(l[:, None] - l[None, :]))
    q_decay = jnp.exp(log_g[:, None] * (l + 1.0))[None, :, :, None]
    k_decay = jnp.exp(log_g[:, None] * (CHUNK - 1.0 - l))[None, :, :, None]
    chunk_decay = jnp.exp(log_g * CHUNK)[None, :, None, None]
    qc, kc, vc = to_chunks(q), to_chunks(k), to_chunks(v)
    scores = jnp.einsum('cbhld,cbhmd->cbhlm', qc, kc) * intra_decay
    o_intra = jnp.einsum('cbhlm,cbhmv->cbhlv', scores, vc)

    def step(state, inp):
        q_c, k_c, v_c = inp
        cross = jnp.einsum('bhld,bhdv->bhlv', q_c, state) * q_decay
        state = chunk_decay * state + jnp.einsum('bhld,bhlv->bhdv', k_c * k_decay, v_c)
        return state, cross

    state0 = jnp.zeros((b, h, dk, dv), jnp.float32)
    _, o_cross = lax.scan(step, state0, (qc, kc, vc))
    return from_chunks(o_intra + o_cross)

def mlstm(q, k, v, i_pre, log_f):
    b, s, h, d = q.shape
    nc = s // CHUNK
    qc, kc, vc = to_chunks(q), to_chunks(k), to_chunks(v)
    ic = i_pre.reshape(b, nc, CHUNK, h).transpose(1, 0, 3, 2)
    fc = log_f.reshape(b, nc, CHUNK, h).transpose(1, 0, 3, 2)
    f_cum = jnp.cumsum(fc, axis=-1)
    a = f_cum[..., -1]
    logw = a[..., None] - f_cum + ic
    m_in = jnp.max(logw, axis=-1)

    def step(carry, inp):
        c_mem, n_mem, m = carry
        q_c, k_c, v_c, logw_c, a_c, m_in_c = inp
        m_new = jnp.maximum(a_c + m, m_in_c)
        decay = jnp.exp(a_c + m - m_new)
        w = jnp.exp(logw_c - m_new[..., None])
        c_mem = decay[..., None, None] * c_mem + jnp.einsum('bhs,bhsk,bhsv->bhkv', w, k_c, v_c)
        n_mem = decay[..., None] * n_mem + jnp.einsum('bhs,bhsk->bhk', w, k_c)
        num = jnp.einsum('bhlk,bhkv->bhlv', q_c, c_mem)
        den = jnp.maximum(jnp.abs(jnp.einsum('bhlk,bhk->bhl', q_c, n_mem)),
                          jnp.exp(-m_new)[..., None])
        return (c_mem, n_mem, m_new), num / den[..., None]

    init = (jnp.zeros((b, h, d, d), jnp.float32),
            jnp.zeros((b, h, d), jnp.float32),
            jnp.zeros((b, h), jnp.float32))
    _, hc = lax.scan(step, init, (qc, kc, vc, logw, a, m_in))
    return from_chunks(hc)

def peer(xn, wq, keys, down, up):
    b, s, d = xn.shape
    t = b * s
    xt = xn.reshape(t, d)
    q = (xt @ wq).reshape(t, PEER_HEADS, 2, PEER_DKEY // 2).astype(jnp.float32)
    sub = jnp.einsum('thpd,hpnd->thpn', q, keys.astype(jnp.float32))
    s_top, i_top = lax.top_k(sub, PEER_TOPK)
    cand = (s_top[:, :, 0, :, None] + s_top[:, :, 1, None, :]).reshape(t, PEER_HEADS, PEER_TOPK * PEER_TOPK)
    best, flat = lax.top_k(cand, PEER_TOPK)
    i1 = jnp.take_along_axis(i_top[:, :, 0, :], flat // PEER_TOPK, axis=-1)
    i2 = jnp.take_along_axis(i_top[:, :, 1, :], flat % PEER_TOPK, axis=-1)
    expert = i1 * PEER_NKEYS + i2
    gates = jax.nn.softmax(best, axis=-1)
    nb = t // PEER_BLOCK
    e_per_tok = PEER_HEADS * PEER_TOPK
    xb = xt.reshape(nb, PEER_BLOCK, d)
    eb = expert.reshape(nb, PEER_BLOCK, e_per_tok)
    gb = gates.astype(xt.dtype).reshape(nb, PEER_BLOCK, e_per_tok)

    def block(args):
        xi, ei, gi = args
        u = jnp.take(down, ei, axis=0)
        act = jax.nn.gelu(jnp.einsum('td,ted->te', xi, u), approximate=False)
        vv = jnp.take(up, ei, axis=0)
        return jnp.einsum('te,ted->td', gi * act, vv)

    out = lax.map(block, (xb, eb, gb))
    return out.reshape(b, s, d)

def hybrid_layer(x, norm1_g, w_in, ret_norm_g, m_conv_w, m_conv_b, m_wq, m_wk,
                 m_b_i, m_b_f, m_norm_g, m_skip, w_out, norm2_g,
                 peer_wq, peer_keys, peer_down, peer_up):
    f32 = jnp.float32
    b, s, _ = x.shape
    pos = jnp.arange(s, dtype=jnp.int32)
    h = rms_norm(x, norm1_g)
    proj = h @ w_in
    split_idx = [int(v) for v in np.cumsum(PROJ_SIZES)[:-1]]
    rq, rk, rv, rg, mx, mv, mo, mi, mf = jnp.split(proj, split_idx, axis=-1)

    rq = rotary(rq.reshape(b, s, RET_HEADS, RET_DK).astype(f32), pos)
    rk = rotary(rk.reshape(b, s, RET_HEADS, RET_DK).astype(f32), pos) * (RET_DK ** -0.5)
    rv = rv.reshape(b, s, RET_HEADS, RET_DV).astype(f32)
    o_ret = head_group_norm(retention(rq, rk, rv), ret_norm_g).reshape(b, s, D_RET)
    y_ret = jax.nn.silu(rg.astype(f32)) * o_ret

    c = jax.nn.silu(causal_dwconv(mx, m_conv_w, m_conv_b)).astype(f32)
    ch = c.reshape(b, s, MLSTM_HEADS, MLSTM_D)
    mq = jnp.einsum('bshd,hde->bshe', ch, m_wq.astype(f32))
    mk = jnp.einsum('bshd,hde->bshe', ch, m_wk.astype(f32)) * (MLSTM_D ** -0.5)
    mvv = mv.reshape(b, s, MLSTM_HEADS, MLSTM_D).astype(f32)
    i_pre = mi.astype(f32) + m_b_i.astype(f32)
    log_f = jax.nn.log_sigmoid(mf.astype(f32) + m_b_f.astype(f32))
    hm = head_group_norm(mlstm(mq, mk, mvv, i_pre, log_f), m_norm_g).reshape(b, s, D_MLSTM)
    y_m = jax.nn.sigmoid(mo.astype(f32)) * (hm + m_skip.astype(f32) * c)

    y = jnp.concatenate([y_ret, y_m], axis=-1).astype(x.dtype) @ w_out
    x = x + y
    x = x + peer(rms_norm(x, norm2_g), peer_wq, peer_keys, peer_down, peer_up)
    return x

def setup_inputs(seed: int = 0) -> dict:
    key = jax.random.key(seed)
    ks = jax.random.split(key, 20)
    f32 = jnp.float32
    nrm = lambda k, shape: jax.random.normal(k, shape, f32)
    L = DEPTH
    return {
        "x": nrm(ks[0], (BATCH, SEQ, D_MODEL)),
        "norm1_g": 1.0 + 0.02 * nrm(ks[1], (L, D_MODEL)),
        "w_in": nrm(ks[2], (L, D_MODEL, D_IN_PROJ)) * D_MODEL ** -0.5,
        "ret_norm_g": 1.0 + 0.02 * nrm(ks[3], (L, RET_HEADS, RET_DV)),
        "m_conv_w": nrm(ks[4], (L, CONV_W, D_MLSTM)) * CONV_W ** -0.5,
        "m_conv_b": 0.02 * nrm(ks[5], (L, D_MLSTM)),
        "m_wq": nrm(ks[6], (L, MLSTM_HEADS, MLSTM_D, MLSTM_D)) * MLSTM_D ** -0.5,
        "m_wk": nrm(ks[7], (L, MLSTM_HEADS, MLSTM_D, MLSTM_D)) * MLSTM_D ** -0.5,
        "m_b_i": 0.1 * nrm(ks[8], (L, MLSTM_HEADS)),
        "m_b_f": jnp.linspace(3.0, 6.0, MLSTM_HEADS, dtype=f32)[None, :] + 0.1 * nrm(ks[9], (L, MLSTM_HEADS)),
        "m_norm_g": 1.0 + 0.02 * nrm(ks[10], (L, MLSTM_HEADS, MLSTM_D)),
        "m_skip": 1.0 + 0.02 * nrm(ks[11], (L, D_MLSTM)),
        "w_out": nrm(ks[12], (L, D_MIX, D_MODEL)) * D_MIX ** -0.5,
        "norm2_g": 1.0 + 0.02 * nrm(ks[13], (L, D_MODEL)),
        "peer_wq": nrm(ks[14], (L, D_MODEL, PEER_HEADS * PEER_DKEY)) * D_MODEL ** -0.5,
        "peer_keys": nrm(ks[15], (L, PEER_HEADS, 2, PEER_NKEYS, PEER_DKEY // 2)) * (PEER_DKEY // 2) ** -0.5,
        "peer_down": nrm(ks[16], (L, PEER_N, D_MODEL)) * D_MODEL ** -0.5,
        "peer_up": nrm(ks[17], (L, PEER_N, D_MODEL)) * PEER_HEADS ** -0.5,
        "final_g": 1.0 + 0.02 * nrm(ks[18], (D_MODEL,)),
    }

def reference(x, norm1_g, w_in, ret_norm_g, m_conv_w, m_conv_b, m_wq, m_wk,
              m_b_i, m_b_f, m_norm_g, m_skip, w_out, norm2_g,
              peer_wq, peer_keys, peer_down, peer_up, final_g):
    for i in range(DEPTH):
        x = hybrid_layer(x, norm1_g[i], w_in[i], ret_norm_g[i], m_conv_w[i], m_conv_b[i],
                         m_wq[i], m_wk[i], m_b_i[i], m_b_f[i], m_norm_g[i], m_skip[i],
                         w_out[i], norm2_g[i], peer_wq[i], peer_keys[i],
                         peer_down[i], peer_up[i])
    return rms_norm(x, final_g)


_drawn_inputs = setup_inputs


def setup_inputs(seed=0):
    import zlib

    import numpy as np

    out = dict(_drawn_inputs(seed))
    spreads = {}
    factors = {'ret_norm_g': 57.817,
     'm_conv_b': 2.883,
     'm_b_i': 64.0,
     'm_norm_g': 80.749,
     'm_skip': 100.172,
     'final_g': 24.388,
     'norm2_g': 20.234}
    for name, (base, spread) in spreads.items():
        noise = np.random.default_rng([zlib.crc32(name.encode()), seed]).standard_normal(out[name].shape)
        drawn = base * np.exp(spread * noise) if base else spread * noise
        out[name] = __import__('jax').numpy.asarray(drawn.astype(out[name].dtype))
    for name, factor in factors.items():
        out[name] = (out[name] * factor).astype(out[name].dtype)
    return out
```

```python
from contextlib import ExitStack

import concourse.bass as bass
from concourse import mybir

F32 = mybir.dt.float32
U32 = mybir.dt.uint32
ALU = mybir.AluOpType
ACT = mybir.ActivationFunctionType
AX = mybir.AxisListType.X

P = 128
EPS = 1e-6
CONV_W = 4
NEG = -3.0e38
PEER_HEADS = 8
TOPK = 16
DOWN_RING = 8


def retention_block_decay():
    return [float((1.0 - 2.0 ** (-5.0 - h)) ** P) for h in range(4)]


class Chain:

    def __init__(self, engine, sem):
        self.engine, self.sem, self.n = engine, sem, 0
        engine.sem_clear(sem)

    def __call__(self, instruction):
        self.n += 1
        instruction.then_inc(self.sem, 1)
        self.engine.wait_ge(self.sem, self.n)


def mix_stage(nc, io, x1_dram):
    D = io["x"].shape[1]
    T = io["x"].shape[0]
    KC = D // P
    NB = T // P
    H = 4
    W = H * P
    RQ, RK, RV, RG, MX, MV, MO, MI, MF = [W * i for i in range(7)] + [7 * W, 7 * W + H]
    gamma_p = retention_block_decay()

    with ExitStack() as ctx:
        def sb(name, shape, dt=F32):
            return ctx.enter_context(nc.sbuf_tensor(name, shape, dt))

        def bank(name):
            return ctx.enter_context(nc.psum_tensor(name, [P, 512], F32))

        def sem(name):
            return ctx.enter_context(nc.semaphore(name))

        w_in = sb("w_in_sb", [P, KC, 7 * W + 2 * H])
        w_out = sb("w_out_sb", [P, KC, D])
        mwq = sb("mwq", [P, H, P])
        mwk = sb("mwk", [P, H, P])
        ident = sb("ident", [P, P])
        decay_t = sb("decay_t", [P, H, P])
        select = sb("select", [H, H, P])
        reset = sb("reset", [H, P])
        half = sb("half", [P, 2])
        g1 = sb("g1", [P, KC])
        ret_g = sb("ret_g", [P, H])
        ml_g = sb("ml_g", [P, H])
        skip = sb("skip", [P, H])
        conv_w = sb("conv_w", [P, CONV_W, H])
        conv_b = sb("conv_b", [P, H])
        b_i = sb("b_i", [H, 1])
        b_f = sb("b_f", [H, 1])
        xa = sb("xa", [P, D])
        xr = sb("xr", [P, D])
        xs = sb("xs", [P, D])
        trig = sb("trig", [P, 4, 4 * 64])
        hT = sb("hT", [P, KC, P])
        ss = sb("ss", [P, 4])
        mxb = sb("mxb", [P, H, P + CONV_W - 1])
        cT = sb("cT", [P, H, P])
        sig = sb("sig", [P, H, P])
        srg = sb("srg", [P, H, P])
        smo = sb("smo", [P, H, P])
        qr = sb("qr", [P, H, P])
        kr = sb("kr", [P, H, P])
        v = sb("v", [P, H, P])
        v1 = sb("v1", [P, H, P])
        wv = sb("wv", [P, 2, H, P])
        qT = sb("qT", [P, H, P])
        kT = sb("kT", [P, H, P])
        gsb = sb("gsb", [P, 2 * H])
        gates = sb("gates", [H, 7, P])
        small = sb("small", [H, 24])
        cat = sb("cat", [H, 4])
        wtok = sb("wtok", [P, 2, H])
        bc = sb("bc", [P, H, 4])
        den = sb("den", [P, 4, H])
        stats = sb("stats", [P, 3, 2 * H])
        S = sb("S", [P, H, P])
        C = sb("C", [P, H, P])
        nm = sb("nm", [P, H])
        m_seq = sb("m_seq", [H, 3])
        G = xs[:, :].rearrange("p (h d) -> p h d", d=P)
        sq = trig[:, :, :].rearrange("p a c -> p (a c)")
        yT = hT
        rot = wv[:, :, :, :].rearrange("p c h d -> p (c h d)").rearrange("p (a h d) -> p a h d", a=4, d=64)
        scd, mqT, mk = qr, qT, kT

        P0, P1, TR0, TR1, RT, UP, NM, SM = [bank(f"bank{i}") for i in range(8)]
        hv = lambda t: t[:, :].rearrange("p (h d) -> p h d", d=P)
        sm_gate, sm_i, sm_f = SM[:, 0:8], SM[0:H, 16:144], SM[0:H, 144:272]
        sm_w, sm_bc = SM[:, 272:276], SM[:, 276:292]
        sm_n, sm_den = SM[:, 292:296], SM[:, 296:300]

        names = ("xs_done xT_ready hT_done gates_ready gsb_done mx_ready mx_copied conv_done "
                 "conv_exp cT_done gateT_ready gate_abs gate_log gate_diff gate_exp w_ready w_copied "
                 "rq_ready rq_read q_parts qr_done rk_ready rk_read k_parts kr_done "
                 "rv_ready v_copied mv_ready v1_copied qT_ready qT_copied kT_ready kT_copied "
                 "scores_ready scd_done rg_ready rg_exp srg_done o_ready o_copied s_ready s_done "
                 "mq_ready mqT_copied mk_ready mk_copied mo_ready mo_exp smo_done wv_done "
                 "c0_ready c0_done c1_ready c1_done num0_ready num1_ready hm_done mean_done sq_done "
                 "var_done ln_done rstd_done g_done yT_ready yr_done ym_done out_ready x1_done "
                 "ss_done eps_done dve_step act_step").split()
        e = {n: sem(n) for n in names}
        loaded = {n: sem("ld_" + n) for n in ("const", "small", "mx", "g", "rq", "rk", "rv", "mv", "rg", "mo", "out",
                                              "xa", "xr", "trig", "x1")}
        zeroed = sem("zeroed")
        block = ctx.enter_context(nc.Block())

        SMALL = 11

        @block.sync
        def _(sp):
            win = io["w_in"].rearrange("(k p) n -> p k n", p=P)
            sp.dma_start(xa[:, :], io["x"][0:P, :]).then_inc(loaded["xa"], 16)
            sp.dma_start(ident[:, :], io["ident"]).then_inc(loaded["const"], 16)
            with nc.allow_non_contiguous_dma(reason="small per-channel vectors"):
                sp.dma_start(g1[:, :], io["norm1_g"].rearrange("(k p) -> p k", p=P)).then_inc(loaded["small"], 16)
                sp.dma_start(w_in[:, :, MI:MI + 2 * H], win[:, :, MI:MI + 2 * H]).then_inc(loaded["g"], 16)
                sp.dma_start(w_in[:, :, MX:MX + W], win[:, :, MX:MX + W]).then_inc(loaded["mx"], 16)
                sp.dma_start(ret_g[:, :], io["ret_norm_g"].rearrange("h p -> p h")).then_inc(loaded["small"], 16)
                sp.dma_start(ml_g[:, :], io["m_norm_g"].rearrange("h p -> p h")).then_inc(loaded["small"], 16)
                sp.dma_start(skip[:, :], io["m_skip"].rearrange("(h p) -> p h", p=P)).then_inc(loaded["small"], 16)
                sp.dma_start(conv_b[:, :], io["m_conv_b"].rearrange("(h p) -> p h", p=P)).then_inc(loaded["small"], 16)
                for j in range(CONV_W):
                    sp.dma_start(conv_w[:, j, :], io["m_conv_w"][j].rearrange("(h p) -> p h", p=P)).then_inc(
                        loaded["small"], 16)
                sp.dma_start(b_i[:, :], io["m_b_i"].rearrange("(h a) -> h a", a=1)).then_inc(loaded["small"], 16)
                sp.dma_start(b_f[:, :], io["m_b_f"].rearrange("(h a) -> h a", a=1)).then_inc(loaded["small"], 16)
            sp.dma_start(reset[:, :], io["reset"]).then_inc(loaded["const"], 16)
            sp.dma_start(half[:, :], io["half"]).then_inc(loaded["const"], 16)
            sp.dma_start(select[:, :, :], io["select"]).then_inc(loaded["const"], 16)
            sp.dma_start(w_in[:, :, RQ:RQ + W], win[:, :, RQ:RQ + W]).then_inc(loaded["rq"], 16)
            sp.dma_start(trig[:, :, :], io["trig"][0:P, :, :]).then_inc(loaded["trig"], 16)
            sp.dma_start(w_in[:, :, RK:RK + W], win[:, :, RK:RK + W]).then_inc(loaded["rk"], 16)
            sp.dma_start(w_in[:, :, RV:RV + W], win[:, :, RV:RV + W]).then_inc(loaded["rv"], 16)
            sp.dma_start(decay_t[:, :, :], io["decay_t"]).then_inc(loaded["const"], 16)
            sp.dma_start(mwq[:, :, :], io["m_wq"].rearrange("h d e -> d h e")).then_inc(loaded["const"], 16)
            sp.dma_start(mwk[:, :, :], io["m_wk"].rearrange("h d e -> d h e")).then_inc(loaded["const"], 16)
            sp.dma_start(w_in[:, :, MV:MV + W], win[:, :, MV:MV + W]).then_inc(loaded["mv"], 16)
            sp.dma_start(w_in[:, :, RG:RG + W], win[:, :, RG:RG + W]).then_inc(loaded["rg"], 16)
            sp.dma_start(w_in[:, :, MO:MO + W], win[:, :, MO:MO + W]).then_inc(loaded["mo"], 16)
            sp.dma_start(w_out[:, :, :], io["w_out"].rearrange("(k p) n -> p k n", p=P)).then_inc(loaded["out"], 16)
            sp.dma_start(xr[:, :], io["x"][0:P, :]).then_inc(loaded["xr"], 16)
            with sp.Fori(1, NB) as b:
                sp.wait_ge(e["xs_done"], b)
                sp.dma_start(xa[:, :], io["x"][bass.ts(b, P), :]).then_inc(loaded["xa"], 16)
                sp.wait_ge(e["rstd_done"], b)
                sp.dma_start(trig[:, :, :], io["trig"][bass.ts(b, P), :, :]).then_inc(loaded["trig"], 16)
                sp.wait_ge(e["x1_done"], b)
                sp.dma_start(xr[:, :], io["x"][bass.ts(b, P), :]).then_inc(loaded["xr"], 16)

        @block.gpsimd
        def _(pool):
            nc.gpsimd.memset(mxb[:, :, :], 0.0).then_inc(zeroed, 1)
            nc.gpsimd.memset(S[:, :, :], 0.0).then_inc(zeroed, 1)
            nc.gpsimd.memset(C[:, :, :], 0.0).then_inc(zeroed, 1)
            nc.gpsimd.memset(nm[:, :], 0.0).then_inc(zeroed, 1)
            nc.gpsimd.memset(m_seq[:, :], 0.0).then_inc(zeroed, 1)
            with pool.Fori(0, NB) as b:
                for name, r in (("q", qr), ("k", kr)):
                    pool.wait_ge(e[name + "_parts"], b + 1)
                    nc.gpsimd.tensor_tensor(r[:, :, 0:64], rot[:, 0, :, :], rot[:, 1, :, :], ALU.subtract)
                    nc.gpsimd.tensor_tensor(r[:, :, 64:128], rot[:, 2, :, :], rot[:, 3, :, :], ALU.add).then_inc(
                        e[name + "r_done"], 1)
                pool.wait_ge(e["x1_done"], b + 1)
                pool.dma_start(x1_dram[bass.ts(b, P), :], xs[:, :]).then_inc(loaded["x1"], 16)
            pool.wait_ge(loaded["x1"], 16 * NB)

        @block.scalar
        def _(act):
            with act.Fori(0, NB) as b:
                step = Chain(act, e["act_step"])
                act.wait_ge(loaded["xa"], 16 * b + 16)
                nc.scalar.activation(xs[:, :], xa[:, :], ACT.Square, accum_out=ss[:, 0:1]).then_inc(e["ss_done"], 1)
                act.wait_ge(e["eps_done"], b + 1)
                step(nc.scalar.activation(ss[:, 2:3], ss[:, 1:2], ACT.Ln))
                step(nc.scalar.activation(ss[:, 3:4], ss[:, 2:3], ACT.Exp, scale=-0.5))
                nc.scalar.activation(xs[:, :], xa[:, :], ACT.Copy, scale=ss[:, 3:4]).then_inc(e["xs_done"], 1)
                act.wait_ge(e["mx_ready"], b + 1)
                nc.scalar.copy(mxb[:, :, CONV_W - 1:], hv(P0)).then_inc(e["mx_copied"], 1)
                act.wait_ge(e["gate_abs"], b + 1)
                step(nc.scalar.activation(gates[:, 2, :], gates[:, 1, :], ACT.Exp, scale=-1.0))
                nc.scalar.activation(gates[:, 3, :], gates[:, 2, :], ACT.Ln, bias=1.0).then_inc(e["gate_log"], 1)
                act.wait_ge(e["gate_diff"], b + 1)
                nc.scalar.activation(gates[:, 2, :], gates[:, 6, :], ACT.Exp)
                nc.scalar.activation(cat[:, 0:2], small[:, 8:10], ACT.Exp)
                nc.scalar.activation(cat[:, 2:4], small[:, 4:6], ACT.Exp, scale=-1.0).then_inc(e["gate_exp"], 1)
                act.wait_ge(e["conv_done"], b + 1)
                nc.scalar.activation(sig[:, :, :], cT[:, :, :], ACT.Exp, scale=-1.0).then_inc(e["conv_exp"], 1)
                act.wait_ge(e["rv_ready"], b + 1)
                nc.scalar.copy(v[:, :, :], hv(P1)).then_inc(e["v_copied"], 1)
                act.wait_ge(e["qT_ready"], b + 1)
                nc.scalar.copy(qT[:, :, :], hv(TR0)).then_inc(e["qT_copied"], 1)
                act.wait_ge(e["kT_ready"], b + 1)
                nc.scalar.copy(kT[:, :, :], hv(TR1)).then_inc(e["kT_copied"], 1)
                act.wait_ge(e["mv_ready"], b + 1)
                nc.scalar.copy(v1[:, :, :], hv(P0)).then_inc(e["v1_copied"], 1)
                act.wait_ge(e["rg_ready"], b + 1)
                nc.scalar.activation(srg[:, :, :], hv(P1), ACT.Exp, scale=-1.0).then_inc(e["rg_exp"], 1)
                act.wait_ge(e["mq_ready"], b + 1)
                nc.scalar.copy(mqT[:, :, :], hv(TR0)).then_inc(e["mqT_copied"], 1)
                act.wait_ge(e["mk_ready"], b + 1)
                nc.scalar.activation(mk[:, :, :], hv(TR1), ACT.Copy, scale=float(P) ** -0.5).then_inc(e["mk_copied"], 1)
                act.wait_ge(e["mo_ready"], b + 1)
                nc.scalar.activation(smo[:, :, :], hv(P0), ACT.Exp, scale=-1.0).then_inc(e["mo_exp"], 1)
                act.wait_ge(e["o_ready"], b + 1)
                nc.scalar.copy(G[:, 0:H, :], hv(RT)).then_inc(e["o_copied"], 1)
                act.wait_ge(e["mean_done"], b + 1)
                nc.scalar.activation(sq, xs[:, :], ACT.Square).then_inc(e["sq_done"], 1)
                act.wait_ge(e["var_done"], b + 1)
                nc.scalar.activation(stats[:, 1, :], stats[:, 2, :], ACT.Ln).then_inc(e["ln_done"], 1)
                act.wait_ge(e["ln_done"], b + 1)
                nc.scalar.activation(stats[:, 0, :], stats[:, 1, :], ACT.Exp, scale=-0.5).then_inc(e["rstd_done"], 1)
                act.wait_ge(loaded["x1"], 16 * b + 16)

        @block.vector
        def _(dve):
            V = nc.vector
            dve.wait_ge(zeroed, 5)
            dve.wait_ge(loaded["small"], 16 * SMALL)
            dve.wait_ge(loaded["const"], 16 * 7)
            with dve.Fori(0, NB) as b:
                step = Chain(dve, e["dve_step"])
                dve.wait_ge(e["ss_done"], b + 1)
                V.tensor_scalar(ss[:, 1:2], ss[:, 0:1], 1.0 / D, EPS, ALU.mult, ALU.add).then_inc(e["eps_done"], 1)
                dve.wait_ge(e["xT_ready"], b + 1)
                for k2, bk in enumerate((TR0, TR1)):
                    gain = g1[:, 4 * k2:4 * k2 + 4].unsqueeze(2).broadcast_to([P, 4, P])
                    last = V.tensor_tensor(hT[:, 4 * k2:4 * k2 + 4, :], hv(bk), gain, ALU.mult)
                last.then_inc(e["hT_done"], 1)
                dve.wait_ge(e["gates_ready"], b + 1)
                V.tensor_copy(gsb[:, :], sm_gate).then_inc(e["gsb_done"], 1)
                dve.wait_ge(e["gateT_ready"], b + 1)
                step(V.tensor_scalar(gates[:, 0, :], sm_f, b_f[:, 0:1], None, ALU.add))
                step(V.tensor_scalar(gates[:, 4, :], sm_i, b_i[:, 0:1], None, ALU.add))
                V.scalar_tensor_tensor(gates[:, 1, :], gates[:, 0, :], -1.0, gates[:, 0, :], ALU.mult,
                                       ALU.max).then_inc(e["gate_abs"], 1)
                dve.wait_ge(e["gate_log"], b + 1)
                step(V.scalar_tensor_tensor(gates[:, 5, :], gates[:, 0, :], 0.0, gates[:, 3, :], ALU.min, ALU.subtract))
                step(V.tensor_tensor_scan(gates[:, 1, :], reset[:, :], gates[:, 5, :], 0.0, ALU.mult, ALU.add))
                step(V.tensor_copy(small[:, 0:2], gates[:, 1, 63:128:64]))
                step(V.tensor_tensor(gates[:, 4, :], gates[:, 4, :], gates[:, 1, :], ALU.subtract))
                g2v = lambda i: gates[:, i, :].rearrange("h (c l) -> h c l", l=64)
                a_wide = small[:, 0:2].unsqueeze(2).broadcast_to([H, 2, 64])
                step(V.tensor_tensor(g2v(5), g2v(4), a_wide, ALU.add))
                step(V.tensor_reduce(small[:, 2:4], g2v(5), AX, ALU.max))
                step(V.tensor_tensor_scan(m_seq[:, 1:3], small[:, 0:2], small[:, 2:4], m_seq[:, 0:1], ALU.add, ALU.max))
                step(V.tensor_tensor(small[:, 6:8], small[:, 0:2], m_seq[:, 0:2], ALU.add))
                step(V.tensor_tensor(small[:, 8:10], small[:, 6:8], m_seq[:, 1:3], ALU.subtract))
                step(V.tensor_copy(small[:, 4:6], m_seq[:, 1:3]))
                m_wide = small[:, 4:6].unsqueeze(2).broadcast_to([H, 2, 64])
                step(V.tensor_tensor(g2v(6), g2v(5), m_wide, ALU.subtract))
                V.tensor_copy(m_seq[:, 0:1], small[:, 5:6]).then_inc(e["gate_diff"], 1)
                dve.wait_ge(e["mx_copied"], b + 1)
                for h in range(H):
                    last = V.tensor_scalar(cT[:, h, :], mxb[:, h, 0:P], conv_w[:, 0, h:h + 1], conv_b[:, h:h + 1],
                                           ALU.mult, ALU.add)
                step(last)
                for j in range(1, CONV_W):
                    for h in range(H):
                        last = V.scalar_tensor_tensor(cT[:, h, :], mxb[:, h, j:j + P], conv_w[:, j, h:h + 1],
                                                      cT[:, h, :], ALU.mult, ALU.add)
                    if j < CONV_W - 1:
                        step(last)
                last.then_inc(e["conv_done"], 1)
                dve.wait_ge(e["conv_done"], b + 1)
                V.tensor_copy(mxb[:, :, 0:CONV_W - 1], mxb[:, :, P:])
                dve.wait_ge(e["conv_exp"], b + 1)
                step(V.tensor_scalar(sig[:, :, :], sig[:, :, :], 1.0, None, ALU.add))
                step(V.reciprocal(sig[:, :, :], sig[:, :, :]))
                V.tensor_tensor(cT[:, :, :], cT[:, :, :], sig[:, :, :], ALU.mult).then_inc(e["cT_done"], 1)
                dve.wait_ge(loaded["trig"], 16 * b + 16)
                for name, bk, t0 in (("q", P1, 0), ("k", P0, 2)):
                    dve.wait_ge(e[f"r{name}_ready"], b + 1)
                    if name == "k":
                        dve.wait_ge(e["qr_done"], b + 1)
                    cos = trig[:, t0, :].rearrange("p (h d) -> p h d", h=H)
                    sin = trig[:, t0 + 1, :].rearrange("p (h d) -> p h d", h=H)
                    lo, hi = hv(bk)[:, :, 0:64], hv(bk)[:, :, 64:128]
                    V.tensor_tensor(rot[:, 0, :, :], lo, cos, ALU.mult)
                    V.tensor_tensor(rot[:, 1, :, :], hi, sin, ALU.mult)
                    V.tensor_tensor(rot[:, 2, :, :], lo, sin, ALU.mult)
                    V.tensor_tensor(rot[:, 3, :, :], hi, cos, ALU.mult).then_inc(e[name + "_parts"], 1)
                dve.wait_ge(e["w_ready"], b + 1)
                for c in range(2):
                    V.tensor_scalar(wtok[:, c, :], sm_w, half[:, c:c + 1], None, ALU.mult)
                V.tensor_copy(bc[:, :, :], sm_bc.rearrange("p (h c) -> p h c", h=H)).then_inc(e["w_copied"], 1)
                dve.wait_ge(e["scores_ready"], b + 1)
                V.tensor_tensor(scd[:, :, :], hv(RT), decay_t[:, :, :], ALU.mult).then_inc(e["scd_done"], 1)
                dve.wait_ge(e["w_copied"], b + 1)
                dve.wait_ge(e["v1_copied"], b + 1)
                for c in range(2):
                    last = V.tensor_tensor(wv[:, c, :, :], v1[:, :, :],
                                           wtok[:, c, :].unsqueeze(2).broadcast_to([P, H, P]), ALU.mult)
                last.then_inc(e["wv_done"], 1)
                dve.wait_ge(e["rg_exp"], b + 1)
                step(V.tensor_scalar(srg[:, :, :], srg[:, :, :], 1.0, None, ALU.add))
                step(V.reciprocal(srg[:, :, :], srg[:, :, :]))
                V.tensor_tensor(srg[:, :, :], hv(P1), srg[:, :, :], ALU.mult).then_inc(e["srg_done"], 1)
                dve.wait_ge(e["s_ready"], b + 1)
                for h in range(H):
                    last = V.scalar_tensor_tensor(S[:, h, :], S[:, h, :], gamma_p[h], hv(UP)[:, h, :], ALU.mult, ALU.add)
                last.then_inc(e["s_done"], 1)
                dve.wait_ge(e["mo_exp"], b + 1)
                step(V.tensor_scalar(smo[:, :, :], smo[:, :, :], 1.0, None, ALU.add))
                V.reciprocal(smo[:, :, :], smo[:, :, :]).then_inc(e["smo_done"], 1)
                for c in range(2):
                    dve.wait_ge(e[f"c{c}_ready"], b + 1)
                    if c == 1:
                        dve.wait_ge(e["num0_ready"], b + 1)
                    for h in range(H):
                        V.scalar_tensor_tensor(C[:, h, :], C[:, h, :], bc[:, h, c:c + 1], hv(UP)[:, h, :],
                                               ALU.mult, ALU.add)
                    step(V.tensor_tensor(nm[:, :], nm[:, :], bc[:, :, c], ALU.mult))
                    V.tensor_tensor(nm[:, :], nm[:, :], sm_n, ALU.add).then_inc(e[f"c{c}_done"], 1)
                dve.wait_ge(e["num1_ready"], b + 1)
                V.tensor_copy(den[0:64, 2, :], bc[0:64, :, 2])
                V.tensor_copy(den[64:128, 2, :], bc[64:128, :, 3])
                step(V.tensor_copy(den[:, 0, :], sm_den))
                step(V.scalar_tensor_tensor(den[:, 1, :], den[:, 0, :], -1.0, den[:, 0, :], ALU.mult, ALU.max))
                step(V.tensor_tensor(den[:, 1, :], den[:, 1, :], den[:, 2, :], ALU.max))
                step(V.reciprocal(den[:, 3, :], den[:, 1, :]))
                V.tensor_tensor(G[:, H:2 * H, :], hv(NM), den[:, 3, :].unsqueeze(2).broadcast_to([P, H, P]),
                                ALU.mult).then_inc(e["hm_done"], 1)
                dve.wait_ge(e["hm_done"], b + 1)
                dve.wait_ge(e["o_copied"], b + 1)
                step(V.tensor_reduce(stats[:, 0, :], G, AX, ALU.add))
                step(V.tensor_scalar(stats[:, 1, :], stats[:, 0, :], 1.0 / P, None, ALU.mult))
                V.tensor_tensor(G, G, stats[:, 1, :].unsqueeze(2).broadcast_to([P, 2 * H, P]),
                                ALU.subtract).then_inc(e["mean_done"], 1)
                dve.wait_ge(e["sq_done"], b + 1)
                step(V.tensor_reduce(stats[:, 0, :], sq.rearrange("p (h d) -> p h d", d=P), AX, ALU.add))
                V.tensor_scalar(stats[:, 2, :], stats[:, 0, :], 1.0 / P, EPS, ALU.mult, ALU.add).then_inc(
                    e["var_done"], 1)
                dve.wait_ge(e["rstd_done"], b + 1)
                V.tensor_tensor(G, G, stats[:, 0, :].unsqueeze(2).broadcast_to([P, 2 * H, P]),
                                ALU.mult).then_inc(e["g_done"], 1)
                for h in range(H):
                    last = V.tensor_scalar(sig[:, h, :], cT[:, h, :], skip[:, h:h + 1], None, ALU.mult)
                step(last)
                dve.wait_ge(e["yT_ready"], b + 1)
                for h in range(H):
                    V.scalar_tensor_tensor(yT[:, h, :], hv(TR0)[:, h, :], ret_g[:, h:h + 1], srg[:, h, :],
                                           ALU.mult, ALU.mult)
                for h in range(H):
                    last = V.scalar_tensor_tensor(sig[:, h, :], hv(TR1)[:, h, :], ml_g[:, h:h + 1], sig[:, h, :],
                                                  ALU.mult, ALU.add)
                step(last)
                V.tensor_tensor(yT[:, H:2 * H, :], sig[:, :, :], smo[:, :, :], ALU.mult).then_inc(e["ym_done"], 1)
                dve.wait_ge(e["out_ready"], b + 1)
                dve.wait_ge(loaded["xr"], 16 * b + 16)
                V.tensor_tensor(xs[:, 0:512], P0[:, :], xr[:, 0:512], ALU.add)
                V.tensor_tensor(xs[:, 512:1024], P1[:, :], xr[:, 512:1024], ALU.add).then_inc(e["x1_done"], 1)

        @block.tensor
        def _(pe):
            mm, tp = nc.tensor.matmul, nc.tensor.transpose
            pe.wait_ge(loaded["const"], 16 * 7)

            def by_token(bk, col):
                for k in range(KC):
                    last = mm(bk[:, :], hT[:, k, :], w_in[:, k, col:col + W], start=(k == 0), stop=(k == KC - 1))
                return last

            def by_channel(bk, col):
                for h in range(H):
                    for k in range(KC):
                        last = mm(hv(bk)[:, h, :], w_in[:, k, col + h * P:col + (h + 1) * P], hT[:, k, :],
                                  start=(k == 0), stop=(k == KC - 1))
                return last

            with pe.Fori(0, NB) as b:
                pe.wait_ge(e["xs_done"], b + 1)
                for k in range(KC):
                    last = tp(hv(TR0 if k < 4 else TR1)[:, k % 4, :], xs[:, k * P:(k + 1) * P], ident[:, :])
                last.then_inc(e["xT_ready"], 1)
                pe.wait_ge(e["hT_done"], b + 1)
                pe.wait_ge(loaded["g"], 16)
                for k in range(KC):
                    last = mm(sm_gate, hT[:, k, :], w_in[:, k, MI:MI + 2 * H], start=(k == 0), stop=(k == KC - 1))
                last.then_inc(e["gates_ready"], 1)
                pe.wait_ge(loaded["mx"], 16)
                by_channel(P0, MX).then_inc(e["mx_ready"], 1)
                pe.wait_ge(e["gsb_done"], b + 1)
                tp(sm_i, gsb[:, 0:H], ident[:, :])
                tp(sm_f, gsb[:, H:2 * H], ident[:, :]).then_inc(e["gateT_ready"], 1)
                pe.wait_ge(loaded["rq"], 16)
                by_token(P1, RQ).then_inc(e["rq_ready"], 1)
                pe.wait_ge(loaded["rk"], 16)
                pe.wait_ge(e["mx_copied"], b + 1)
                by_token(P0, RK).then_inc(e["rk_ready"], 1)
                pe.wait_ge(loaded["const"], 16 * 7)
                pe.wait_ge(e["gate_exp"], b + 1)
                tp(sm_w, gates[:, 2, :], ident[0:H, 0:H])
                for h in range(H):
                    last = mm(sm_bc[:, 4 * h:4 * h + 4], select[:, h, :], cat[:, :], start=True, stop=True)
                last.then_inc(e["w_ready"], 1)
                pe.wait_ge(loaded["rv"], 16)
                pe.wait_ge(e["q_parts"], b + 1)
                by_token(P1, RV).then_inc(e["rv_ready"], 1)
                pe.wait_ge(e["qr_done"], b + 1)
                for h in range(H):
                    last = tp(hv(TR0)[:, h, :], qr[:, h, :], ident[:, :])
                last.then_inc(e["qT_ready"], 1)
                pe.wait_ge(e["kr_done"], b + 1)
                for h in range(H):
                    last = tp(hv(TR1)[:, h, :], kr[:, h, :], ident[:, :])
                last.then_inc(e["kT_ready"], 1)
                pe.wait_ge(loaded["mv"], 16)
                by_token(P0, MV).then_inc(e["mv_ready"], 1)
                pe.wait_ge(e["qT_copied"], b + 1)
                pe.wait_ge(e["kT_copied"], b + 1)
                for h in range(H):
                    last = mm(hv(RT)[:, h, :], kT[:, h, :], qT[:, h, :], start=True, stop=True)
                last.then_inc(e["scores_ready"], 1)
                pe.wait_ge(loaded["rg"], 16)
                pe.wait_ge(e["v_copied"], b + 1)
                by_channel(P1, RG).then_inc(e["rg_ready"], 1)
                pe.wait_ge(e["scd_done"], b + 1)
                for h in range(H):
                    mm(hv(RT)[:, h, :], scd[:, h, :], v[:, h, :], start=True, stop=False)
                    last = mm(hv(RT)[:, h, :], qT[:, h, :], S[:, h, :], start=False, stop=True)
                last.then_inc(e["o_ready"], 1)
                for h in range(H):
                    last = mm(hv(UP)[:, h, :], kr[:, h, :], v[:, h, :], start=True, stop=True)
                last.then_inc(e["s_ready"], 1)
                pe.wait_ge(e["cT_done"], b + 1)
                for h in range(H):
                    last = mm(hv(TR0)[:, h, :], mwq[:, h, :], cT[:, h, :], start=True, stop=True)
                last.then_inc(e["mq_ready"], 1)
                for h in range(H):
                    last = mm(hv(TR1)[:, h, :], cT[:, h, :], mwk[:, h, :], start=True, stop=True)
                last.then_inc(e["mk_ready"], 1)
                pe.wait_ge(loaded["mo"], 16)
                pe.wait_ge(e["v1_copied"], b + 1)
                by_channel(P0, MO).then_inc(e["mo_ready"], 1)
                pe.wait_ge(e["wv_done"], b + 1)
                pe.wait_ge(e["mqT_copied"], b + 1)
                pe.wait_ge(e["mk_copied"], b + 1)
                for c in range(2):
                    pe.wait_ge(e["s_done" if c == 0 else "c0_done"], b + 1)
                    for h in range(H):
                        mm(hv(UP)[:, h, :], mk[:, h, :], wv[:, c, h, :], start=True, stop=True)
                    for h in range(H):
                        last = mm(sm_n[:, h:h + 1], mk[:, h, :], wtok[:, c, h:h + 1], start=True, stop=True)
                    last.then_inc(e[f"c{c}_ready"], 1)
                    pe.wait_ge(e[f"c{c}_done"], b + 1)
                    rows = slice(64 * c, 64 * c + 64)
                    for h in range(H):
                        mm(hv(NM)[rows, h, :], mqT[:, h, rows], C[:, h, :], start=True, stop=True)
                    for h in range(H):
                        last = mm(sm_den[rows, h:h + 1], mqT[:, h, rows], nm[:, h:h + 1], start=True, stop=True)
                    last.then_inc(e[f"num{c}_ready"], 1)
                pe.wait_ge(e["g_done"], b + 1)
                for h in range(2 * H):
                    last = tp(hv(TR0 if h < H else TR1)[:, h % H, :], G[:, h, :], ident[:, :])
                last.then_inc(e["yT_ready"], 1)
                pe.wait_ge(loaded["out"], 16)
                pe.wait_ge(e["ym_done"], b + 1)
                for n, bk in enumerate((P0, P1)):
                    for k in range(KC):
                        last = mm(bk[:, :], yT[:, k, :], w_out[:, k, n * 512:(n + 1) * 512],
                                  start=(k == 0), stop=(k == KC - 1))
                last.then_inc(e["out_ready"], 1)
                pe.wait_ge(e["x1_done"], b + 1)


def router_stage(nc, io, x1_dram, xn, xo, expert, gate):
    T, D = io["x"].shape
    KC = D // P
    NB = T // P
    J = 2 * PEER_HEADS
    with ExitStack() as ctx:
        def sb(name, shape, dt=F32):
            return ctx.enter_context(nc.sbuf_tensor(name, shape, dt))

        def sem(name):
            return ctx.enter_context(nc.semaphore(name))

        wq = sb("wq", [P, KC, J * P])
        keysT = sb("keysT", [P, J, P])
        ident = sb("ident2", [P, P])
        iota = sb("iota", [P, TOPK])
        g2 = sb("g2", [P, D])
        xh = sb("xh", [P, D])
        x2T = sb("x2T", [P, KC, P])
        qT = sb("pqT", [P, J, P])
        sub = sb("sub", [P, J, P])
        sub2 = sb("sub2", [P, P])
        cand = sb("cand", [P, TOPK, TOPK])
        cand2 = sb("cand2", [P, TOPK * TOPK])
        top = sb("top", [P, J, TOPK])
        top_i = sb("top_i", [P, J, TOPK], U32)
        top_f = sb("top_f", [P, J, TOPK])
        best = sb("best", [P, PEER_HEADS, TOPK])
        flat = sb("flat", [P, PEER_HEADS, TOPK], U32)
        digit = sb("digit", [P, 2, PEER_HEADS * TOPK], U32)
        digit_f = sb("digit_f", [P, 2, PEER_HEADS * TOPK])
        hit = sb("hit", [P, PEER_HEADS * TOPK, TOPK])
        picked = sb("picked", [P, 2, PEER_HEADS * TOPK])
        row_f = sb("row_f", [P, PEER_HEADS * TOPK])
        sums = sb("sums", [P, 2, PEER_HEADS])
        ss = sb("ss2", [P, 4])
        keys = sub
        banks = [ctx.enter_context(nc.psum_tensor(f"pb{i}", [P, 512], F32)) for i in range(8)]
        hv = lambda t: t[:, :].rearrange("p (h d) -> p h d", d=P)

        ld = {n: sem("r_ld_" + n) for n in ("const", "keys", "wq", "x1")}
        names = ("keysT_ready keysT_done ss_done eps_done ln_done rstd_done xh_done xT_ready xT_copied "
                 "sub_copied best_done exp_done act_step dve_step topk_done").split()
        e = {n: sem("r_" + n) for n in names}
        q_ready = [sem(f"r_q_ready{i}") for i in range(4)]
        q_copied = [sem(f"r_q_copied{i}") for i in range(4)]
        s_ready = [sem(f"r_s_ready{i}") for i in range(4)]
        block = ctx.enter_context(nc.Block())

        @block.sync
        def _(sp):
            sp.dma_start(ident[:, :], io["ident"]).then_inc(ld["const"], 16)
            sp.dma_start(g2[:, :], io["norm2_g"].partition_broadcast(P)).then_inc(ld["const"], 16)
            sp.dma_start(iota[:, :], io["iota"]).then_inc(ld["const"], 16)
            for b in range(NB):
                sp.dma_start(xo[:, b, :], x1_dram[b * P:(b + 1) * P, :]).then_inc(ld["x1"], 16)
            sp.dma_start(keys[:, :, :], io["peer_keys"].rearrange("h t n d -> n (h t) d")).then_inc(ld["keys"], 16)
            for k in range(KC):
                sp.dma_start(wq[:, k, :], io["peer_wq"][k * P:(k + 1) * P, :]).then_inc(ld["wq"], 16)

        @block.scalar
        def _(act):
            act.wait_ge(ld["x1"], 16 * NB)
            for i in range(4):
                act.wait_ge(e["keysT_ready"], i + 1)
                nc.scalar.copy(keysT[:, 4 * i:4 * i + 4, :], hv(banks[i])).then_inc(e["keysT_done"], 1)
            with act.Fori(0, NB) as b:
                xb = xo[:, bass.ds(b, 1), :].rearrange("p a d -> p (a d)")
                nc.scalar.activation(xh[:, :], xb, ACT.Square, accum_out=ss[:, 0:1]).then_inc(e["ss_done"], 1)
                act.wait_ge(e["eps_done"], b + 1)
                nc.scalar.activation(ss[:, 2:3], ss[:, 1:2], ACT.Ln).then_inc(e["ln_done"], 1)
                act.wait_ge(e["ln_done"], b + 1)
                nc.scalar.activation(ss[:, 3:4], ss[:, 2:3], ACT.Exp, scale=-0.5).then_inc(e["rstd_done"], 1)
                act.wait_ge(e["xT_ready"], b + 1)
                nc.scalar.copy(x2T[:, 0:4, :], hv(banks[0]))
                nc.scalar.copy(x2T[:, 4:8, :], hv(banks[1])).then_inc(e["xT_copied"], 1)
                for i in range(4):
                    act.wait_ge(q_ready[i], b + 1)
                    nc.scalar.copy(qT[:, 4 * i:4 * i + 4, :], hv(banks[2 + i])).then_inc(q_copied[i], 1)
                for i in range(4):
                    act.wait_ge(s_ready[i], b + 1)
                    nc.scalar.copy(sub[:, 4 * i:4 * i + 4, :], hv(banks[2 + i])).then_inc(e["sub_copied"], 1)
                act.wait_ge(e["best_done"], b + 1)
                nc.scalar.activation(hit[:, 0:8, :], hit[:, 8:16, :], ACT.Exp).then_inc(e["exp_done"], 1)
                act.wait_ge(e["topk_done"], b + 1)

        @block.tensor
        def _(pe):
            mm, tp = nc.tensor.matmul, nc.tensor.transpose
            pe.wait_ge(ld["const"], 48)
            pe.wait_ge(ld["keys"], 16)
            for j in range(J):
                last = tp(hv(banks[j // 4])[:, j % 4, :], keys[:, j, :], ident[:, :])
                if j % 4 == 3:
                    last.then_inc(e["keysT_ready"], 1)
            pe.wait_ge(e["keysT_done"], 4)
            pe.wait_ge(ld["wq"], 16 * KC)
            with pe.Fori(0, NB) as b:
                pe.wait_ge(e["xh_done"], b + 1)
                for k in range(KC):
                    last = tp(hv(banks[k // 4])[:, k % 4, :], xh[:, k * P:(k + 1) * P], ident[:, :])
                last.then_inc(e["xT_ready"], 1)
                pe.wait_ge(e["xT_copied"], b + 1)
                for j in range(J):
                    for k in range(KC):
                        last = mm(hv(banks[2 + j // 4])[:, j % 4, :], wq[:, k, j * P:(j + 1) * P], x2T[:, k, :],
                                  start=(k == 0), stop=(k == KC - 1))
                    if j % 4 == 3:
                        last.then_inc(q_ready[j // 4], 1)
                for j in range(J):
                    if j % 4 == 0:
                        pe.wait_ge(q_copied[j // 4], b + 1)
                    last = mm(hv(banks[2 + j // 4])[:, j % 4, :], qT[:, j, :], keysT[:, j, :], start=True, stop=True)
                    if j % 4 == 3:
                        last.then_inc(s_ready[j // 4], 1)
                pe.wait_ge(e["sub_copied"], 4 * b + 4)

        @block.vector
        def _(dve):
            V = nc.vector
            N = PEER_HEADS * TOPK
            dve.wait_ge(ld["const"], 48)
            V.memset(expert[:, NB * N:], 0)
            with dve.Fori(0, NB) as b:
                step = Chain(dve, e["dve_step"])
                dve.wait_ge(e["ss_done"], b + 1)
                V.tensor_scalar(ss[:, 1:2], ss[:, 0:1], 1.0 / D, EPS, ALU.mult, ALU.add).then_inc(e["eps_done"], 1)
                dve.wait_ge(e["rstd_done"], b + 1)
                xb = xo[:, bass.ds(b, 1), :].rearrange("p a d -> p (a d)")
                V.scalar_tensor_tensor(xh[:, :], xb, ss[:, 3:4], g2[:, :], ALU.mult, ALU.mult).then_inc(e["xh_done"], 1)
                dve.wait_ge(e["xh_done"], b + 1)
                V.tensor_copy(xn[:, bass.ds(b, 1), :].rearrange("p a d -> p (a d)"), xh[:, :])
                dve.wait_ge(e["sub_copied"], 4 * b + 4)
                V.tensor_copy(cand2[:, 0:1], iota[:, 0:1])

                def top16(values, scratch, out, index):
                    step(V.max(out[:, 0:8], values))
                    V.max_index(index[:, 0:8], out[:, 0:8], values)
                    step(V.match_replace(scratch, out[:, 0:8], values, NEG))
                    step(V.max(out[:, 8:16], scratch))
                    step(V.max_index(index[:, 8:16], out[:, 8:16], scratch))

                for j in range(J):
                    top16(sub[:, j, :], sub2[:, :], top[:, j, :], top_i[:, j, :])
                for h in range(PEER_HEADS):
                    step(V.tensor_tensor(cand[:, :, :], top[:, 2 * h, :].unsqueeze(2).broadcast_to([P, TOPK, TOPK]),
                                         top[:, 2 * h + 1, :].unsqueeze(1).broadcast_to([P, TOPK, TOPK]), ALU.add))
                    top16(cand[:, :, :].rearrange("p a c -> p (a c)"), cand2[:, :], best[:, h, :], flat[:, h, :])
                step(V.tensor_tensor(hit[:, 8:16, :], best[:, :, :], best[:, :, 0:1].broadcast_to([P, PEER_HEADS, TOPK]),
                                     ALU.subtract))
                V.tensor_copy(top_f[:, :, :], top_i[:, :, :]).then_inc(e["best_done"], 1)
                dve.wait_ge(e["exp_done"], b + 1)
                step(V.tensor_reduce(sums[:, 0, :], hit[:, 0:8, :], AX, ALU.add))
                step(V.reciprocal(sums[:, 1, :], sums[:, 0, :]))
                step(V.tensor_tensor(gate[:, bass.ds(b * N, N)].rearrange("p (h k) -> p h k", h=PEER_HEADS),
                                     hit[:, 0:8, :], sums[:, 1, :].unsqueeze(2).broadcast_to([P, PEER_HEADS, TOPK]),
                                     ALU.mult))
                fl = flat[:, :, :].rearrange("p h k -> p (h k)")
                V.tensor_scalar(digit[:, 0, :], fl, 4, None, ALU.logical_shift_right)
                step(V.tensor_scalar(digit[:, 1, :], fl, 15, None, ALU.bitwise_and))
                step(V.tensor_copy(digit_f[:, :, :], digit[:, :, :]))
                for s in range(2):
                    step(V.tensor_tensor(hit[:, :, :], digit_f[:, s, :].unsqueeze(2).broadcast_to([P, N, TOPK]),
                                         iota[:, :].unsqueeze(1).broadcast_to([P, N, TOPK]), ALU.is_equal))
                    for h in range(PEER_HEADS):
                        hh = hit[:, h * TOPK:(h + 1) * TOPK, :]
                        last = V.tensor_tensor(hh, hh, top_f[:, 2 * h + s, :].unsqueeze(1).broadcast_to([P, TOPK, TOPK]),
                                               ALU.mult)
                    step(last)
                    step(V.tensor_reduce(picked[:, s, :], hit[:, :, :], AX, ALU.add))
                step(V.scalar_tensor_tensor(row_f[:, :], picked[:, 0, :], float(P), picked[:, 1, :], ALU.mult, ALU.add))
                V.tensor_copy(expert[:, bass.ds(b * N, N)], row_f[:, :]).then_inc(
                    e["topk_done"], 1)


def expert_stage(nc, io, xn, xo, expert, gate, out):
    T, D = io["x"].shape
    NB = T // P
    NH = PEER_HEADS
    with ExitStack() as ctx:
        def sb(name, shape, dt=F32):
            return ctx.enter_context(nc.sbuf_tensor(name, shape, dt))

        def sem(name):
            return ctx.enter_context(nc.semaphore(name))

        down = [sb(f"down{i}", [P, D]) for i in range(DOWN_RING)]
        up = [sb(f"up{i}", [P, D]) for i in range(TOPK)]
        fg = sb("fg", [P, D])
        done = sb("done", [P, D])
        rows = [sb(f"rows{i}", [P, TOPK], U32) for i in range(2)]
        act_in = [sb(f"act_in{i}", [P, TOPK]) for i in range(2)]
        act_out = [sb(f"act_out{i}", [P, TOPK]) for i in range(2)]
        weight = [sb(f"weight{i}", [P, TOPK]) for i in range(2)]
        ss = sb("ss3", [P, 4])
        down_in = [sem(f"x_down_in{i}") for i in range(DOWN_RING)]
        up_in = [sem(f"x_up_in{i}") for i in range(TOPK)]
        names = "rows_set dots gelu_done weighed sums ss_done eps_done ln_done rstd_done out_done stored".split()
        e = {n: sem("x_" + n) for n in names}
        fg_in = sem("x_fg_in")
        block = ctx.enter_context(nc.Block())

        @block.sync
        def _(sp):
            sp.dma_start(fg[:, :], io["final_g"].partition_broadcast(P)).then_inc(fg_in, 16)
            with sp.Fori(0, NB) as b:
                sp.wait_ge(e["out_done"], b + 1)
                sp.dma_start(out[bass.ts(b, P), :], done[:, :]).then_inc(e["stored"], 16)
            sp.wait_ge(e["stored"], 16 * NB)

        @block.gpsimd
        def _(pool):
            def gather(table, buf, rows_of, k, arrived):
                nc.gpsimd.indirect_dma_start(
                    buf[:, :], None, table, bass.IndirectOffsetOnAxis(ap=rows_of[:, k:k + 1], axis=0),
                ).then_inc(arrived, 16)

            turns = pool.alloc_register("turns")

            def counted(sem, value):
                pool.reg_mov(turns, value)
                pool.wait_ge(e["rows_set"], 1)
                pool.wait_ge(sem, turns)

            def head(g, turn, first):
                counted(e["rows_set"], g + 1)
                for k in range(TOPK):
                    if not (first and k < DOWN_RING):
                        counted(e["dots"], g * TOPK + (k - DOWN_RING + 1))
                    gather(io["peer_down"], down[k % DOWN_RING], rows[turn], k, down_in[k % DOWN_RING])
                    if not first:
                        counted(e["sums"], g * TOPK + (k - TOPK + 1))
                    gather(io["peer_up"], up[k], rows[turn], k, up_in[k])

            head(0, 0, True)
            head(1, 1, False)
            with pool.Fori(1, NB * NH // 2) as pair:
                head(pair * 2, 0, False)
                head(pair * 2 + 1, 1, False)

        @block.scalar
        def _(act):
            with act.Fori(0, NB) as b:
                with act.Fori(0, NH // 2) as pair:
                    for turn in range(2):
                        g = b * NH + pair * 2 + turn
                        act.wait_ge(e["dots"], g * TOPK + TOPK)
                        nc.scalar.activation(act_out[turn][:, :], act_in[turn][:, :], ACT.Gelu).then_inc(
                            e["gelu_done"], 1)
                act.wait_ge(e["sums"], (b + 1) * (NH * TOPK))
                xb = xo[:, bass.ds(b, 1), :].rearrange("p a d -> p (a d)")
                nc.scalar.activation(done[:, :], xb, ACT.Square, accum_out=ss[:, 0:1]).then_inc(e["ss_done"], 1)
                act.wait_ge(e["eps_done"], b + 1)
                nc.scalar.activation(ss[:, 2:3], ss[:, 1:2], ACT.Ln).then_inc(e["ln_done"], 1)
                act.wait_ge(e["ln_done"], b + 1)
                nc.scalar.activation(ss[:, 3:4], ss[:, 2:3], ACT.Exp, scale=-0.5).then_inc(e["rstd_done"], 1)
                act.wait_ge(e["stored"], b * 16 + 16)

        @block.vector
        def _(dve):
            V = nc.vector

            def set_rows(g, turn):
                V.tensor_copy(rows[turn][:, :], expert[:, bass.ds(g * TOPK, TOPK)]).then_inc(e["rows_set"], 1)

            dve.wait_ge(fg_in, 16)
            set_rows(0, 0)
            set_rows(1, 1)
            with dve.Fori(0, NB) as b:
                xb = xo[:, bass.ds(b, 1), :].rearrange("p a d -> p (a d)")
                xnb = xn[:, bass.ds(b, 1), :].rearrange("p a d -> p (a d)")
                with dve.Fori(0, NH // 2) as pair:
                    for turn in range(2):
                        g = b * NH + pair * 2 + turn
                        for k in range(TOPK):
                            dve.wait_ge(down_in[k % DOWN_RING], g * 32 + (16 * (k // DOWN_RING) + 16))
                            slot = down[k % DOWN_RING][:, :]
                            V.scalar_tensor_tensor(slot, slot, 1.0, xnb, ALU.mult, ALU.mult,
                                                   accum_out=act_in[turn][:, k:k + 1]).then_inc(e["dots"], 1)
                        dve.wait_ge(e["gelu_done"], g + 1)
                        V.tensor_tensor(weight[turn][:, :], act_out[turn][:, :], gate[:, bass.ds(g * TOPK, TOPK)],
                                        ALU.mult).then_inc(e["weighed"], 1)
                        dve.wait_ge(e["weighed"], g + 1)
                        for k in range(TOPK):
                            dve.wait_ge(up_in[k], g * 16 + 16)
                            if k > 0:
                                dve.wait_ge(e["sums"], g * TOPK + k)
                            V.scalar_tensor_tensor(xb, up[k][:, :], weight[turn][:, k:k + 1], xb, ALU.mult,
                                                   ALU.add).then_inc(e["sums"], 1)
                        dve.wait_ge(e["sums"], g * TOPK + TOPK)
                        set_rows(g + 2, turn)
                dve.wait_ge(e["ss_done"], b + 1)
                V.tensor_scalar(ss[:, 1:2], ss[:, 0:1], 1.0 / D, EPS, ALU.mult, ALU.add).then_inc(e["eps_done"], 1)
                dve.wait_ge(e["rstd_done"], b + 1)
                V.scalar_tensor_tensor(done[:, :], xb, ss[:, 3:4], fg[:, :], ALU.mult, ALU.mult).then_inc(
                    e["out_done"], 1)


def build(nc, io, out):
    T, D = io["x"].shape
    NB = T // P
    N = PEER_HEADS * TOPK
    x1_dram = nc.dram_tensor("x1_scratch", (T, D), F32, kind="Internal").ap()
    mix_stage(nc, io, x1_dram)
    with ExitStack() as ctx:
        xo = ctx.enter_context(nc.sbuf_tensor("xo", [P, NB, D], F32))
        xn = ctx.enter_context(nc.sbuf_tensor("xn", [P, NB, D], F32))
        expert = ctx.enter_context(nc.sbuf_tensor("expert", [P, NB * N + 2 * TOPK], U32))
        gate = ctx.enter_context(nc.sbuf_tensor("gate", [P, NB * N], F32))
        router_stage(nc, io, x1_dram, xn, xo, expert, gate)
        expert_stage(nc, io, xn, xo, expert, gate, out)


def shape_constants(np, T):
    H, half_w = 4, 64
    gamma = 1.0 - 2.0 ** (-5.0 - np.arange(H, dtype=np.float64))
    inv = (np.float64(10000.0) ** (-np.arange(half_w, dtype=np.float64) / half_w)).astype(np.float32)
    angle = (np.arange(T, dtype=np.float32)[:, None] * inv[None, :]).astype(np.float64)
    place = np.arange(T) % P
    q_decay = gamma[None, :] ** (place[:, None] + 1.0)
    k_decay = gamma[None, :] ** (P - 1.0 - place[:, None]) * float(P) ** -0.5
    trig = np.stack([f(angle)[:, None, :] * d[:, :, None] for d in (q_decay, k_decay) for f in (np.cos, np.sin)], 1)
    l, m = np.arange(P)[None, :], np.arange(P)[:, None]
    same, past = l // 64 == m // 64, l // 64 > m // 64
    power = np.where(same, np.abs(l - m), l - m) - (l + 1.0) - (P - 1.0 - m)
    decay = np.where((same | past)[None], gamma[:, None, None] ** power[None], 0.0)
    one = np.float32
    return {
        "ident": np.eye(P, dtype=one),
        "iota": np.tile(np.arange(TOPK, dtype=one), (P, 1)),
        "trig": trig.reshape(T, 4, H * half_w).astype(one),
        "decay_t": np.ascontiguousarray(decay.transpose(1, 0, 2)).astype(one),
        "select": np.ascontiguousarray(np.repeat(np.eye(H, dtype=one)[:, :, None], P, axis=2)),
        "reset": np.tile((np.arange(P) % 64 != 0).astype(one), (H, 1)),
        "half": np.stack([np.arange(P) < 64, np.arange(P) >= 64], 1).astype(one),
    }


_LAYER = ["norm1_g", "w_in", "ret_norm_g", "m_conv_w", "m_conv_b", "m_wq", "m_wk", "m_b_i", "m_b_f", "m_norm_g",
          "m_skip", "w_out", "norm2_g", "peer_wq", "peer_keys", "peer_down", "peer_up"]


def kernel(**inputs):
    import numpy as np
    import concourse.bacc as bacc
    from concourse.bass_utils import run_bass_kernel_spmd

    x = np.ascontiguousarray(inputs["x"])
    arrays = {"x": x[0], "final_g": np.ascontiguousarray(inputs["final_g"])}
    for name in _LAYER:
        arrays[name] = np.ascontiguousarray(inputs[name])[0]
    arrays.update(shape_constants(np, x.shape[1]))
    nc = bacc.Bacc("TRN2", target_bir_lowering=False, num_devices=1)
    io = {name: nc.dram_tensor(f"in_{name}", a.shape, mybir.dt.from_np(a.dtype), kind="ExternalInput").ap()
          for name, a in arrays.items()}
    out = nc.dram_tensor("out_x", x.shape[1:], F32, kind="ExternalOutput").ap()
    build(nc, io, out)
    r = run_bass_kernel_spmd(nc, [{f"in_{n}": a for n, a in arrays.items()}], core_ids=[0])
    return r.results[0]["out_x"].reshape(x.shape)
```

```python
from contextlib import ExitStack

import concourse.bass as bass
from concourse import mybir

F32 = mybir.dt.float32
F32R = mybir.dt.float32r
U32 = mybir.dt.uint32
ALU = mybir.AluOpType
ACT = mybir.ActivationFunctionType
AX = mybir.AxisListType.X

P = 128
EPS = 1e-6
CONV_W = 4
NEG = -3.0e38
PEER_HEADS = 8
TOPK = 16
DOWN_RING, UP_RING = 4, 8


def retention_block_decay():
    return [float((1.0 - 2.0 ** (-5.0 - h)) ** P) for h in range(4)]


class Chain:

    def __init__(self, engine, sem):
        self.engine, self.sem, self.n = engine, sem, 0
        engine.sem_clear(sem)

    def __call__(self, instruction):
        self.n += 1
        instruction.then_inc(self.sem, 1)
        self.engine.wait_ge(self.sem, self.n)


def clear_semaphores(nc, held):
    nc.clear_and_free_semaphores(held)
    nc.all_engine_barrier()


def mix_stage(nc, io, x1_dram):
    D = io["x"].shape[1]
    T = io["x"].shape[0]
    KC = D // P
    NB = T // P
    H = 4
    W = H * P
    RQ, RK, RV, RG, MX, MV, MO, MI, MF = [W * i for i in range(7)] + [7 * W, 7 * W + H]
    gamma_p = retention_block_decay()

    held = []
    with ExitStack() as ctx:
        ctx.callback(clear_semaphores, nc, held)

        def sb(name, shape, dt=F32):
            return ctx.enter_context(nc.sbuf_tensor(name, shape, dt))

        def bank(name):
            return ctx.enter_context(nc.psum_tensor(name, [P, 512], F32))

        def sem(name):
            held.append(nc.alloc_semaphore(name))
            return held[-1]

        w_in = sb("w_in_sb", [P, KC, 7 * W + 2 * H])
        w_out = sb("w_out_sb", [P, KC, D])
        mwq = sb("mwq", [P, H, P])
        mwk = sb("mwk", [P, H, P])
        ident = sb("ident", [P, P])
        decay_t = sb("decay_t", [P, H, P])
        select = sb("select", [H, H, P])
        reset = sb("reset", [H, P])
        half = sb("half", [P, 2])
        g1 = sb("g1", [P, KC])
        ret_g = sb("ret_g", [P, H])
        ml_g = sb("ml_g", [P, H])
        skip = sb("skip", [P, H])
        conv_w = sb("conv_w", [P, CONV_W, H])
        conv_b = sb("conv_b", [P, H])
        b_i = sb("b_i", [H, 1])
        b_f = sb("b_f", [H, 1])
        xa = sb("xa", [P, D])
        xr = sb("xr", [P, D])
        xs = sb("xs", [P, D])
        trig = sb("trig", [P, 4, 4 * 64])
        hT = sb("hT", [P, KC, P])
        ss = sb("ss", [P, 4])
        mxb = sb("mxb", [P, H, P + CONV_W - 1])
        cT = sb("cT", [P, H, P])
        sig = sb("sig", [P, H, P])
        srg = sb("srg", [P, H, P])
        smo = sb("smo", [P, H, P])
        qr = sb("qr", [P, H, P])
        kr = sb("kr", [P, H, P])
        v = sb("v", [P, H, P])
        v1 = sb("v1", [P, H, P])
        wv = sb("wv", [P, 2, H, P])
        qT = sb("qT", [P, H, P])
        kT = sb("kT", [P, H, P])
        gsb = sb("gsb", [P, 2 * H])
        gates = sb("gates", [H, 7, P])
        small = sb("small", [H, 24])
        cat = sb("cat", [H, 4])
        wtok = sb("wtok", [P, 2, H])
        bc = sb("bc", [P, H, 4])
        den = sb("den", [P, 4, H])
        stats = sb("stats", [P, 3, 2 * H])
        S = sb("S", [P, H, P])
        C = sb("C", [P, H, P])
        nm = sb("nm", [P, H])
        m_seq = sb("m_seq", [H, 3])
        G = xs[:, :].rearrange("p (h d) -> p h d", d=P)
        sq = trig[:, :, :].rearrange("p a c -> p (a c)")
        yT = hT
        rot = wv[:, :, :, :].rearrange("p c h d -> p (c h d)").rearrange("p (a h d) -> p a h d", a=4, d=64)
        scd, mqT, mk = qr, qT, kT

        P0, P1, TR0, TR1, RT, UP, NM, SM = [bank(f"bank{i}") for i in range(8)]
        hv = lambda t: t[:, :].rearrange("p (h d) -> p h d", d=P)
        sm_gate, sm_i, sm_f = SM[:, 0:8], SM[0:H, 16:144], SM[0:H, 144:272]
        sm_w, sm_bc = SM[:, 272:276], SM[:, 276:292]
        sm_n, sm_den = SM[:, 292:296], SM[:, 296:300]

        names = ("xs_done xT_ready hT_done gates_ready gsb_done mx_ready mx_copied conv_done "
                 "conv_exp cT_done gateT_ready gate_abs gate_log gate_diff gate_exp w_ready w_copied "
                 "rq_ready rq_read q_parts qr_done rk_ready rk_read k_parts kr_done "
                 "rv_ready v_copied mv_ready v1_copied qT_ready qT_copied kT_ready kT_copied "
                 "scores_ready scd_done rg_ready rg_exp srg_done o_ready o_copied s_ready s_done "
                 "mq_ready mqT_copied mk_ready mk_copied mo_ready mo_exp smo_done wv_done "
                 "c0_ready c0_done c1_ready c1_done num0_ready num1_ready hm_done mean_done sq_done "
                 "var_done ln_done rstd_done g_done yT_ready yr_done ym_done out_ready x1_done "
                 "ss_done eps_done dve_step act_step").split()
        e = {n: sem(n) for n in names}
        loaded = {n: sem("ld_" + n) for n in ("const", "small", "mx", "g", "rq", "rk", "rv", "mv", "rg", "mo", "out",
                                              "xa", "xr", "trig", "x1")}
        zeroed = sem("zeroed")
        block = ctx.enter_context(nc.Block())

        SMALL = 11

        @block.sync
        def _(sp):
            win = io["w_in"].rearrange("(k p) n -> p k n", p=P)
            sp.dma_start(xa[:, :], io["x"][0:P, :]).then_inc(loaded["xa"], 16)
            sp.dma_start(ident[:, :], io["ident"]).then_inc(loaded["const"], 16)
            with nc.allow_non_contiguous_dma(reason="small per-channel vectors"):
                sp.dma_start(g1[:, :], io["norm1_g"].rearrange("(k p) -> p k", p=P)).then_inc(loaded["small"], 16)
                sp.dma_start(w_in[:, :, MI:MI + 2 * H], win[:, :, MI:MI + 2 * H]).then_inc(loaded["g"], 16)
                sp.dma_start(w_in[:, :, MX:MX + W], win[:, :, MX:MX + W]).then_inc(loaded["mx"], 16)
                sp.dma_start(ret_g[:, :], io["ret_norm_g"].rearrange("h p -> p h")).then_inc(loaded["small"], 16)
                sp.dma_start(ml_g[:, :], io["m_norm_g"].rearrange("h p -> p h")).then_inc(loaded["small"], 16)
                sp.dma_start(skip[:, :], io["m_skip"].rearrange("(h p) -> p h", p=P)).then_inc(loaded["small"], 16)
                sp.dma_start(conv_b[:, :], io["m_conv_b"].rearrange("(h p) -> p h", p=P)).then_inc(loaded["small"], 16)
                for j in range(CONV_W):
                    sp.dma_start(conv_w[:, j, :], io["m_conv_w"][j].rearrange("(h p) -> p h", p=P)).then_inc(
                        loaded["small"], 16)
                sp.dma_start(b_i[:, :], io["m_b_i"].rearrange("(h a) -> h a", a=1)).then_inc(loaded["small"], 16)
                sp.dma_start(b_f[:, :], io["m_b_f"].rearrange("(h a) -> h a", a=1)).then_inc(loaded["small"], 16)
            sp.dma_start(reset[:, :], io["reset"]).then_inc(loaded["const"], 16)
            sp.dma_start(half[:, :], io["half"]).then_inc(loaded["const"], 16)
            sp.dma_start(select[:, :, :], io["select"]).then_inc(loaded["const"], 16)
            sp.dma_start(w_in[:, :, RQ:RQ + W], win[:, :, RQ:RQ + W]).then_inc(loaded["rq"], 16)
            sp.dma_start(trig[:, :, :], io["trig"][0:P, :, :]).then_inc(loaded["trig"], 16)
            sp.dma_start(w_in[:, :, RK:RK + W], win[:, :, RK:RK + W]).then_inc(loaded["rk"], 16)
            sp.dma_start(w_in[:, :, RV:RV + W], win[:, :, RV:RV + W]).then_inc(loaded["rv"], 16)
            sp.dma_start(decay_t[:, :, :], io["decay_t"]).then_inc(loaded["const"], 16)
            sp.dma_start(mwq[:, :, :], io["m_wq"].rearrange("h d e -> d h e")).then_inc(loaded["const"], 16)
            sp.dma_start(mwk[:, :, :], io["m_wk"].rearrange("h d e -> d h e")).then_inc(loaded["const"], 16)
            sp.dma_start(w_in[:, :, MV:MV + W], win[:, :, MV:MV + W]).then_inc(loaded["mv"], 16)
            sp.dma_start(w_in[:, :, RG:RG + W], win[:, :, RG:RG + W]).then_inc(loaded["rg"], 16)
            sp.dma_start(w_in[:, :, MO:MO + W], win[:, :, MO:MO + W]).then_inc(loaded["mo"], 16)
            sp.dma_start(w_out[:, :, :], io["w_out"].rearrange("(k p) n -> p k n", p=P)).then_inc(loaded["out"], 16)
            sp.dma_start(xr[:, :], io["x"][0:P, :]).then_inc(loaded["xr"], 16)
            with sp.Fori(1, NB) as b:
                sp.wait_ge(e["xs_done"], b)
                sp.dma_start(xa[:, :], io["x"][bass.ts(b, P), :]).then_inc(loaded["xa"], 16)
                sp.wait_ge(e["rstd_done"], b)
                sp.dma_start(trig[:, :, :], io["trig"][bass.ts(b, P), :, :]).then_inc(loaded["trig"], 16)
                sp.wait_ge(e["x1_done"], b)
                sp.dma_start(xr[:, :], io["x"][bass.ts(b, P), :]).then_inc(loaded["xr"], 16)

        @block.gpsimd
        def _(pool):
            nc.gpsimd.memset(mxb[:, :, :], 0.0).then_inc(zeroed, 1)
            nc.gpsimd.memset(S[:, :, :], 0.0).then_inc(zeroed, 1)
            nc.gpsimd.memset(C[:, :, :], 0.0).then_inc(zeroed, 1)
            nc.gpsimd.memset(nm[:, :], 0.0).then_inc(zeroed, 1)
            nc.gpsimd.memset(m_seq[:, :], 0.0).then_inc(zeroed, 1)
            with pool.Fori(0, NB) as b:
                for name, r in (("q", qr), ("k", kr)):
                    pool.wait_ge(e[name + "_parts"], b + 1)
                    nc.gpsimd.tensor_tensor(r[:, :, 0:64], rot[:, 0, :, :], rot[:, 1, :, :], ALU.subtract)
                    nc.gpsimd.tensor_tensor(r[:, :, 64:128], rot[:, 2, :, :], rot[:, 3, :, :], ALU.add).then_inc(
                        e[name + "r_done"], 1)
                pool.wait_ge(e["x1_done"], b + 1)
                pool.dma_start(x1_dram[bass.ts(b, P), :], xs[:, :]).then_inc(loaded["x1"], 16)
            pool.wait_ge(loaded["x1"], 16 * NB)

        @block.scalar
        def _(act):
            with act.Fori(0, NB) as b:
                step = Chain(act, e["act_step"])
                act.wait_ge(loaded["xa"], 16 * b + 16)
                nc.scalar.activation(xs[:, :], xa[:, :], ACT.Square, accum_out=ss[:, 0:1]).then_inc(e["ss_done"], 1)
                act.wait_ge(e["eps_done"], b + 1)
                step(nc.scalar.activation(ss[:, 2:3], ss[:, 1:2], ACT.Ln))
                step(nc.scalar.activation(ss[:, 3:4], ss[:, 2:3], ACT.Exp, scale=-0.5))
                nc.scalar.activation(xs[:, :], xa[:, :], ACT.Copy, scale=ss[:, 3:4]).then_inc(e["xs_done"], 1)
                act.wait_ge(e["mx_ready"], b + 1)
                nc.scalar.copy(mxb[:, :, CONV_W - 1:], hv(P0)).then_inc(e["mx_copied"], 1)
                act.wait_ge(e["gate_abs"], b + 1)
                step(nc.scalar.activation(gates[:, 2, :], gates[:, 1, :], ACT.Exp, scale=-1.0))
                nc.scalar.activation(gates[:, 3, :], gates[:, 2, :], ACT.Ln, bias=1.0).then_inc(e["gate_log"], 1)
                act.wait_ge(e["gate_diff"], b + 1)
                nc.scalar.activation(gates[:, 2, :], gates[:, 6, :], ACT.Exp)
                nc.scalar.activation(cat[:, 0:2], small[:, 8:10], ACT.Exp)
                nc.scalar.activation(cat[:, 2:4], small[:, 4:6], ACT.Exp, scale=-1.0).then_inc(e["gate_exp"], 1)
                act.wait_ge(e["conv_done"], b + 1)
                nc.scalar.activation(sig[:, :, :], cT[:, :, :], ACT.Exp, scale=-1.0).then_inc(e["conv_exp"], 1)
                act.wait_ge(e["rv_ready"], b + 1)
                nc.scalar.copy(v[:, :, :], hv(P1)).then_inc(e["v_copied"], 1)
                act.wait_ge(e["qT_ready"], b + 1)
                nc.scalar.copy(qT[:, :, :], hv(TR0)).then_inc(e["qT_copied"], 1)
                act.wait_ge(e["kT_ready"], b + 1)
                nc.scalar.copy(kT[:, :, :], hv(TR1)).then_inc(e["kT_copied"], 1)
                act.wait_ge(e["mv_ready"], b + 1)
                nc.scalar.copy(v1[:, :, :], hv(P0)).then_inc(e["v1_copied"], 1)
                act.wait_ge(e["rg_ready"], b + 1)
                nc.scalar.activation(srg[:, :, :], hv(P1), ACT.Exp, scale=-1.0).then_inc(e["rg_exp"], 1)
                act.wait_ge(e["mq_ready"], b + 1)
                nc.scalar.copy(mqT[:, :, :], hv(TR0)).then_inc(e["mqT_copied"], 1)
                act.wait_ge(e["mk_ready"], b + 1)
                nc.scalar.activation(mk[:, :, :], hv(TR1), ACT.Copy, scale=float(P) ** -0.5).then_inc(e["mk_copied"], 1)
                act.wait_ge(e["mo_ready"], b + 1)
                nc.scalar.activation(smo[:, :, :], hv(P0), ACT.Exp, scale=-1.0).then_inc(e["mo_exp"], 1)
                act.wait_ge(e["o_ready"], b + 1)
                nc.scalar.copy(G[:, 0:H, :], hv(RT)).then_inc(e["o_copied"], 1)
                act.wait_ge(e["mean_done"], b + 1)
                nc.scalar.activation(sq, xs[:, :], ACT.Square).then_inc(e["sq_done"], 1)
                act.wait_ge(e["var_done"], b + 1)
                nc.scalar.activation(stats[:, 1, :], stats[:, 2, :], ACT.Ln).then_inc(e["ln_done"], 1)
                act.wait_ge(e["ln_done"], b + 1)
                nc.scalar.activation(stats[:, 0, :], stats[:, 1, :], ACT.Exp, scale=-0.5).then_inc(e["rstd_done"], 1)
                act.wait_ge(loaded["x1"], 16 * b + 16)

        @block.vector
        def _(dve):
            V = nc.vector
            dve.wait_ge(zeroed, 5)
            dve.wait_ge(loaded["small"], 16 * SMALL)
            dve.wait_ge(loaded["const"], 16 * 7)
            with dve.Fori(0, NB) as b:
                step = Chain(dve, e["dve_step"])
                dve.wait_ge(e["ss_done"], b + 1)
                V.tensor_scalar(ss[:, 1:2], ss[:, 0:1], 1.0 / D, EPS, ALU.mult, ALU.add).then_inc(e["eps_done"], 1)
                dve.wait_ge(e["xT_ready"], b + 1)
                for k2, bk in enumerate((TR0, TR1)):
                    gain = g1[:, 4 * k2:4 * k2 + 4].unsqueeze(2).broadcast_to([P, 4, P])
                    last = V.tensor_tensor(hT[:, 4 * k2:4 * k2 + 4, :], hv(bk), gain, ALU.mult)
                last.then_inc(e["hT_done"], 1)
                dve.wait_ge(e["gates_ready"], b + 1)
                V.tensor_copy(gsb[:, :], sm_gate).then_inc(e["gsb_done"], 1)
                dve.wait_ge(e["gateT_ready"], b + 1)
                step(V.tensor_scalar(gates[:, 0, :], sm_f, b_f[:, 0:1], None, ALU.add))
                step(V.tensor_scalar(gates[:, 4, :], sm_i, b_i[:, 0:1], None, ALU.add))
                V.scalar_tensor_tensor(gates[:, 1, :], gates[:, 0, :], -1.0, gates[:, 0, :], ALU.mult,
                                       ALU.max).then_inc(e["gate_abs"], 1)
                dve.wait_ge(e["gate_log"], b + 1)
                step(V.scalar_tensor_tensor(gates[:, 5, :], gates[:, 0, :], 0.0, gates[:, 3, :], ALU.min, ALU.subtract))
                step(V.tensor_tensor_scan(gates[:, 1, :], reset[:, :], gates[:, 5, :], 0.0, ALU.mult, ALU.add))
                step(V.tensor_copy(small[:, 0:2], gates[:, 1, 63:128:64]))
                step(V.tensor_tensor(gates[:, 4, :], gates[:, 4, :], gates[:, 1, :], ALU.subtract))
                g2v = lambda i: gates[:, i, :].rearrange("h (c l) -> h c l", l=64)
                a_wide = small[:, 0:2].unsqueeze(2).broadcast_to([H, 2, 64])
                step(V.tensor_tensor(g2v(5), g2v(4), a_wide, ALU.add))
                step(V.tensor_reduce(small[:, 2:4], g2v(5), AX, ALU.max))
                step(V.tensor_tensor_scan(m_seq[:, 1:3], small[:, 0:2], small[:, 2:4], m_seq[:, 0:1], ALU.add, ALU.max))
                step(V.tensor_tensor(small[:, 6:8], small[:, 0:2], m_seq[:, 0:2], ALU.add))
                step(V.tensor_tensor(small[:, 8:10], small[:, 6:8], m_seq[:, 1:3], ALU.subtract))
                step(V.tensor_copy(small[:, 4:6], m_seq[:, 1:3]))
                m_wide = small[:, 4:6].unsqueeze(2).broadcast_to([H, 2, 64])
                step(V.tensor_tensor(g2v(6), g2v(5), m_wide, ALU.subtract))
                V.tensor_copy(m_seq[:, 0:1], small[:, 5:6]).then_inc(e["gate_diff"], 1)
                dve.wait_ge(e["mx_copied"], b + 1)
                for h in range(H):
                    last = V.tensor_scalar(cT[:, h, :], mxb[:, h, 0:P], conv_w[:, 0, h:h + 1], conv_b[:, h:h + 1],
                                           ALU.mult, ALU.add)
                step(last)
                for j in range(1, CONV_W):
                    for h in range(H):
                        last = V.scalar_tensor_tensor(cT[:, h, :], mxb[:, h, j:j + P], conv_w[:, j, h:h + 1],
                                                      cT[:, h, :], ALU.mult, ALU.add)
                    if j < CONV_W - 1:
                        step(last)
                last.then_inc(e["conv_done"], 1)
                dve.wait_ge(e["conv_done"], b + 1)
                V.tensor_copy(mxb[:, :, 0:CONV_W - 1], mxb[:, :, P:])
                dve.wait_ge(e["conv_exp"], b + 1)
                step(V.tensor_scalar(sig[:, :, :], sig[:, :, :], 1.0, None, ALU.add))
                step(V.reciprocal(sig[:, :, :], sig[:, :, :]))
                V.tensor_tensor(cT[:, :, :], cT[:, :, :], sig[:, :, :], ALU.mult).then_inc(e["cT_done"], 1)
                dve.wait_ge(loaded["trig"], 16 * b + 16)
                for name, bk, t0 in (("q", P1, 0), ("k", P0, 2)):
                    dve.wait_ge(e[f"r{name}_ready"], b + 1)
                    if name == "k":
                        dve.wait_ge(e["qr_done"], b + 1)
                    cos = trig[:, t0, :].rearrange("p (h d) -> p h d", h=H)
                    sin = trig[:, t0 + 1, :].rearrange("p (h d) -> p h d", h=H)
                    lo, hi = hv(bk)[:, :, 0:64], hv(bk)[:, :, 64:128]
                    V.tensor_tensor(rot[:, 0, :, :], lo, cos, ALU.mult)
                    V.tensor_tensor(rot[:, 1, :, :], hi, sin, ALU.mult)
                    V.tensor_tensor(rot[:, 2, :, :], lo, sin, ALU.mult)
                    V.tensor_tensor(rot[:, 3, :, :], hi, cos, ALU.mult).then_inc(e[name + "_parts"], 1)
                dve.wait_ge(e["w_ready"], b + 1)
                for c in range(2):
                    V.tensor_scalar(wtok[:, c, :], sm_w, half[:, c:c + 1], None, ALU.mult)
                V.tensor_copy(bc[:, :, :], sm_bc.rearrange("p (h c) -> p h c", h=H)).then_inc(e["w_copied"], 1)
                dve.wait_ge(e["scores_ready"], b + 1)
                V.tensor_tensor(scd[:, :, :], hv(RT), decay_t[:, :, :], ALU.mult).then_inc(e["scd_done"], 1)
                dve.wait_ge(e["w_copied"], b + 1)
                dve.wait_ge(e["v1_copied"], b + 1)
                for c in range(2):
                    last = V.tensor_tensor(wv[:, c, :, :], v1[:, :, :],
                                           wtok[:, c, :].unsqueeze(2).broadcast_to([P, H, P]), ALU.mult)
                last.then_inc(e["wv_done"], 1)
                dve.wait_ge(e["rg_exp"], b + 1)
                step(V.tensor_scalar(srg[:, :, :], srg[:, :, :], 1.0, None, ALU.add))
                step(V.reciprocal(srg[:, :, :], srg[:, :, :]))
                V.tensor_tensor(srg[:, :, :], hv(P1), srg[:, :, :], ALU.mult).then_inc(e["srg_done"], 1)
                dve.wait_ge(e["s_ready"], b + 1)
                for h in range(H):
                    last = V.scalar_tensor_tensor(S[:, h, :], S[:, h, :], gamma_p[h], hv(UP)[:, h, :], ALU.mult, ALU.add)
                last.then_inc(e["s_done"], 1)
                dve.wait_ge(e["mo_exp"], b + 1)
                step(V.tensor_scalar(smo[:, :, :], smo[:, :, :], 1.0, None, ALU.add))
                V.reciprocal(smo[:, :, :], smo[:, :, :]).then_inc(e["smo_done"], 1)
                for c in range(2):
                    dve.wait_ge(e[f"c{c}_ready"], b + 1)
                    if c == 1:
                        dve.wait_ge(e["num0_ready"], b + 1)
                    for h in range(H):
                        V.scalar_tensor_tensor(C[:, h, :], C[:, h, :], bc[:, h, c:c + 1], hv(UP)[:, h, :],
                                               ALU.mult, ALU.add)
                    step(V.tensor_tensor(nm[:, :], nm[:, :], bc[:, :, c], ALU.mult))
                    V.tensor_tensor(nm[:, :], nm[:, :], sm_n, ALU.add).then_inc(e[f"c{c}_done"], 1)
                dve.wait_ge(e["num1_ready"], b + 1)
                V.tensor_copy(den[0:64, 2, :], bc[0:64, :, 2])
                V.tensor_copy(den[64:128, 2, :], bc[64:128, :, 3])
                step(V.tensor_copy(den[:, 0, :], sm_den))
                step(V.scalar_tensor_tensor(den[:, 1, :], den[:, 0, :], -1.0, den[:, 0, :], ALU.mult, ALU.max))
                step(V.tensor_tensor(den[:, 1, :], den[:, 1, :], den[:, 2, :], ALU.max))
                step(V.reciprocal(den[:, 3, :], den[:, 1, :]))
                V.tensor_tensor(G[:, H:2 * H, :], hv(NM), den[:, 3, :].unsqueeze(2).broadcast_to([P, H, P]),
                                ALU.mult).then_inc(e["hm_done"], 1)
                dve.wait_ge(e["hm_done"], b + 1)
                dve.wait_ge(e["o_copied"], b + 1)
                step(V.tensor_reduce(stats[:, 0, :], G, AX, ALU.add))
                step(V.tensor_scalar(stats[:, 1, :], stats[:, 0, :], 1.0 / P, None, ALU.mult))
                V.tensor_tensor(G, G, stats[:, 1, :].unsqueeze(2).broadcast_to([P, 2 * H, P]),
                                ALU.subtract).then_inc(e["mean_done"], 1)
                dve.wait_ge(e["sq_done"], b + 1)
                step(V.tensor_reduce(stats[:, 0, :], sq.rearrange("p (h d) -> p h d", d=P), AX, ALU.add))
                V.tensor_scalar(stats[:, 2, :], stats[:, 0, :], 1.0 / P, EPS, ALU.mult, ALU.add).then_inc(
                    e["var_done"], 1)
                dve.wait_ge(e["rstd_done"], b + 1)
                V.tensor_tensor(G, G, stats[:, 0, :].unsqueeze(2).broadcast_to([P, 2 * H, P]),
                                ALU.mult).then_inc(e["g_done"], 1)
                for h in range(H):
                    last = V.tensor_scalar(sig[:, h, :], cT[:, h, :], skip[:, h:h + 1], None, ALU.mult)
                step(last)
                dve.wait_ge(e["yT_ready"], b + 1)
                for h in range(H):
                    V.scalar_tensor_tensor(yT[:, h, :], hv(TR0)[:, h, :], ret_g[:, h:h + 1], srg[:, h, :],
                                           ALU.mult, ALU.mult)
                for h in range(H):
                    last = V.scalar_tensor_tensor(sig[:, h, :], hv(TR1)[:, h, :], ml_g[:, h:h + 1], sig[:, h, :],
                                                  ALU.mult, ALU.add)
                step(last)
                V.tensor_tensor(yT[:, H:2 * H, :], sig[:, :, :], smo[:, :, :], ALU.mult).then_inc(e["ym_done"], 1)
                dve.wait_ge(e["out_ready"], b + 1)
                dve.wait_ge(loaded["xr"], 16 * b + 16)
                V.tensor_tensor(xs[:, 0:512], P0[:, :], xr[:, 0:512], ALU.add)
                V.tensor_tensor(xs[:, 512:1024], P1[:, :], xr[:, 512:1024], ALU.add).then_inc(e["x1_done"], 1)

        @block.tensor
        def _(pe):
            mm, tp = nc.tensor.matmul, nc.tensor.transpose
            pe.wait_ge(loaded["const"], 16 * 7)

            def by_token(bk, col):
                for k in range(KC):
                    last = mm(bk[:, :], hT[:, k, :], w_in[:, k, col:col + W], start=(k == 0), stop=(k == KC - 1))
                return last

            def by_channel(bk, col):
                for h in range(H):
                    for k in range(KC):
                        last = mm(hv(bk)[:, h, :], w_in[:, k, col + h * P:col + (h + 1) * P], hT[:, k, :],
                                  start=(k == 0), stop=(k == KC - 1))
                return last

            with pe.Fori(0, NB) as b:
                pe.wait_ge(e["xs_done"], b + 1)
                for k in range(KC):
                    last = tp(hv(TR0 if k < 4 else TR1)[:, k % 4, :], xs[:, k * P:(k + 1) * P], ident[:, :])
                last.then_inc(e["xT_ready"], 1)
                pe.wait_ge(e["hT_done"], b + 1)
                pe.wait_ge(loaded["g"], 16)
                for k in range(KC):
                    last = mm(sm_gate, hT[:, k, :], w_in[:, k, MI:MI + 2 * H], start=(k == 0), stop=(k == KC - 1))
                last.then_inc(e["gates_ready"], 1)
                pe.wait_ge(loaded["mx"], 16)
                by_channel(P0, MX).then_inc(e["mx_ready"], 1)
                pe.wait_ge(e["gsb_done"], b + 1)
                tp(sm_i, gsb[:, 0:H], ident[:, :])
                tp(sm_f, gsb[:, H:2 * H], ident[:, :]).then_inc(e["gateT_ready"], 1)
                pe.wait_ge(loaded["rq"], 16)
                by_token(P1, RQ).then_inc(e["rq_ready"], 1)
                pe.wait_ge(loaded["rk"], 16)
                pe.wait_ge(e["mx_copied"], b + 1)
                by_token(P0, RK).then_inc(e["rk_ready"], 1)
                pe.wait_ge(loaded["const"], 16 * 7)
                pe.wait_ge(e["gate_exp"], b + 1)
                tp(sm_w, gates[:, 2, :], ident[0:H, 0:H])
                for h in range(H):
                    last = mm(sm_bc[:, 4 * h:4 * h + 4], select[:, h, :], cat[:, :], start=True, stop=True)
                last.then_inc(e["w_ready"], 1)
                pe.wait_ge(loaded["rv"], 16)
                pe.wait_ge(e["q_parts"], b + 1)
                by_token(P1, RV).then_inc(e["rv_ready"], 1)
                pe.wait_ge(e["qr_done"], b + 1)
                for h in range(H):
                    last = tp(hv(TR0)[:, h, :], qr[:, h, :], ident[:, :])
                last.then_inc(e["qT_ready"], 1)
                pe.wait_ge(e["kr_done"], b + 1)
                for h in range(H):
                    last = tp(hv(TR1)[:, h, :], kr[:, h, :], ident[:, :])
                last.then_inc(e["kT_ready"], 1)
                pe.wait_ge(loaded["mv"], 16)
                by_token(P0, MV).then_inc(e["mv_ready"], 1)
                pe.wait_ge(e["qT_copied"], b + 1)
                pe.wait_ge(e["kT_copied"], b + 1)
                for h in range(H):
                    last = mm(hv(RT)[:, h, :], kT[:, h, :], qT[:, h, :], start=True, stop=True)
                last.then_inc(e["scores_ready"], 1)
                pe.wait_ge(loaded["rg"], 16)
                pe.wait_ge(e["v_copied"], b + 1)
                by_channel(P1, RG).then_inc(e["rg_ready"], 1)
                pe.wait_ge(e["scd_done"], b + 1)
                for h in range(H):
                    mm(hv(RT)[:, h, :], scd[:, h, :], v[:, h, :], start=True, stop=False)
                    last = mm(hv(RT)[:, h, :], qT[:, h, :], S[:, h, :], start=False, stop=True)
                last.then_inc(e["o_ready"], 1)
                for h in range(H):
                    last = mm(hv(UP)[:, h, :], kr[:, h, :], v[:, h, :], start=True, stop=True)
                last.then_inc(e["s_ready"], 1)
                pe.wait_ge(e["cT_done"], b + 1)
                for h in range(H):
                    last = mm(hv(TR0)[:, h, :], mwq[:, h, :], cT[:, h, :], start=True, stop=True)
                last.then_inc(e["mq_ready"], 1)
                for h in range(H):
                    last = mm(hv(TR1)[:, h, :], cT[:, h, :], mwk[:, h, :], start=True, stop=True)
                last.then_inc(e["mk_ready"], 1)
                pe.wait_ge(loaded["mo"], 16)
                pe.wait_ge(e["v1_copied"], b + 1)
                by_channel(P0, MO).then_inc(e["mo_ready"], 1)
                pe.wait_ge(e["wv_done"], b + 1)
                pe.wait_ge(e["mqT_copied"], b + 1)
                pe.wait_ge(e["mk_copied"], b + 1)
                for c in range(2):
                    pe.wait_ge(e["s_done" if c == 0 else "c0_done"], b + 1)
                    for h in range(H):
                        mm(hv(UP)[:, h, :], mk[:, h, :], wv[:, c, h, :], start=True, stop=True)
                    for h in range(H):
                        last = mm(sm_n[:, h:h + 1], mk[:, h, :], wtok[:, c, h:h + 1], start=True, stop=True)
                    last.then_inc(e[f"c{c}_ready"], 1)
                    pe.wait_ge(e[f"c{c}_done"], b + 1)
                    rows = slice(64 * c, 64 * c + 64)
                    for h in range(H):
                        mm(hv(NM)[rows, h, :], mqT[:, h, rows], C[:, h, :], start=True, stop=True)
                    for h in range(H):
                        last = mm(sm_den[rows, h:h + 1], mqT[:, h, rows], nm[:, h:h + 1], start=True, stop=True)
                    last.then_inc(e[f"num{c}_ready"], 1)
                pe.wait_ge(e["g_done"], b + 1)
                for h in range(2 * H):
                    last = tp(hv(TR0 if h < H else TR1)[:, h % H, :], G[:, h, :], ident[:, :])
                last.then_inc(e["yT_ready"], 1)
                pe.wait_ge(loaded["out"], 16)
                pe.wait_ge(e["ym_done"], b + 1)
                for n, bk in enumerate((P0, P1)):
                    for k in range(KC):
                        last = mm(bk[:, :], yT[:, k, :], w_out[:, k, n * 512:(n + 1) * 512],
                                  start=(k == 0), stop=(k == KC - 1))
                last.then_inc(e["out_ready"], 1)
                pe.wait_ge(e["x1_done"], b + 1)


class Count:

    def __init__(self, sem, credit=0):
        self.sem, self.credit = sem, credit

    def give(self, engine):
        engine.sem_inc(self.sem, self.credit)

    def wait(self, engine, n):
        engine.wait_ge(self.sem, n + self.credit)


def router_stage(nc, io, x1_dram, xn_dram, blocks, xt_hi, xt_lo, expert, gate, pair_t):
    T, D = io["x"].shape
    KC = D // P
    NB = T // P
    J = 2 * PEER_HEADS
    N = PEER_HEADS * TOPK
    gathered = blocks
    held = []
    with ExitStack() as ctx:
        ctx.callback(clear_semaphores, nc, held)

        def sb(name, shape, dt=F32):
            return ctx.enter_context(nc.sbuf_tensor(name, shape, dt))

        def sem(name):
            held.append(nc.alloc_semaphore(name))
            return held[-1]

        wq = sb("wq", [P, KC, J * P])
        keysT = sb("keysT", [P, J, P])
        ident = sb("ident2", [P, P])
        iota = sb("iota", [P, P])
        g2 = sb("g2", [P, D])
        xin = sb("xin", [P, D])
        xsq = sb("xsq", [P, D])
        xh = sb("xh", [P, D])
        x2T = sb("x2T", [P, KC, P])
        qT = sb("pqT", [P, J, P])
        sub = sb("sub", [P, J, P])
        sub2 = sb("sub2", [P, P])
        cand = sb("cand", [P, TOPK, TOPK])
        cand2 = sb("cand2", [P, TOPK * TOPK])
        top = sb("top", [P, J, TOPK])
        top_i = sb("top_i", [P, J, TOPK], U32)
        top_f = sb("top_f", [P, J, TOPK])
        best = sb("best", [P, PEER_HEADS, TOPK])
        soft = sb("soft", [P, 2, PEER_HEADS, TOPK])
        flat = sb("flat", [P, PEER_HEADS, TOPK], U32)
        digit = sb("digit", [P, 2, N], U32)
        digit_f = sb("digit_f", [P, 2, N])
        hit = sb("hit", [P, N, TOPK])
        picked = sb("picked", [P, 3, N])
        row_f = sb("row_f", [P, N])
        sums = sb("sums", [P, 2, PEER_HEADS])
        ss = sb("ss2", [P, 4])
        keys = sub
        banks = [ctx.enter_context(nc.psum_tensor(f"pb{i}", [P, 512], F32)) for i in range(8)]
        hv = lambda t: t[:, :].rearrange("p (h d) -> p h d", d=P)

        ld = {n: sem("r_ld_" + n) for n in ("const", "keys", "wq", "x", "xn")}
        names = ("keysT_ready keysT_done ss_done eps_done ln_done rstd_done xh_done xT_ready xT_copied xT_hi "
                 "xT_split sub_copied best_done exp_done dve_step topk_done pair_ready pair_copied").split()
        e = {n: sem("r_" + n) for n in names}
        q_ready = [sem(f"r_q_ready{i}") for i in range(4)]
        q_copied = [sem(f"r_q_copied{i}") for i in range(4)]
        s_ready = [sem(f"r_s_ready{i}") for i in range(4)]
        block = ctx.enter_context(nc.Block())

        @block.sync
        def _(sp):
            sp.dma_start(xin[:, :], x1_dram[0:P, :]).then_inc(ld["x"], 16)
            sp.dma_start(ident[:, :], io["ident"]).then_inc(ld["const"], 16)
            sp.dma_start(g2[:, :], io["norm2_g"].partition_broadcast(P)).then_inc(ld["const"], 16)
            sp.dma_start(iota[:, :], io["iota"]).then_inc(ld["const"], 16)
            sp.dma_start(keys[:, :, :], io["peer_keys"].rearrange("h t n d -> n (h t) d")).then_inc(ld["keys"], 16)
            for k in range(KC):
                sp.dma_start(wq[:, k, :], io["peer_wq"][k * P:(k + 1) * P, :]).then_inc(ld["wq"], 16)
            with sp.Fori(1, NB) as b:
                sp.wait_ge(e["xh_done"], b)
                sp.dma_start(xin[:, :], x1_dram[bass.ts(b, P), :]).then_inc(ld["x"], 16)

        @block.gpsimd
        def _(pool):
            with pool.Fori(0, gathered) as b:
                pool.wait_ge(e["xh_done"], b + 1)
                pool.dma_start(xn_dram[bass.ts(b, P), :], xh[:, :]).then_inc(ld["xn"], 16)
            pool.wait_ge(ld["xn"], 16 * gathered)

        @block.scalar
        def _(act):
            def front(b, dense):
                act.wait_ge(ld["x"], 16 * b + 16)
                nc.scalar.activation(xsq[:, :], xin[:, :], ACT.Square, accum_out=ss[:, 0:1]).then_inc(e["ss_done"], 1)
                act.wait_ge(e["eps_done"], b + 1)
                nc.scalar.activation(ss[:, 2:3], ss[:, 1:2], ACT.Ln).then_inc(e["ln_done"], 1)
                act.wait_ge(e["ln_done"], b + 1)
                nc.scalar.activation(ss[:, 3:4], ss[:, 2:3], ACT.Exp, scale=-0.5).then_inc(e["rstd_done"], 1)
                act.wait_ge(e["xT_ready"], b + 1)
                nc.scalar.copy(x2T[:, 0:4, :], hv(banks[0]))
                nc.scalar.copy(x2T[:, 4:8, :], hv(banks[1])).then_inc(e["xT_copied"], 1)
                if dense:
                    act.wait_ge(e["xT_copied"], b + 1)
                    nc.scalar.copy(xt_hi[:, :, bass.ds((b - gathered) * P, P)], x2T[:, :, :]).then_inc(e["xT_hi"], 1)
                for i in range(4):
                    act.wait_ge(q_ready[i], b + 1)
                    nc.scalar.copy(qT[:, 4 * i:4 * i + 4, :], hv(banks[2 + i])).then_inc(q_copied[i], 1)

            def scores(b):
                for i in range(4):
                    act.wait_ge(s_ready[i], b + 1)
                    nc.scalar.copy(sub[:, 4 * i:4 * i + 4, :], hv(banks[2 + i])).then_inc(e["sub_copied"], 1)

            def body(b, next_dense, last=False):
                if not last:
                    front(b + 1, next_dense)
                act.wait_ge(e["best_done"], b + 1)
                nc.scalar.activation(soft[:, 1, :, :], soft[:, 0, :, :], ACT.Exp).then_inc(e["exp_done"], 1)
                if not last:
                    scores(b + 1)

            for i in range(4):
                act.wait_ge(e["keysT_ready"], i + 1)
                nc.scalar.copy(keysT[:, 4 * i:4 * i + 4, :], hv(banks[i])).then_inc(e["keysT_done"], 1)
            front(0, False)
            scores(0)
            with act.Fori(0, gathered - 1) as b:
                body(b, False)
            with act.Fori(gathered - 1, NB - 1) as b:
                body(b, True)
            body(NB - 1, True, last=True)

        @block.tensor
        def _(pe):
            mm, tp = nc.tensor.matmul, nc.tensor.transpose

            def front(b):
                pe.wait_ge(e["xh_done"], b + 1)
                for k in range(KC):
                    last = tp(hv(banks[k // 4])[:, k % 4, :], xh[:, k * P:(k + 1) * P], ident[:, :])
                last.then_inc(e["xT_ready"], 1)
                pe.wait_ge(e["xT_copied"], b + 1)
                for j in range(J):
                    for k in range(KC):
                        last = mm(hv(banks[2 + j // 4])[:, j % 4, :], wq[:, k, j * P:(j + 1) * P], x2T[:, k, :],
                                  start=(k == 0), stop=(k == KC - 1))
                    if j % 4 == 3:
                        last.then_inc(q_ready[j // 4], 1)
                for j in range(J):
                    if j % 4 == 0:
                        pe.wait_ge(q_copied[j // 4], b + 1)
                    last = mm(hv(banks[2 + j // 4])[:, j % 4, :], qT[:, j, :], keysT[:, j, :], start=True, stop=True)
                    if j % 4 == 3:
                        last.then_inc(s_ready[j // 4], 1)

            def pairs(b):
                pe.wait_ge(ld["const"], 48)
                pe.wait_ge(e["topk_done"], b + 1)
                for i in range(3):
                    last = tp(hv(banks[6])[:, i, :], picked[:, i, :], ident[:, :])
                last.then_inc(e["pair_ready"], 1)

            pe.wait_ge(ld["const"], 48)
            pe.wait_ge(ld["keys"], 16)
            for j in range(J):
                last = tp(hv(banks[j // 4])[:, j % 4, :], keys[:, j, :], ident[:, :])
                if j % 4 == 3:
                    last.then_inc(e["keysT_ready"], 1)
            pe.wait_ge(e["keysT_done"], 4)
            pe.wait_ge(ld["wq"], 16 * KC)
            front(0)
            with pe.Fori(0, gathered) as b:
                pe.wait_ge(e["sub_copied"], 4 * b + 4)
                front(b + 1)
            with pe.Fori(gathered, NB - 1) as b:
                pe.wait_ge(e["sub_copied"], 4 * b + 4)
                front(b + 1)
                pairs(b)
            pairs(NB - 1)

        @block.vector
        def _(dve):
            V = nc.vector

            def norm(b, dense):
                dve.wait_ge(e["ss_done"], b + 1)
                V.tensor_scalar(ss[:, 1:2], ss[:, 0:1], 1.0 / D, EPS, ALU.mult, ALU.add).then_inc(e["eps_done"], 1)
                dve.wait_ge(e["rstd_done"], b + 1)
                if dense:
                    dve.wait_ge(ld["xn"], 16 * gathered)
                elif not isinstance(b, int):
                    dve.wait_ge(ld["xn"], 16 * b)
                V.scalar_tensor_tensor(xh[:, :], xin[:, :], ss[:, 3:4], g2[:, :], ALU.mult, ALU.mult).then_inc(
                    e["xh_done"], 1)

            def top16(step, values, scratch, out, index):
                step(V.max(out[:, 0:8], values))
                V.max_index(index[:, 0:8], out[:, 0:8], values)
                step(V.match_replace(scratch, out[:, 0:8], values, NEG))
                step(V.max(out[:, 8:16], scratch))
                step(V.max_index(index[:, 8:16], out[:, 8:16], scratch))

            def body(b, dense, next_dense, last=False):
                step = Chain(dve, e["dve_step"])
                dve.wait_ge(e["sub_copied"], 4 * b + 4)
                V.tensor_copy(cand2[:, 0:1], iota[:, 0:1])
                for j in range(J):
                    top16(step, sub[:, j, :], sub2[:, :], top[:, j, :], top_i[:, j, :])
                if not last:
                    norm(b + 1, next_dense)
                for h in range(PEER_HEADS):
                    step(V.tensor_tensor(cand[:, :, :], top[:, 2 * h, :].unsqueeze(2).broadcast_to([P, TOPK, TOPK]),
                                         top[:, 2 * h + 1, :].unsqueeze(1).broadcast_to([P, TOPK, TOPK]), ALU.add))
                    top16(step, cand[:, :, :].rearrange("p a c -> p (a c)"), cand2[:, :], best[:, h, :], flat[:, h, :])
                if next_dense and not last:
                    dve.wait_ge(e["xT_hi"], b + 1 - (gathered - 1))
                    cols = bass.ds((b + 1 - gathered) * P, P)
                    V.tensor_tensor(xt_lo[:, :, cols], x2T[:, :, :], xt_hi[:, :, cols].bitcast(F32), ALU.subtract)
                step(V.tensor_tensor(soft[:, 0, :, :], best[:, :, :],
                                     best[:, :, 0:1].broadcast_to([P, PEER_HEADS, TOPK]), ALU.subtract))
                V.tensor_copy(top_f[:, :, :], top_i[:, :, :]).then_inc(e["best_done"], 1)
                fl = flat[:, :, :].rearrange("p h k -> p (h k)")
                V.tensor_scalar(digit[:, 0, :], fl, 4, None, ALU.logical_shift_right)
                step(V.tensor_scalar(digit[:, 1, :], fl, 15, None, ALU.bitwise_and))
                step(V.tensor_copy(digit_f[:, :, :], digit[:, :, :]))
                if dense:
                    dve.wait_ge(e["pair_copied"], b - gathered + 1)
                for s in range(2):
                    step(V.tensor_tensor(hit[:, :, :], digit_f[:, s, :].unsqueeze(2).broadcast_to([P, N, TOPK]),
                                         iota[:, 0:TOPK].unsqueeze(1).broadcast_to([P, N, TOPK]), ALU.is_equal))
                    for h in range(PEER_HEADS):
                        hh = hit[:, h * TOPK:(h + 1) * TOPK, :]
                        last_op = V.tensor_tensor(hh, hh, top_f[:, 2 * h + s, :].unsqueeze(1).broadcast_to(
                            [P, TOPK, TOPK]), ALU.mult)
                    step(last_op)
                    step(V.tensor_reduce(picked[:, s, :], hit[:, :, :], AX, ALU.add))
                dve.wait_ge(e["exp_done"], b + 1)
                step(V.tensor_reduce(sums[:, 0, :], soft[:, 1, :, :], AX, ALU.add))
                step(V.reciprocal(sums[:, 1, :], sums[:, 0, :]))
                share = sums[:, 1, :].unsqueeze(2).broadcast_to([P, PEER_HEADS, TOPK])
                by_head = lambda t: t.rearrange("p (h k) -> p h k", h=PEER_HEADS)
                if dense:
                    V.tensor_tensor(by_head(picked[:, 2, :]), soft[:, 1, :, :], share, ALU.mult).then_inc(
                        e["topk_done"], 1)
                    dve.wait_ge(e["pair_ready"], b - gathered + 1)
                    V.tensor_copy(pair_t[:, :, bass.ds((b - gathered) * P, P)], hv(banks[6])[:, 0:3, :]).then_inc(
                        e["pair_copied"], 1)
                else:
                    step(V.tensor_tensor(by_head(gate[:, bass.ds(b * N, N)]), soft[:, 1, :, :], share, ALU.mult))
                    step(V.scalar_tensor_tensor(row_f[:, :], picked[:, 0, :], float(P), picked[:, 1, :], ALU.mult,
                                                ALU.add))
                    V.tensor_copy(expert[:, bass.ds(b * N, N)], row_f[:, :]).then_inc(e["topk_done"], 1)

            dve.wait_ge(ld["const"], 48)
            V.memset(expert[:, gathered * N:], 0).then_inc(e["pair_copied"], 1)
            norm(0, False)
            with dve.Fori(0, gathered - 1) as b:
                body(b, False, False)
            body(gathered - 1, False, True)
            with dve.Fori(gathered, NB - 1) as b:
                body(b, True, True)
            body(NB - 1, True, True, last=True)


def pair_stage(nc, io, g_dram, pair_t, blocks):
    GROUP, SLOTS = 4, 8
    PER = SLOTS
    held = []
    with ExitStack() as ctx:
        ctx.callback(clear_semaphores, nc, held)

        def sb(name, shape, dt=F32):
            return ctx.enter_context(nc.sbuf_tensor(name, shape, dt))

        def sem(name):
            held.append(nc.alloc_semaphore(name))
            return held[-1]

        first = [sb(f"first{i}", [P, P]) for i in range(SLOTS)]
        second = [sb(f"second{i}", [P, P]) for i in range(SLOTS)]
        iota = sb("iota2", [P, P])
        whole = [sb(f"whole{i}", [P, P, P]) for i in range(2)]
        banks = [ctx.enter_context(nc.psum_tensor(f"gb{i}", [P, 512], F32)) for i in range(2)]
        iota_in, stored = sem("g_iota_in"), [sem(f"g_stored{i}") for i in range(2)]
        hot = [sem(f"g_hot{i}") for i in range(2)]
        used = [Count(sem(f"g_used{i}"), 1) for i in range(2)]
        copied = [Count(sem(f"g_copied{i}"), 1) for i in range(2)]
        block = ctx.enter_context(nc.Block())
        LOOPS = P // PER

        @block.sync
        def _(sp):
            sp.dma_start(iota[:, :], io["iota"]).then_inc(iota_in, 16)
            for b in range(blocks):
                for i in range(2):
                    copied[i].wait(sp, (b + 1) * LOOPS)
                sp.dma_start(g_dram[:, :, b * P:(b + 1) * P].rearrange("a c t -> c a t"), whole[b % 2][:, :, :]).then_inc(
                    stored[b % 2], 16)
            for i in range(2):
                sp.wait_ge(stored[i], 16 * (blocks // 2))

        @block.vector
        def _(dve):
            dve.wait_ge(iota_in, 16)
            with dve.Fori(0, blocks * LOOPS) as n:
                for i in range(2):
                    used[i].wait(dve, n)
                    for t in range(GROUP):
                        at = bass.ds(n * PER + (i * GROUP + t), 1)
                        slot = i * GROUP + t
                        nc.vector.tensor_scalar(first[slot][:, :], iota[:, :], pair_t[:, 0, at], pair_t[:, 2, at],
                                                ALU.is_equal, ALU.mult)
                        last = nc.vector.tensor_scalar(second[slot][:, :], iota[:, :], pair_t[:, 1, at], None,
                                                       ALU.is_equal)
                    last.then_inc(hot[i], 1)

        @block.tensor
        def _(pe):
            for i in range(2):
                used[i].give(pe)
            with pe.Fori(0, blocks * LOOPS) as n:
                for i in range(2):
                    pe.wait_ge(hot[i], n + 1)
                    copied[i].wait(pe, n)
                    for t in range(GROUP):
                        slot = i * GROUP + t
                        last = nc.tensor.matmul(banks[i][:, t * P:(t + 1) * P], second[slot][:, :], first[slot][:, :],
                                                start=True, stop=True)
                    last.then_inc(used[i].sem, 1)

        @block.scalar
        def _(act):
            for i in range(2):
                copied[i].give(act)
            for b in range(blocks):
                if b >= 2:
                    act.wait_ge(stored[b % 2], 16 * (b // 2))
                with act.Fori(0, LOOPS) as n:
                    for i in range(2):
                        used[i].wait(act, n + (b * LOOPS + 1))
                        nc.scalar.copy(whole[b % 2][:, :, bass.ds(n * PER + i * GROUP, GROUP)],
                                       banks[i][:, :].rearrange("p (t a) -> p a t", t=GROUP)).then_inc(copied[i].sem, 1)


def expert_stage(nc, io, x1_dram, xn_dram, g_dram, xt_hi, xt_lo, expert, gate, blocks, out):
    T, D = io["x"].shape
    NB = T // P
    KC = D // P
    NH = PEER_HEADS
    DENSE = NB - blocks
    TD = DENSE * P
    WINDOWS = io["peer_down"].shape[0] // P // 2
    assert WINDOWS == 2 * NH * blocks and DENSE == 4
    held = []
    with ExitStack() as ctx:
        ctx.callback(clear_semaphores, nc, held)

        def sb(name, shape, dt=F32):
            return ctx.enter_context(nc.sbuf_tensor(name, shape, dt))

        def sem(name):
            held.append(nc.alloc_semaphore(name))
            return held[-1]

        down = [sb(f"down{i}", [P, D]) for i in range(DOWN_RING)]
        up = [sb(f"up{i}", [P, D]) for i in range(UP_RING)]
        fg = sb("fg", [P, D])
        xg = sb("xg", [P, D])
        xng = sb("xng", [P, D])
        rows = [sb(f"rows{i}", [P, TOPK], U32) for i in range(2)]
        act_in = sb("act_in", [P, TOPK])
        act_out = sb("act_out", [P, TOPK])
        weight = sb("weight", [P, TOPK])
        ss = sb("ss3", [P, 4])
        ident = sb("ident3", [P, P])
        raw = [sb(f"raw{j}", [P, D]) for j in range(2)]
        dt_hi = [sb(f"dt_hi{j}", [P, KC, P], F32R) for j in range(2)]
        dt_lo = [sb(f"dt_lo{j}", [P, KC, P], F32R) for j in range(2)]
        upr = [sb(f"upr{j}", [P, D]) for j in range(2)]
        up_hi = [[sb(f"up_hi{w}{j}", [P, D], F32R) for j in range(2)] for w in range(2)]
        up_lo = [[sb(f"up_lo{w}{j}", [P, D], F32R) for j in range(2)] for w in range(2)]
        gw = [sb(f"gw{j}", [P, TD]) for j in range(2)]
        pr = [sb(f"pr{j}", [P, TD]) for j in range(2)]
        s_hi = [[sb(f"s_hi{w}{j}", [P, TD], F32R) for j in range(2)] for w in range(2)]
        s_lo = [[sb(f"s_lo{w}{j}", [P, TD], F32R) for j in range(2)] for w in range(2)]
        xo = sb("xo", [P, DENSE, D])
        done = sb("done", [P, D])
        TR = [ctx.enter_context(nc.psum_tensor(f"tr{i}", [P, 512], F32)) for i in range(2)]
        PB = [ctx.enter_context(nc.psum_tensor(f"pj{i}", [P, 512], F32)) for i in range(2)]
        OB = [ctx.enter_context(nc.psum_tensor(f"ob{i}", [P, 512], F32)) for i in range(4)]
        hv = lambda t: t[:, :].rearrange("p (h d) -> p h d", d=P)

        down_in = [sem(f"x_down_in{i}") for i in range(DOWN_RING)]
        up_in = [sem(f"x_up_in{i}") for i in range(UP_RING)]
        names = ("rows_set gelu_g weighed ss_done eps_done ln_done rstd_done out_done stored fg_in xg_in "
                 "xng_in ident_in xo_in u_ready cleared norm_start").split()
        e = {n: sem("x_" + n) for n in names}
        dots, sums = Count(sem("x_dots"), DOWN_RING), Count(sem("x_sums"), UP_RING)
        adds = Count(sem("x_adds"), 2)
        two = lambda name: [sem(f"x_{name}{j}") for j in range(2)]
        free = lambda name: [Count(sem(f"x_{name}{j}"), 1) for j in range(2)]
        raw_in, upr_in, gw_in = two("raw_in"), two("upr_in"), two("gw_in")
        t_done, hi_done, p_ready = free("t_done"), two("hi_done"), two("p_ready")
        gelu_d, shi_done, uphi_done = free("gelu_d"), two("shi_done"), two("uphi_done")
        lo_done, pg_done, slo_done, uplo_done = free("lo_done"), free("pg_done"), free("slo_done"), free("uplo_done")
        block = ctx.enter_context(nc.Block())
        down_rows, up_rows = io["peer_down"], io["peer_up"]

        @block.sync
        def _(sp):
            def fetch(w, j, chunk):
                t_done[j].wait(sp, w)
                sp.dma_start(raw[j][:, :], down_rows[bass.ts(chunk, P), :]).then_inc(raw_in[j], 16)
                pg_done[j].wait(sp, w)
                sp.dma_start(gw[j][:, :], g_dram[bass.ds(chunk, 1), :, :].rearrange("a c t -> c (a t)")).then_inc(
                    gw_in[j], 16)
                uplo_done[j].wait(sp, w)
                sp.dma_start(upr[j][:, :], up_rows[bass.ts(chunk, P), :]).then_inc(upr_in[j], 16)

            sp.dma_start(ident[:, :], io["ident"]).then_inc(e["ident_in"], 16)
            for j in range(2):
                fetch(0, j, j)
            sp.dma_start(xo[:, :, :], x1_dram[blocks * P:, :].rearrange("(b p) d -> p b d", p=P)).then_inc(
                e["xo_in"], 16)
            sp.dma_start(fg[:, :], io["final_g"].partition_broadcast(P)).then_inc(e["fg_in"], 16)
            with sp.Fori(1, WINDOWS) as w:
                for j in range(2):
                    fetch(w, j, w * 2 + j)
            t_done[0].wait(sp, WINDOWS)
            sp.dma_start(raw[0][:, :], down_rows[0:P, :]).then_inc(raw_in[0], 16)

        @block.gpsimd
        def _(pool):
            turns = pool.alloc_register("turns")

            def counted(count, n):
                pool.reg_mov(turns, n + count.credit)
                pool.wait_ge(e["rows_set"], 1)
                pool.wait_ge(count.sem, turns)

            def gather(table, buf, index, arrived):
                nc.gpsimd.indirect_dma_start(
                    buf[:, :], None, table, bass.IndirectOffsetOnAxis(ap=index, axis=0)).then_inc(arrived, 16)

            def low_part(w, turn, j):
                pool.wait_ge(uphi_done[j], w + 1)
                nc.gpsimd.tensor_tensor(up_lo[turn][j][:, :], upr[j][:, :], up_hi[turn][j][:, :].bitcast(F32),
                                        ALU.subtract).then_inc(uplo_done[j].sem, 1)

            for j in range(2):
                for t in (s_hi[1][j], s_lo[1][j], up_hi[1][j], up_lo[1][j]):
                    nc.gpsimd.memset(t[:, :].bitcast(F32), 0.0).then_inc(e["cleared"], 1)
                uplo_done[j].give(pool)
            with pool.Fori(0, blocks * NH // 2) as pair:
                for turn in range(2):
                    g = pair * 2 + turn
                    counted(Count(e["rows_set"]), g + 1)
                    for k in range(TOPK):
                        counted(dots, g * TOPK + (k - DOWN_RING + 1))
                        gather(down_rows, down[k % DOWN_RING], rows[turn][:, k:k + 1], down_in[k % DOWN_RING])
                        if k in (7, 12):
                            low_part(g * 2, 0, int(k == 12))
                    for k in range(TOPK):
                        counted(sums, g * TOPK + (k - UP_RING + 1))
                        gather(up_rows, up[k % UP_RING], rows[turn][:, k:k + 1], up_in[k % UP_RING])
                        if k in (9, 14):
                            low_part(g * 2 + 1, 1, int(k == 14))

        @block.tensor
        def _(pe):
            mm, tp = nc.tensor.matmul, nc.tensor.transpose

            def turn_down(w, j, n_before):
                pe.wait_ge(raw_in[j], w * 16 + 16)
                lo_done[1 - j].wait(pe, n_before)
                for k in range(KC):
                    last = tp(hv(TR[k // 4])[:, k % 4, :], raw[j][:, k * P:(k + 1) * P], ident[:, :])
                last.then_inc(t_done[j].sem, 1)

            def activations(w, j):
                lo_done[j].wait(pe, w + 1)
                gelu_d[j].wait(pe, w)
                parts = ((dt_hi, xt_hi), (dt_lo, xt_hi), (dt_hi, xt_lo))
                for k in range(KC):
                    for n, (a, x) in enumerate(parts):
                        last = mm(PB[j][:, :], a[j][:, k, :], x[:, k, :], start=(k == 0 and n == 0),
                                  stop=(k == KC - 1 and n == 2))
                last.then_inc(p_ready[j], 1)

            def outputs(v, turn):
                for j in range(2):
                    slo_done[j].wait(pe, v)
                    uplo_done[j].wait(pe, v)
                for tb in range(DENSE):
                    adds.wait(pe, v * DENSE + (tb - 1))
                    tok = slice(tb * P, (tb + 1) * P)
                    for half in range(2):
                        d = slice(half * 512, half * 512 + 512)
                        n = 0
                        for j in range(2):
                            for a, u in ((s_hi, up_hi), (s_lo, up_hi), (s_hi, up_lo)):
                                last = mm(OB[(tb % 2) * 2 + half][:, :], a[turn][j][:, tok], u[turn][j][:, d],
                                          start=(n == 0), stop=(n == 5))
                                n += 1
                    last.then_inc(e["u_ready"], 1)

            for j in range(2):
                t_done[j].give(pe)
            pe.wait_ge(e["ident_in"], 16)
            pe.wait_ge(e["cleared"], 8)
            turn_down(0, 0, 0)
            with pe.Fori(0, WINDOWS // 2) as pair:
                for turn in range(2):
                    w = pair * 2 + turn
                    turn_down(w, 1, w + 1)
                    activations(w, 0)
                    turn_down(w + 1, 0, w + 1)
                    activations(w, 1)
                    outputs(w, 1 - turn)
            outputs(WINDOWS, 1)

        @block.scalar
        def _(act):
            A = nc.scalar

            def split_down(w, j):
                t_done[j].wait(act, w + 1)
                A.copy(dt_hi[j][:, 0:4, :], hv(TR[0]))
                A.copy(dt_hi[j][:, 4:8, :], hv(TR[1])).then_inc(hi_done[j], 1)

            def gelu(w, j):
                act.wait_ge(p_ready[j], w + 1)
                pg_done[j].wait(act, w)
                shi_free = w
                A.activation(pr[j][:, :], PB[j][:, :], ACT.Gelu).then_inc(gelu_d[j].sem, 1)

            def split_up(w, turn, j):
                act.wait_ge(upr_in[j], w * 16 + 16)
                A.copy(up_hi[turn][j][:, :], upr[j][:, :]).then_inc(uphi_done[j], 1)

            def split_s(w, turn, j):
                pg_done[j].wait(act, w + 1)
                A.copy(s_hi[turn][j][:, :], pr[j][:, :]).then_inc(shi_done[j], 1)

            def window(w, turn):
                split_down(w, 1)
                gelu(w, 0)
                split_down(w + 1, 0)
                split_up(w, turn, 0)
                split_s(w, turn, 0)
                gelu(w, 1)
                split_up(w, turn, 1)
                split_s(w, turn, 1)

            def root(n):
                act.wait_ge(e["eps_done"], n)
                A.activation(ss[:, 2:3], ss[:, 1:2], ACT.Ln).then_inc(e["ln_done"], 1)
                act.wait_ge(e["ln_done"], n)
                A.activation(ss[:, 3:4], ss[:, 2:3], ACT.Exp, scale=-0.5).then_inc(e["rstd_done"], 1)

            for j in range(2):
                gelu_d[j].give(act)
            split_down(0, 0)
            with act.Fori(0, blocks) as b:
                act.dma_start(xng[:, :], xn_dram[bass.ts(b, P), :]).then_inc(e["xng_in"], 16)
                act.dma_start(xg[:, :], x1_dram[bass.ts(b, P), :]).then_inc(e["xg_in"], 16)
                with act.Fori(0, NH) as h:
                    g = b * NH + h
                    window(g * 2, 0)
                    dots.wait(act, g * TOPK + TOPK)
                    A.activation(act_out[:, :], act_in[:, :], ACT.Gelu).then_inc(e["gelu_g"], 1)
                    window(g * 2 + 1, 1)
                act.wait_ge(e["norm_start"], b + 1)
                A.activation(done[:, :], xg[:, :], ACT.Square, accum_out=ss[:, 0:1]).then_inc(e["ss_done"], 1)
                root(b + 1)
                act.wait_ge(e["out_done"], b + 1)
                act.dma_start(out[bass.ts(b, P), :], done[:, :]).then_inc(e["stored"], 16)
                act.wait_ge(e["stored"], b * 16 + 16)
            for t in range(DENSE):
                n = blocks + t
                adds.wait(act, DENSE * WINDOWS + t + 1)
                A.activation(done[:, :], xo[:, t, :], ACT.Square, accum_out=ss[:, 0:1]).then_inc(e["ss_done"], 1)
                root(n + 1)
                act.wait_ge(e["out_done"], n + 1)
                act.dma_start(out[n * P:(n + 1) * P, :], done[:, :]).then_inc(e["stored"], 16)
                act.wait_ge(e["stored"], n * 16 + 16)

        @block.vector
        def _(dve):
            V = nc.vector

            def set_rows(g, turn):
                V.tensor_copy(rows[turn][:, :], expert[:, bass.ds(g * TOPK, TOPK)]).then_inc(e["rows_set"], 1)

            def dot(g, k):
                slot = down[k % DOWN_RING][:, :]
                per = 16 * (TOPK // DOWN_RING)
                dve.wait_ge(down_in[k % DOWN_RING], g * per + (16 * (k // DOWN_RING) + 16))
                V.scalar_tensor_tensor(slot, slot, 1.0, xng[:, :], ALU.mult, ALU.mult,
                                       accum_out=act_in[:, k:k + 1]).then_inc(dots.sem, 1)

            def add_row(g, k):
                slot = up[k % UP_RING][:, :]
                per = 16 * (TOPK // UP_RING)
                dve.wait_ge(up_in[k % UP_RING], g * per + (16 * (k // UP_RING) + 16))
                if k > 0:
                    sums.wait(dve, g * TOPK + k)
                V.scalar_tensor_tensor(xg[:, :], slot, weight[:, k:k + 1], xg[:, :], ALU.mult, ALU.add).then_inc(
                    sums.sem, 1)

            def split_down(w, j):
                dve.wait_ge(hi_done[j], w + 1)
                for i in range(2):
                    last = V.tensor_tensor(dt_lo[j][:, 4 * i:4 * i + 4, :], hv(TR[i]),
                                           dt_hi[j][:, 4 * i:4 * i + 4, :].bitcast(F32), ALU.subtract)
                last.then_inc(lo_done[j].sem, 1)

            def by_gate(w, j):
                dve.wait_ge(gw_in[j], w * 16 + 16)
                gelu_d[j].wait(dve, w + 1)
                V.tensor_tensor(pr[j][:, :], pr[j][:, :], gw[j][:, :], ALU.mult).then_inc(pg_done[j].sem, 1)

            def split_s(w, turn, j):
                dve.wait_ge(shi_done[j], w + 1)
                V.tensor_tensor(s_lo[turn][j][:, :], pr[j][:, :], s_hi[turn][j][:, :].bitcast(F32),
                                ALU.subtract).then_inc(slo_done[j].sem, 1)

            def add_out(v, tb):
                dve.wait_ge(e["u_ready"], v * DENSE + (tb + 1))
                for half in range(2):
                    d = slice(half * 512, half * 512 + 512)
                    last = V.tensor_tensor(xo[:, tb, d], OB[(tb % 2) * 2 + half][:, :], xo[:, tb, d], ALU.add)
                last.then_inc(adds.sem, 1)

            def window(w, turn, row):
                split_down(w, 1)
                for k in range(4):
                    row(k)
                split_down(w + 1, 0)
                by_gate(w, 0)
                row(4), row(5)
                split_s(w, turn, 0)
                row(6), row(7)
                by_gate(w, 1)
                row(8), row(9)
                split_s(w, turn, 1)
                row(10)
                add_out(w, 0)
                row(11)
                add_out(w, 1)
                row(12), row(13)
                add_out(w, 2)
                row(14), row(15)
                add_out(w, 3)

            def finish(n, rows_in):
                dve.wait_ge(e["ss_done"], n)
                V.tensor_scalar(ss[:, 1:2], ss[:, 0:1], 1.0 / D, EPS, ALU.mult, ALU.add).then_inc(e["eps_done"], 1)
                dve.wait_ge(e["rstd_done"], n)
                V.scalar_tensor_tensor(done[:, :], rows_in, ss[:, 3:4], fg[:, :], ALU.mult, ALU.mult).then_inc(
                    e["out_done"], 1)

            dots.give(dve)
            sums.give(dve)
            adds.give(dve)
            for j in range(2):
                lo_done[j].give(dve)
                pg_done[j].give(dve)
                slo_done[j].give(dve)
            dve.wait_ge(e["fg_in"], 16)
            dve.wait_ge(e["xo_in"], 16)
            set_rows(0, 0)
            set_rows(1, 1)
            split_down(0, 0)
            with dve.Fori(0, blocks) as b:
                with dve.Fori(0, NH // 2) as pair:
                    for turn in range(2):
                        g = b * NH + pair * 2 + turn
                        dve.wait_ge(e["xng_in"], b * 16 + 16)
                        window(g * 2, 0, lambda k: dot(g, k))
                        dve.wait_ge(e["gelu_g"], g + 1)
                        V.tensor_tensor(weight[:, :], act_out[:, :], gate[:, bass.ds(g * TOPK, TOPK)],
                                        ALU.mult).then_inc(e["weighed"], 1)
                        dve.wait_ge(e["xg_in"], b * 16 + 16)
                        dve.wait_ge(e["weighed"], g + 1)
                        window(g * 2 + 1, 1, lambda k: add_row(g, k))
                        sums.wait(dve, g * TOPK + TOPK)
                        set_rows(g + 2, turn)
                V.tensor_copy(weight[:, 0:1], xg[:, 0:1]).then_inc(e["norm_start"], 1)
                finish(b + 1, xg[:, :])
            for tb in range(DENSE):
                add_out(WINDOWS, tb)
            for t in range(DENSE):
                finish(blocks + t + 1, xo[:, t, :])


def build(nc, io, out):
    T, D = io["x"].shape
    NB = T // P
    N = PEER_HEADS * TOPK
    gathered = NB // 2
    dense = (NB - gathered) * P
    x1_dram = nc.dram_tensor("x1_scratch", (T, D), F32, kind="Internal").ap()
    xn_dram = nc.dram_tensor("xn_scratch", (gathered * P, D), F32, kind="Internal").ap()
    g_dram = nc.dram_tensor("gate_scratch", (P, P, dense), F32, kind="Internal").ap()
    mix_stage(nc, io, x1_dram)
    with ExitStack() as ctx:
        xt_hi = ctx.enter_context(nc.sbuf_tensor("xt_hi", [P, D // P, dense], F32R))
        xt_lo = ctx.enter_context(nc.sbuf_tensor("xt_lo", [P, D // P, dense], F32R))
        expert = ctx.enter_context(nc.sbuf_tensor("expert", [P, gathered * N + 2 * TOPK], U32))
        gate = ctx.enter_context(nc.sbuf_tensor("gate", [P, gathered * N], F32))
        with ExitStack() as inner:
            pair_t = inner.enter_context(nc.sbuf_tensor("pair_t", [P, 3, dense], F32))
            router_stage(nc, io, x1_dram, xn_dram, gathered, xt_hi, xt_lo, expert, gate, pair_t)
            pair_stage(nc, io, g_dram, pair_t, NB - gathered)
        expert_stage(nc, io, x1_dram, xn_dram, g_dram, xt_hi, xt_lo, expert, gate, gathered, out)


def shape_constants(np, T):
    H, half_w = 4, 64
    gamma = 1.0 - 2.0 ** (-5.0 - np.arange(H, dtype=np.float64))
    inv = (np.float64(10000.0) ** (-np.arange(half_w, dtype=np.float64) / half_w)).astype(np.float32)
    angle = (np.arange(T, dtype=np.float32)[:, None] * inv[None, :]).astype(np.float64)
    place = np.arange(T) % P
    q_decay = gamma[None, :] ** (place[:, None] + 1.0)
    k_decay = gamma[None, :] ** (P - 1.0 - place[:, None]) * float(P) ** -0.5
    trig = np.stack([f(angle)[:, None, :] * d[:, :, None] for d in (q_decay, k_decay) for f in (np.cos, np.sin)], 1)
    l, m = np.arange(P)[None, :], np.arange(P)[:, None]
    same, past = l // 64 == m // 64, l // 64 > m // 64
    power = np.where(same, np.abs(l - m), l - m) - (l + 1.0) - (P - 1.0 - m)
    decay = np.where((same | past)[None], gamma[:, None, None] ** power[None], 0.0)
    one = np.float32
    return {
        "ident": np.eye(P, dtype=one),
        "iota": np.tile(np.arange(P, dtype=one), (P, 1)),
        "trig": trig.reshape(T, 4, H * half_w).astype(one),
        "decay_t": np.ascontiguousarray(decay.transpose(1, 0, 2)).astype(one),
        "select": np.ascontiguousarray(np.repeat(np.eye(H, dtype=one)[:, :, None], P, axis=2)),
        "reset": np.tile((np.arange(P) % 64 != 0).astype(one), (H, 1)),
        "half": np.stack([np.arange(P) < 64, np.arange(P) >= 64], 1).astype(one),
    }


_LAYER = ["norm1_g", "w_in", "ret_norm_g", "m_conv_w", "m_conv_b", "m_wq", "m_wk", "m_b_i", "m_b_f", "m_norm_g",
          "m_skip", "w_out", "norm2_g", "peer_wq", "peer_keys", "peer_down", "peer_up"]


def kernel(**inputs):
    import numpy as np
    import concourse.bacc as bacc
    from concourse.bass_utils import run_bass_kernel_spmd

    x = np.ascontiguousarray(inputs["x"])
    arrays = {"x": x[0], "final_g": np.ascontiguousarray(inputs["final_g"])}
    for name in _LAYER:
        arrays[name] = np.ascontiguousarray(inputs[name])[0]
    arrays.update(shape_constants(np, x.shape[1]))
    nc = bacc.Bacc("TRN2", target_bir_lowering=False, num_devices=1)
    io = {name: nc.dram_tensor(f"in_{name}", a.shape, mybir.dt.from_np(a.dtype), kind="ExternalInput").ap()
          for name, a in arrays.items()}
    out = nc.dram_tensor("out_x", x.shape[1:], F32, kind="ExternalOutput").ap()
    build(nc, io, out)
    r = run_bass_kernel_spmd(nc, [{f"in_{n}": a for n, a in arrays.items()}], core_ids=[0])
    return r.results[0]["out_x"].reshape(x.shape)
```

```python
from contextlib import ExitStack

import concourse.bass as bass
from concourse import mybir

F32 = mybir.dt.float32
F32R = mybir.dt.float32r
U32 = mybir.dt.uint32
ALU = mybir.AluOpType
ACT = mybir.ActivationFunctionType
AX = mybir.AxisListType.X

P = 128
EPS = 1e-6
CONV_W = 4
NEG = -3.0e38
PEER_HEADS = 8
TOPK = 16
PAIRS = 64
RING = 8


def retention_block_decay():
    return [float((1.0 - 2.0 ** (-5.0 - h)) ** P) for h in range(4)]


class Chain:

    def __init__(self, engine, sem):
        self.engine, self.sem, self.n = engine, sem, 0
        engine.sem_clear(sem)

    def __call__(self, instruction):
        self.n += 1
        instruction.then_inc(self.sem, 1)
        self.engine.wait_ge(self.sem, self.n)


def clear_semaphores(nc, held):
    nc.clear_and_free_semaphores(held)
    nc.all_engine_barrier()


def router_weights(weights):
    W = 4 * P
    return (weights[:, :, 0:4 * W], weights[:, :, 4 * W:6 * W], weights[:, 0:4, 6 * W:7 * W],
            weights[:, 4:8, 6 * W:7 * W])


def mix_stage(nc, io, y_dram, weights, ident):
    T, D = io["x"].shape
    KC = D // P
    NB = T // P
    H = 4
    W = H * P
    RQ, RK, RV, RG, MX, MV, MO, MI = [W * i for i in range(8)]
    gamma_p = retention_block_decay()

    held = []
    with ExitStack() as ctx:
        ctx.callback(clear_semaphores, nc, held)

        def sb(name, shape, dt=F32):
            return ctx.enter_context(nc.sbuf_tensor(name, shape, dt))

        def bank(name):
            return ctx.enter_context(nc.psum_tensor(name, [P, 512], F32))

        def sem(name):
            held.append(nc.alloc_semaphore(name))
            return held[-1]

        w_in = weights
        mwq = sb("mwq", [P, H, P])
        mwk = sb("mwk", [P, H, P])
        decay_t = sb("decay_t", [P, H, P])
        select = sb("select", [H, H, P])
        reset = sb("reset", [H, P])
        half = sb("half", [P, 2])
        g1 = sb("g1", [P, KC])
        ret_g = sb("ret_g", [P, H])
        ml_g = sb("ml_g", [P, H])
        skip = sb("skip", [P, H])
        conv_w = sb("conv_w", [P, CONV_W, H])
        conv_b = sb("conv_b", [P, H])
        b_i = sb("b_i", [H, 1])
        b_f = sb("b_f", [H, 1])
        xa = sb("xa", [P, D])
        xs = sb("xs", [P, D])
        trig = sb("trig", [P, 4, 4 * 64])
        hT = sb("hT", [P, KC, P])
        ss = sb("ss", [P, 4])
        mxb = sb("mxb", [P, H, P + CONV_W - 1])
        cT = sb("cT", [P, H, P])
        sig = sb("sig", [P, H, P])
        skc = sb("skc", [P, H, P])
        srg = sb("srg", [P, H, P])
        smo = sb("smo", [P, H, P])
        rot = sb("rot", [P, 4, H, 64])
        qr = sb("qr", [P, H, P])
        kr = sb("kr", [P, H, P])
        v = sb("v", [P, H, P])
        v1 = sb("v1", [P, H, P])
        wv = sb("wv", [P, 2, H, P])
        qT = sb("qT", [P, H, P])
        kT = sb("kT", [P, H, P])
        gsb = sb("gsb", [P, 2 * H])
        gates = sb("gates", [H, 7, P])
        small = sb("small", [H, 24])
        cat = sb("cat", [H, 4])
        wtok = sb("wtok", [P, 2, H])
        bc = sb("bc", [P, H, 4])
        den = sb("den", [P, 4, H])
        stats = sb("stats", [P, 3, 2 * H])
        G = sb("G", [P, 2 * H, P])
        sq = sb("sq", [P, 2 * H, P])
        yT = sb("yT", [P, 2 * H, P])
        S = sb("S", [P, H, P])
        C = sb("C", [P, H, P])
        nm = sb("nm", [P, H])
        m_seq = sb("m_seq", [H, 3])
        scd, mqT, mk = qr, qT, kT

        P0, P1, TR0, TR1, RT, UP, NM, SM = [bank(f"bank{i}") for i in range(8)]
        hv = lambda t: t[:, :].rearrange("p (h d) -> p h d", d=P)
        sm_gate, sm_i, sm_f = SM[:, 0:8], SM[0:H, 16:144], SM[0:H, 144:272]
        sm_w, sm_bc = SM[:, 272:276], SM[:, 276:292]
        sm_n, sm_den = SM[:, 292:296], SM[:, 296:300]

        names = ("ss_done eps_done xs_done xT_ready hT_done gates_ready gsb_done mx_ready mx_copied conv_done "
                 "conv_exp cT_done gateT_ready gate_read gate_abs gate_log gate_diff gate_exp w_ready w_copied "
                 "rq_ready q_parts qr_done rk_ready k_parts kr_done rv_ready v_copied mv_ready v1_copied "
                 "qT_ready qT_copied kT_ready kT_copied scores_ready scd_done rg_ready rg_exp srg_done "
                 "mo_ready mo_exp smo_done wv_done o_ready o_copied s_ready s_done mq_ready mqT_copied "
                 "mk_ready mk_copied c0_ready c0_done c1_ready c1_done num0_ready num1_ready den_read hm_done "
                 "mean_done sq_done var_done ln_done rstd_done g_done yT_ready ym_done dve_step act_step").split()
        e = {n: sem(n) for n in names}
        loaded = {n: sem("ld_" + n) for n in ("ident", "tables", "late", "small", "mx", "g", "rq", "rk", "rv", "mv",
                                              "rg", "mo",
                                              "xa", "trig", "next")}
        y_stored, zeroed = sem("y_stored"), sem("zeroed")
        block = ctx.enter_context(nc.Block())
        SMALL, TABLES, LATE = 11, 3, 3

        @block.sync
        def _(sp):
            win = io["w_in"].rearrange("(k p) n -> p k n", p=P)

            def columns(name, col, n=W):
                sp.dma_start(w_in[:, :, col:col + n], win[:, :, col:col + n]).then_inc(loaded[name], 16)

            sp.dma_start(xa[:, :], io["x"][0:P, :]).then_inc(loaded["xa"], 16)
            sp.dma_start(ident[:, :], io["ident"]).then_inc(loaded["ident"], 16)
            with nc.allow_non_contiguous_dma(reason="small per-channel vectors"):
                sp.dma_start(g1[:, :], io["norm1_g"].rearrange("(k p) -> p k", p=P)).then_inc(loaded["small"], 16)
                columns("g", MI, 2 * H)
                columns("mx", MX)
                sp.dma_start(ret_g[:, :], io["ret_norm_g"].rearrange("h p -> p h")).then_inc(loaded["small"], 16)
                sp.dma_start(ml_g[:, :], io["m_norm_g"].rearrange("h p -> p h")).then_inc(loaded["small"], 16)
                sp.dma_start(skip[:, :], io["m_skip"].rearrange("(h p) -> p h", p=P)).then_inc(loaded["small"], 16)
                sp.dma_start(conv_b[:, :], io["m_conv_b"].rearrange("(h p) -> p h", p=P)).then_inc(loaded["small"], 16)
                for j in range(CONV_W):
                    sp.dma_start(conv_w[:, j, :], io["m_conv_w"][j].rearrange("(h p) -> p h", p=P)).then_inc(
                        loaded["small"], 16)
                sp.dma_start(b_i[:, :], io["m_b_i"].rearrange("(h a) -> h a", a=1)).then_inc(loaded["small"], 16)
                sp.dma_start(b_f[:, :], io["m_b_f"].rearrange("(h a) -> h a", a=1)).then_inc(loaded["small"], 16)
            columns("rq", RQ)
            sp.dma_start(trig[:, :, :], io["trig"][0:P, :, :]).then_inc(loaded["trig"], 16)
            columns("rk", RK)
            sp.dma_start(reset[:, :], io["reset"]).then_inc(loaded["tables"], 16)
            sp.dma_start(half[:, :], io["half"]).then_inc(loaded["tables"], 16)
            sp.dma_start(select[:, :, :], io["select"]).then_inc(loaded["tables"], 16)
            columns("rv", RV)
            columns("mv", MV)
            columns("rg", RG)
            columns("mo", MO)
            sp.dma_start(decay_t[:, :, :], io["decay_t"]).then_inc(loaded["late"], 16)
            sp.dma_start(mwq[:, :, :], io["m_wq"].rearrange("h d e -> d h e")).then_inc(loaded["late"], 16)
            sp.dma_start(mwk[:, :, :], io["m_wk"].rearrange("h d e -> d h e")).then_inc(loaded["late"], 16)
            with sp.Fori(1, NB) as b:
                sp.wait_ge(e["xs_done"], b)
                sp.dma_start(xa[:, :], io["x"][bass.ts(b, P), :]).then_inc(loaded["xa"], 16)
                sp.wait_ge(e["k_parts"], b)
                sp.dma_start(trig[:, :, :], io["trig"][bass.ts(b, P), :, :]).then_inc(loaded["trig"], 16)
            wq, w_out, keys, _ = router_weights(weights)
            wq_rows = io["peer_wq"].rearrange("(k p) n -> p k n", p=P)
            out_rows = io["w_out"].rearrange("(k p) n -> p k n", p=P)

            def replace(name, to, rows, n):
                sp.wait_ge(e[name + "_ready"], NB)
                sp.dma_start(to[:, :, n * W:(n + 1) * W], rows[:, :, n * W:(n + 1) * W]).then_inc(loaded["next"], 16)

            replace("mx", w_out, out_rows, 0)
            replace("rq", wq, wq_rows, 0)
            replace("rk", wq, wq_rows, 1)
            replace("rv", wq, wq_rows, 2)
            replace("mv", w_out, out_rows, 1)
            replace("rg", wq, wq_rows, 3)
            sp.wait_ge(e["mo_ready"], NB)
            with nc.allow_non_contiguous_dma(reason="rows of 128 values"):
                for k in range(4):
                    sp.dma_start(keys[:, k, :].rearrange("n (h d) -> n h d", d=P),
                                 io["peer_keys"][2 * k:2 * k + 2].rearrange("h t n d -> n (h t) d")).then_inc(
                        loaded["next"], 16)
            sp.wait_ge(loaded["next"], 16 * (6 + 4))

        @block.gpsimd
        def _(pool):
            nc.gpsimd.memset(mxb[:, :, :], 0.0).then_inc(zeroed, 1)
            nc.gpsimd.memset(S[:, :, :], 0.0).then_inc(zeroed, 1)
            nc.gpsimd.memset(C[:, :, :], 0.0).then_inc(zeroed, 1)
            nc.gpsimd.memset(nm[:, :], 0.0).then_inc(zeroed, 1)
            nc.gpsimd.memset(m_seq[:, :], 0.0).then_inc(zeroed, 1)

            def rotate(b):
                for name, r in (("q", qr), ("k", kr)):
                    pool.wait_ge(e[name + "_parts"], b + 1)
                    nc.gpsimd.tensor_tensor(r[:, :, 0:64], rot[:, 0, :, :], rot[:, 1, :, :], ALU.subtract)
                    nc.gpsimd.tensor_tensor(r[:, :, 64:128], rot[:, 2, :, :], rot[:, 3, :, :], ALU.add).then_inc(
                        e[name + "r_done"], 1)

            def store(b):
                pool.wait_ge(e["ym_done"], b + 1)
                pool.dma_start(y_dram[bass.ds(b, 1), :, :].rearrange("a p n -> p (a n)"),
                               yT[:, :, :].rearrange("p h t -> p (h t)")).then_inc(y_stored, 16)

            rotate(0)
            with pool.Fori(1, NB) as b:
                rotate(b)
                store(b - 1)
            store(NB - 1)
            pool.wait_ge(y_stored, 16 * NB)

        @block.scalar
        def _(act):
            A = nc.scalar

            def norm(b):
                step = Chain(act, e["act_step"])
                act.wait_ge(loaded["xa"], 16 * b + 16)
                if not (isinstance(b, int) and b == 0):
                    act.wait_ge(e["xT_ready"], b)
                A.activation(xs[:, :], xa[:, :], ACT.Square, accum_out=ss[:, 0:1]).then_inc(e["ss_done"], 1)
                act.wait_ge(e["eps_done"], b + 1)
                step(A.activation(ss[:, 2:3], ss[:, 1:2], ACT.Ln))
                step(A.activation(ss[:, 3:4], ss[:, 2:3], ACT.Exp, scale=-0.5))
                A.activation(xs[:, :], xa[:, :], ACT.Copy, scale=ss[:, 3:4]).then_inc(e["xs_done"], 1)

            def copy(out, src, after, n, signal, **kw):
                act.wait_ge(e[after], n)
                A.activation(out, src, ACT.Copy, **kw).then_inc(e[signal], 1)

            def body(b, front=True, tail=True, more=True):
                if tail:
                    copy(G[:, 0:H, :], hv(RT), "o_ready", b, "o_copied")
                    copy(mqT[:, :, :], hv(TR0), "mq_ready", b, "mqT_copied")
                    copy(mk[:, :, :], hv(TR1), "mk_ready", b, "mk_copied", scale=float(P) ** -0.5)
                if front:
                    copy(mxb[:, :, CONV_W - 1:], hv(P0), "mx_ready", b + 1, "mx_copied")
                    act.wait_ge(e["conv_done"], b + 1)
                    A.activation(sig[:, :, :], cT[:, :, :], ACT.Exp, scale=-1.0).then_inc(e["conv_exp"], 1)
                    step = Chain(act, e["act_step"])
                    act.wait_ge(e["gate_abs"], b + 1)
                    step(A.activation(gates[:, 2, :], gates[:, 1, :], ACT.Exp, scale=-1.0))
                    A.activation(gates[:, 3, :], gates[:, 2, :], ACT.Ln, bias=1.0).then_inc(e["gate_log"], 1)
                    copy(v[:, :, :], hv(P1), "rv_ready", b + 1, "v_copied")
                    act.wait_ge(e["gate_diff"], b + 1)
                    A.activation(gates[:, 2, :], gates[:, 6, :], ACT.Exp)
                    A.activation(cat[:, 0:2], small[:, 8:10], ACT.Exp)
                    A.activation(cat[:, 2:4], small[:, 4:6], ACT.Exp, scale=-1.0).then_inc(e["gate_exp"], 1)
                if tail:
                    act.wait_ge(e["mean_done"], b)
                    A.activation(sq[:, :, :], G[:, :, :], ACT.Square).then_inc(e["sq_done"], 1)
                    act.wait_ge(e["var_done"], b)
                    A.activation(stats[:, 1, :], stats[:, 2, :], ACT.Ln).then_inc(e["ln_done"], 1)
                    act.wait_ge(e["ln_done"], b)
                    A.activation(stats[:, 0, :], stats[:, 1, :], ACT.Exp, scale=-0.5).then_inc(e["rstd_done"], 1)
                if front:
                    copy(v1[:, :, :], hv(P0), "mv_ready", b + 1, "v1_copied")
                    if more:
                        norm(b + 1)
                    act.wait_ge(e["rg_ready"], b + 1)
                    if tail:
                        act.wait_ge(e["ym_done"], b)
                    A.activation(srg[:, :, :], hv(P1), ACT.Exp, scale=-1.0).then_inc(e["rg_exp"], 1)
                    act.wait_ge(e["mo_ready"], b + 1)
                    A.activation(smo[:, :, :], hv(P0), ACT.Exp, scale=-1.0).then_inc(e["mo_exp"], 1)
                    copy(qT[:, :, :], hv(TR0), "qT_ready", b + 1, "qT_copied")
                    copy(kT[:, :, :], hv(TR1), "kT_ready", b + 1, "kT_copied")

            norm(0)
            body(0, tail=False)
            with act.Fori(1, NB - 1) as b:
                body(b)
            body(NB - 1, more=False)
            body(NB, front=False)

        @block.vector
        def _(dve):
            V = nc.vector

            def eps(b):
                dve.wait_ge(e["ss_done"], b + 1)
                V.tensor_scalar(ss[:, 1:2], ss[:, 0:1], 1.0 / D, EPS, ALU.mult, ALU.add).then_inc(e["eps_done"], 1)

            def memory(step, b, c):
                dve.wait_ge(e[f"c{c}_ready"], b)
                if c == 1:
                    dve.wait_ge(e["num0_ready"], b)
                for h in range(H):
                    V.scalar_tensor_tensor(C[:, h, :], C[:, h, :], bc[:, h, c:c + 1], hv(UP)[:, h, :],
                                           ALU.mult, ALU.add)
                step(V.tensor_tensor(nm[:, :], nm[:, :], bc[:, :, c], ALU.mult))
                V.tensor_tensor(nm[:, :], nm[:, :], sm_n, ALU.add).then_inc(e[f"c{c}_done"], 1)

            def body(b, front=True, tail=True, more=True):
                step = Chain(dve, e["dve_step"])
                if front:
                    dve.wait_ge(e["xT_ready"], b + 1)
                    for k2, bk in enumerate((TR0, TR1)):
                        gain = g1[:, 4 * k2:4 * k2 + 4].unsqueeze(2).broadcast_to([P, 4, P])
                        last = V.tensor_tensor(hT[:, 4 * k2:4 * k2 + 4, :], hv(bk), gain, ALU.mult)
                    last.then_inc(e["hT_done"], 1)
                    dve.wait_ge(e["gates_ready"], b + 1)
                    V.tensor_copy(gsb[:, :], sm_gate).then_inc(e["gsb_done"], 1)
                if tail:
                    dve.wait_ge(e["s_ready"], b)
                    for h in range(H):
                        last = V.scalar_tensor_tensor(S[:, h, :], S[:, h, :], gamma_p[h], hv(UP)[:, h, :],
                                                      ALU.mult, ALU.add)
                    last.then_inc(e["s_done"], 1)
                    memory(step, b, 0)
                if front:
                    dve.wait_ge(e["mx_copied"], b + 1)
                    for h in range(H):
                        last = V.tensor_scalar(cT[:, h, :], mxb[:, h, 0:P], conv_w[:, 0, h:h + 1], conv_b[:, h:h + 1],
                                               ALU.mult, ALU.add)
                    step(last)
                    for j in range(1, CONV_W):
                        for h in range(H):
                            last = V.scalar_tensor_tensor(cT[:, h, :], mxb[:, h, j:j + P], conv_w[:, j, h:h + 1],
                                                          cT[:, h, :], ALU.mult, ALU.add)
                        if j < CONV_W - 1:
                            step(last)
                    last.then_inc(e["conv_done"], 1)
                    dve.wait_ge(e["conv_done"], b + 1)
                    V.tensor_copy(mxb[:, :, 0:CONV_W - 1], mxb[:, :, P:])
                    dve.wait_ge(e["conv_exp"], b + 1)
                    step(V.tensor_scalar(sig[:, :, :], sig[:, :, :], 1.0, None, ALU.add))
                    step(V.reciprocal(sig[:, :, :], sig[:, :, :]))
                    V.tensor_tensor(cT[:, :, :], cT[:, :, :], sig[:, :, :], ALU.mult).then_inc(e["cT_done"], 1)
                    dve.wait_ge(loaded["trig"], 16 * b + 16)
                    rotary(b, "q", P1, 0)
                if tail:
                    memory(step, b, 1)
                if front:
                    rotary(b, "k", P0, 2)
                    gate_chain(step, b)
                if tail:
                    head_norm(step, b)
                if front:
                    dve.wait_ge(e["w_ready"], b + 1)
                    for c in range(2):
                        V.tensor_scalar(wtok[:, c, :], sm_w, half[:, c:c + 1], None, ALU.mult)
                    V.tensor_copy(bc[:, :, :], sm_bc.rearrange("p (h c) -> p h c", h=H)).then_inc(e["w_copied"], 1)
                if tail:
                    dve.wait_ge(e["yT_ready"], b)
                    if not (isinstance(b, int) and b == 1):
                        dve.wait_ge(y_stored, 16 * b - 16)
                    for h in range(H):
                        V.scalar_tensor_tensor(yT[:, h, :], hv(TR0)[:, h, :], ret_g[:, h:h + 1], srg[:, h, :],
                                               ALU.mult, ALU.mult)
                    for h in range(H):
                        last = V.scalar_tensor_tensor(skc[:, h, :], hv(TR1)[:, h, :], ml_g[:, h:h + 1], skc[:, h, :],
                                                      ALU.mult, ALU.add)
                    step(last)
                    V.tensor_tensor(yT[:, H:2 * H, :], skc[:, :, :], smo[:, :, :], ALU.mult).then_inc(e["ym_done"], 1)
                if front:
                    if more:
                        eps(b + 1)
                    dve.wait_ge(e["rg_exp"], b + 1)
                    step(V.tensor_scalar(srg[:, :, :], srg[:, :, :], 1.0, None, ALU.add))
                    step(V.reciprocal(srg[:, :, :], srg[:, :, :]))
                    V.tensor_tensor(srg[:, :, :], hv(P1), srg[:, :, :], ALU.mult).then_inc(e["srg_done"], 1)
                    for h in range(H):
                        V.tensor_scalar(skc[:, h, :], cT[:, h, :], skip[:, h:h + 1], None, ALU.mult)
                    dve.wait_ge(e["w_copied"], b + 1)
                    dve.wait_ge(e["v1_copied"], b + 1)
                    for c in range(2):
                        last = V.tensor_tensor(wv[:, c, :, :], v1[:, :, :],
                                               wtok[:, c, :].unsqueeze(2).broadcast_to([P, H, P]), ALU.mult)
                    last.then_inc(e["wv_done"], 1)
                    dve.wait_ge(e["mo_exp"], b + 1)
                    step(V.tensor_scalar(smo[:, :, :], smo[:, :, :], 1.0, None, ALU.add))
                    V.reciprocal(smo[:, :, :], smo[:, :, :]).then_inc(e["smo_done"], 1)
                    dve.wait_ge(loaded["late"], 16 * LATE)
                    dve.wait_ge(e["scores_ready"], b + 1)
                    V.tensor_tensor(scd[:, :, :], hv(RT), decay_t[:, :, :], ALU.mult).then_inc(e["scd_done"], 1)

            def rotary(b, name, bk, t0):
                dve.wait_ge(e[f"r{name}_ready"], b + 1)
                if name == "k":
                    dve.wait_ge(e["qr_done"], b + 1)
                elif not (isinstance(b, int) and b == 0):
                    dve.wait_ge(e["kr_done"], b)
                cos = trig[:, t0, :].rearrange("p (h d) -> p h d", h=H)
                sin = trig[:, t0 + 1, :].rearrange("p (h d) -> p h d", h=H)
                lo, hi = hv(bk)[:, :, 0:64], hv(bk)[:, :, 64:128]
                V.tensor_tensor(rot[:, 0, :, :], lo, cos, ALU.mult)
                V.tensor_tensor(rot[:, 1, :, :], hi, sin, ALU.mult)
                V.tensor_tensor(rot[:, 2, :, :], lo, sin, ALU.mult)
                V.tensor_tensor(rot[:, 3, :, :], hi, cos, ALU.mult).then_inc(e[name + "_parts"], 1)

            def gate_chain(step, b):
                dve.wait_ge(e["gateT_ready"], b + 1)
                step(V.tensor_scalar(gates[:, 0, :], sm_f, b_f[:, 0:1], None, ALU.add))
                V.tensor_scalar(gates[:, 4, :], sm_i, b_i[:, 0:1], None, ALU.add).then_inc(e["gate_read"], 1)
                V.scalar_tensor_tensor(gates[:, 1, :], gates[:, 0, :], -1.0, gates[:, 0, :], ALU.mult,
                                       ALU.max).then_inc(e["gate_abs"], 1)
                dve.wait_ge(e["gate_read"], b + 1)
                dve.wait_ge(e["gate_log"], b + 1)
                step(V.scalar_tensor_tensor(gates[:, 5, :], gates[:, 0, :], 0.0, gates[:, 3, :], ALU.min, ALU.subtract))
                dve.wait_ge(loaded["tables"], 16 * TABLES)
                step(V.tensor_tensor_scan(gates[:, 1, :], reset[:, :], gates[:, 5, :], 0.0, ALU.mult, ALU.add))
                V.tensor_copy(small[:, 0:2], gates[:, 1, 63:128:64])
                step(V.tensor_tensor(gates[:, 4, :], gates[:, 4, :], gates[:, 1, :], ALU.subtract))
                g2v = lambda i: gates[:, i, :].rearrange("h (c l) -> h c l", l=64)
                wide = lambda t: t.unsqueeze(2).broadcast_to([H, 2, 64])
                step(V.tensor_tensor(g2v(5), g2v(4), wide(small[:, 0:2]), ALU.add))
                step(V.tensor_reduce(small[:, 2:4], g2v(5), AX, ALU.max))
                step(V.tensor_tensor_scan(m_seq[:, 1:3], small[:, 0:2], small[:, 2:4], m_seq[:, 0:1], ALU.add, ALU.max))
                V.tensor_tensor(small[:, 6:8], small[:, 0:2], m_seq[:, 0:2], ALU.add)
                step(V.tensor_copy(small[:, 4:6], m_seq[:, 1:3]))
                V.tensor_tensor(small[:, 8:10], small[:, 6:8], m_seq[:, 1:3], ALU.subtract)
                step(V.tensor_tensor(g2v(6), g2v(5), wide(small[:, 4:6]), ALU.subtract))
                V.tensor_copy(m_seq[:, 0:1], small[:, 5:6]).then_inc(e["gate_diff"], 1)

            def head_norm(step, b):
                dve.wait_ge(e["num1_ready"], b)
                V.tensor_copy(den[0:64, 2, :], bc[0:64, :, 2])
                V.tensor_copy(den[64:128, 2, :], bc[64:128, :, 3])
                V.tensor_copy(den[:, 0, :], sm_den).then_inc(e["den_read"], 1)
                dve.wait_ge(e["den_read"], b)
                step(V.scalar_tensor_tensor(den[:, 1, :], den[:, 0, :], -1.0, den[:, 0, :], ALU.mult, ALU.max))
                step(V.tensor_tensor(den[:, 1, :], den[:, 1, :], den[:, 2, :], ALU.max))
                step(V.reciprocal(den[:, 3, :], den[:, 1, :]))
                V.tensor_tensor(G[:, H:2 * H, :], hv(NM), den[:, 3, :].unsqueeze(2).broadcast_to([P, H, P]),
                                ALU.mult).then_inc(e["hm_done"], 1)
                dve.wait_ge(e["hm_done"], b)
                dve.wait_ge(e["o_copied"], b)
                heads = lambda t: t.unsqueeze(2).broadcast_to([P, 2 * H, P])
                step(V.tensor_reduce(stats[:, 0, :], G[:, :, :], AX, ALU.add))
                step(V.tensor_scalar(stats[:, 1, :], stats[:, 0, :], 1.0 / P, None, ALU.mult))
                V.tensor_tensor(G[:, :, :], G[:, :, :], heads(stats[:, 1, :]), ALU.subtract).then_inc(
                    e["mean_done"], 1)
                dve.wait_ge(e["sq_done"], b)
                step(V.tensor_reduce(stats[:, 0, :], sq[:, :, :], AX, ALU.add))
                V.tensor_scalar(stats[:, 2, :], stats[:, 0, :], 1.0 / P, EPS, ALU.mult, ALU.add).then_inc(
                    e["var_done"], 1)
                dve.wait_ge(e["rstd_done"], b)
                V.tensor_tensor(G[:, :, :], G[:, :, :], heads(stats[:, 0, :]), ALU.mult).then_inc(e["g_done"], 1)

            dve.wait_ge(zeroed, 5)
            eps(0)
            dve.wait_ge(loaded["small"], 16 * SMALL)
            body(0, tail=False)
            with dve.Fori(1, NB - 1) as b:
                body(b)
            body(NB - 1, more=False)
            body(NB, front=False)

        @block.tensor
        def _(pe):
            mm, tp = nc.tensor.matmul, nc.tensor.transpose

            def by_token(b, bk, name, col, free):
                pe.wait_ge(loaded[name], 16)
                if free:
                    pe.wait_ge(e[free], b + 1)
                for k in range(KC):
                    last = mm(bk[:, :], hT[:, k, :], w_in[:, k, col:col + W], start=(k == 0), stop=(k == KC - 1))
                last.then_inc(e[name + "_ready"], 1)

            def by_channel(b, bk, name, col, free):
                pe.wait_ge(loaded[name], 16)
                if free:
                    pe.wait_ge(e[free], b + 1)
                for h in range(H):
                    for k in range(KC):
                        last = mm(hv(bk)[:, h, :], w_in[:, k, col + h * P:col + (h + 1) * P], hT[:, k, :],
                                  start=(k == 0), stop=(k == KC - 1))
                last.then_inc(e[name + "_ready"], 1)

            def memory(b, c):
                if c == 0:
                    pe.wait_ge(e["wv_done"], b)
                    pe.wait_ge(e["mk_copied"], b)
                    pe.wait_ge(e["s_done"], b)
                for h in range(H):
                    mm(hv(UP)[:, h, :], mk[:, h, :], wv[:, c, h, :], start=True, stop=True)
                for h in range(H):
                    last = mm(sm_n[:, h:h + 1], mk[:, h, :], wtok[:, c, h:h + 1], start=True, stop=True)
                last.then_inc(e[f"c{c}_ready"], 1)

            def readout(b, c):
                pe.wait_ge(e[f"c{c}_done"], b)
                rows = slice(64 * c, 64 * c + 64)
                for h in range(H):
                    mm(hv(NM)[rows, h, :], mqT[:, h, rows], C[:, h, :], start=True, stop=True)
                for h in range(H):
                    last = mm(sm_den[rows, h:h + 1], mqT[:, h, rows], nm[:, h:h + 1], start=True, stop=True)
                last.then_inc(e[f"num{c}_ready"], 1)

            def body(b, front=True, tail=True):
                first = isinstance(b, int) and b == 0
                if front:
                    pe.wait_ge(e["xs_done"], b + 1)
                    if tail:
                        pe.wait_ge(e["kT_copied"], b)
                    for k in range(KC):
                        last = tp(hv(TR0 if k < 4 else TR1)[:, k % 4, :], xs[:, k * P:(k + 1) * P], ident[:, :])
                    last.then_inc(e["xT_ready"], 1)
                    pe.wait_ge(e["hT_done"], b + 1)
                    pe.wait_ge(loaded["g"], 16)
                    for k in range(KC):
                        last = mm(sm_gate, hT[:, k, :], w_in[:, k, MI:MI + 2 * H], start=(k == 0), stop=(k == KC - 1))
                    last.then_inc(e["gates_ready"], 1)
                if tail:
                    pe.wait_ge(e["scd_done"], b)
                    for h in range(H):
                        mm(hv(RT)[:, h, :], scd[:, h, :], v[:, h, :], start=True, stop=False)
                        last = mm(hv(RT)[:, h, :], qT[:, h, :], S[:, h, :], start=False, stop=True)
                    last.then_inc(e["o_ready"], 1)
                    for h in range(H):
                        last = mm(hv(UP)[:, h, :], kr[:, h, :], v[:, h, :], start=True, stop=True)
                    last.then_inc(e["s_ready"], 1)
                    pe.wait_ge(loaded["late"], 16 * LATE)
                    for h in range(H):
                        last = mm(hv(TR0)[:, h, :], mwq[:, h, :], cT[:, h, :], start=True, stop=True)
                    last.then_inc(e["mq_ready"], 1)
                    for h in range(H):
                        last = mm(hv(TR1)[:, h, :], cT[:, h, :], mwk[:, h, :], start=True, stop=True)
                    last.then_inc(e["mk_ready"], 1)
                if front:
                    if tail:
                        pe.wait_ge(e["smo_done"], b)
                    by_channel(b, P0, "mx", MX, None)
                    pe.wait_ge(e["gsb_done"], b + 1)
                if tail:
                    memory(b, 0)
                if front:
                    if tail:
                        pe.wait_ge(e["srg_done"], b)
                    by_token(b, P1, "rq", RQ, None)
                if tail:
                    pe.wait_ge(e["mqT_copied"], b)
                    readout(b, 0)
                    memory(b, 1)
                if front:
                    by_token(b, P0, "rk", RK, "mx_copied")
                    if tail:
                        pe.wait_ge(e["c1_done"], b)
                    tp(sm_i, gsb[:, 0:H], ident[:, :])
                    tp(sm_f, gsb[:, H:2 * H], ident[:, :]).then_inc(e["gateT_ready"], 1)
                    by_token(b, P1, "rv", RV, "q_parts")
                    pe.wait_ge(e["gate_read"], b + 1)
                if tail:
                    readout(b, 1)
                if front:
                    by_token(b, P0, "mv", MV, "k_parts")
                    pe.wait_ge(loaded["tables"], 16 * TABLES)
                    if tail:
                        pe.wait_ge(e["den_read"], b)
                    pe.wait_ge(e["gate_exp"], b + 1)
                    tp(sm_w, gates[:, 2, :], ident[0:H, 0:H])
                    for h in range(H):
                        last = mm(sm_bc[:, 4 * h:4 * h + 4], select[:, h, :], cat[:, :], start=True, stop=True)
                    last.then_inc(e["w_ready"], 1)
                    by_channel(b, P1, "rg", RG, "v_copied")
                if tail:
                    pe.wait_ge(e["g_done"], b)
                    for h in range(2 * H):
                        last = tp(hv(TR0 if h < H else TR1)[:, h % H, :], G[:, h, :], ident[:, :])
                    last.then_inc(e["yT_ready"], 1)
                if front:
                    by_channel(b, P0, "mo", MO, "v1_copied")
                    if tail:
                        pe.wait_ge(e["ym_done"], b)
                    pe.wait_ge(e["qr_done"], b + 1)
                    for h in range(H):
                        last = tp(hv(TR0)[:, h, :], qr[:, h, :], ident[:, :])
                    last.then_inc(e["qT_ready"], 1)
                    pe.wait_ge(e["kr_done"], b + 1)
                    for h in range(H):
                        last = tp(hv(TR1)[:, h, :], kr[:, h, :], ident[:, :])
                    last.then_inc(e["kT_ready"], 1)
                    pe.wait_ge(e["qT_copied"], b + 1)
                    pe.wait_ge(e["kT_copied"], b + 1)
                    if tail:
                        pe.wait_ge(e["o_copied"], b)
                    for h in range(H):
                        last = mm(hv(RT)[:, h, :], kT[:, h, :], qT[:, h, :], start=True, stop=True)
                    last.then_inc(e["scores_ready"], 1)

            pe.wait_ge(loaded["ident"], 16)
            body(0, tail=False)
            with pe.Fori(1, NB) as b:
                body(b)
            body(NB, front=False)


class Count:

    def __init__(self, sem, credit=0):
        self.sem, self.credit = sem, credit

    def give(self, engine):
        engine.sem_inc(self.sem, self.credit)

    def wait(self, engine, n):
        engine.wait_ge(self.sem, n + self.credit)


def router_stage(nc, io, weights, ident, y_dram, x1_dram, xn_dram, blocks, xt_hi, xt_lo, expert, gate, pair_t):
    T, D = io["x"].shape
    KC = D // P
    NB = T // P
    J = 2 * PEER_HEADS
    N = PEER_HEADS * TOPK
    gathered = blocks
    held = []
    with ExitStack() as ctx:
        ctx.callback(clear_semaphores, nc, held)

        def sb(name, shape, dt=F32):
            return ctx.enter_context(nc.sbuf_tensor(name, shape, dt))

        def sem(name):
            held.append(nc.alloc_semaphore(name))
            return held[-1]

        wq, w_out, keys, keysT = router_weights(weights)
        by_key = lambda t, j: t[:, j // 4, (j % 4) * P:(j % 4 + 1) * P]
        iota = sb("iota", [P, TOPK])
        g2 = sb("g2", [P, D])
        xin = sb("xin", [P, D])
        yT = sb("yT2", [P, KC, P])
        xh = sb("xh", [P, D])
        x2T = sb("x2T", [P, KC, P])
        qT = sb("pqT", [P, J, P])
        sub = keys
        top = sb("top", [P, J, TOPK])
        top_i = sb("top_i", [P, J, TOPK], U32)
        top_f = sb("top_f", [P, J, TOPK])
        best = sb("best", [P, PEER_HEADS, TOPK])
        soft = sb("soft", [P, 2, PEER_HEADS, TOPK])
        flat = sb("flat", [P, PEER_HEADS, TOPK], U32)
        digit_f = sb("digit_f", [P, 2, N])
        hit = sb("hit", [P, N, TOPK])
        picked = sb("picked", [P, 3, N])
        sums = sb("sums", [P, 2, PEER_HEADS])
        ss = sb("ss2", [P, 4])
        xsq = hit[:, 0:64, :].rearrange("p a c -> p (a c)")
        spare = hit[:, 64:128, :].rearrange("p a c -> p (a c)")
        cand = hit[:, 96:128, :].rearrange("p (h a) c -> p h (a c)", h=PEER_HEADS)
        place, start = [spare[:, i * N:(i + 1) * N] for i in range(2)]
        digit = top_i[:, :, :].rearrange("p (i j) k -> p i (j k)", i=2)
        row_f = digit_f[:, 0, :]
        banks = [ctx.enter_context(nc.psum_tensor(f"pb{i}", [P, 512], F32)) for i in range(8)]
        hv = lambda t: t[:, :].rearrange("p (h d) -> p h d", d=P)

        ld = {n: sem("r_ld_" + n) for n in ("const", "x", "y", "xn", "x1")}
        names = ("out_ready x1_done keysT_ready keysT_done ss_done eps_done ln_done rstd_done xh_done xT_ready "
                 "xT_copied xT_hi sub_copied best_done exp_done dve_step topk_done pair_ready pair_copied").split()
        e = {n: sem("r_" + n) for n in names}
        q_ready = [sem(f"r_q_ready{i}") for i in range(4)]
        q_copied = [sem(f"r_q_copied{i}") for i in range(4)]
        s_ready = [sem(f"r_s_ready{i}") for i in range(4)]
        block = ctx.enter_context(nc.Block())

        @block.sync
        def _(sp):
            sp.dma_start(yT[:, :, :], y_dram[0, :, :].rearrange("p (h t) -> p h t", t=P)).then_inc(ld["y"], 16)
            sp.dma_start(xin[:, :], io["x"][0:P, :]).then_inc(ld["x"], 16)
            sp.dma_start(g2[:, :], io["norm2_g"].partition_broadcast(P)).then_inc(ld["const"], 16)
            sp.dma_start(iota[:, :], io["iota"][:, 0:TOPK]).then_inc(ld["const"], 16)
            with sp.Fori(1, NB) as b:
                sp.wait_ge(e["x1_done"], b)
                sp.dma_start(yT[:, :, :],
                             y_dram[bass.ds(b, 1), :, :].rearrange("a p (h t) -> p (a h) t", t=P)).then_inc(ld["y"], 16)
                sp.dma_start(x1_dram[bass.ts(b - 1, P), :], xin[:, :]).then_inc(ld["x1"], 16)
                sp.wait_ge(ld["x1"], 16 * b)
                sp.wait_ge(e["xh_done"], b)
                sp.dma_start(xin[:, :], io["x"][bass.ts(b, P), :]).then_inc(ld["x"], 16)
            sp.wait_ge(e["x1_done"], NB)
            sp.dma_start(x1_dram[T - P:, :], xin[:, :]).then_inc(ld["x1"], 16)
            sp.wait_ge(ld["x1"], 16 * NB)

        @block.gpsimd
        def _(pool):
            with pool.Fori(0, NB) as b:
                pool.wait_ge(e["xh_done"], b + 1)
                pool.dma_start(xn_dram[bass.ts(b, P), :], xh[:, :]).then_inc(ld["xn"], 16)
            pool.wait_ge(ld["xn"], 16 * NB)

        @block.scalar
        def _(act):
            def norm(b):
                act.wait_ge(e["x1_done"], b + 1)
                nc.scalar.activation(xsq, xin[:, :], ACT.Square, accum_out=ss[:, 0:1]).then_inc(e["ss_done"], 1)
                act.wait_ge(e["eps_done"], b + 1)
                nc.scalar.activation(ss[:, 2:3], ss[:, 1:2], ACT.Ln).then_inc(e["ln_done"], 1)
                act.wait_ge(e["ln_done"], b + 1)
                nc.scalar.activation(ss[:, 3:4], ss[:, 2:3], ACT.Exp, scale=-0.5).then_inc(e["rstd_done"], 1)

            def front(b, dense, more=True):
                act.wait_ge(e["xT_ready"], b + 1)
                nc.scalar.copy(x2T[:, 0:4, :], hv(banks[0]))
                nc.scalar.copy(x2T[:, 4:8, :], hv(banks[1])).then_inc(e["xT_copied"], 1)
                if dense:
                    act.wait_ge(e["xT_copied"], b + 1)
                    nc.scalar.copy(xt_hi[:, :, bass.ds((b - gathered) * P, P)], x2T[:, :, :]).then_inc(e["xT_hi"], 1)
                if more:
                    norm(b + 1)
                for i in range(4):
                    act.wait_ge(q_ready[i], b + 1)
                    nc.scalar.copy(qT[:, 4 * i:4 * i + 4, :], hv(banks[2 + i])).then_inc(q_copied[i], 1)

            def scores(b):
                for i in range(4):
                    act.wait_ge(s_ready[i], b + 1)
                    nc.scalar.copy(sub[:, i, :], banks[2 + i][:, :]).then_inc(e["sub_copied"], 1)

            def body(b, next_dense, more=True, last=False):
                if not last:
                    front(b + 1, next_dense, more)
                act.wait_ge(e["best_done"], b + 1)
                nc.scalar.activation(soft[:, 1, :, :], soft[:, 0, :, :], ACT.Exp).then_inc(e["exp_done"], 1)
                if not last:
                    scores(b + 1)

            for i in range(4):
                act.wait_ge(e["keysT_ready"], i + 1)
                nc.scalar.copy(keysT[:, i, :], banks[2 + i][:, :]).then_inc(e["keysT_done"], 1)
            norm(0)
            front(0, False)
            scores(0)
            with act.Fori(0, gathered - 1) as b:
                body(b, False)
            with act.Fori(gathered - 1, NB - 2) as b:
                body(b, True)
            body(NB - 2, True, more=False)
            body(NB - 1, True, last=True)

        @block.tensor
        def _(pe):
            mm, tp = nc.tensor.matmul, nc.tensor.transpose

            def project(b):
                pe.wait_ge(ld["y"], 16 * b + 16)
                for n in range(2):
                    for k in range(KC):
                        last = mm(banks[n][:, :], yT[:, k, :], w_out[:, k, n * 512:(n + 1) * 512],
                                  start=(k == 0), stop=(k == KC - 1))
                last.then_inc(e["out_ready"], 1)

            def front(b, more=True):
                pe.wait_ge(e["xh_done"], b + 1)
                for k in range(KC):
                    last = tp(hv(banks[k // 4])[:, k % 4, :], xh[:, k * P:(k + 1) * P], ident[:, :])
                last.then_inc(e["xT_ready"], 1)
                pe.wait_ge(e["xT_copied"], b + 1)
                if more:
                    project(b + 1)
                for j in range(J):
                    for k in range(KC):
                        last = mm(hv(banks[2 + j // 4])[:, j % 4, :], wq[:, k, j * P:(j + 1) * P], x2T[:, k, :],
                                  start=(k == 0), stop=(k == KC - 1))
                    if j % 4 == 3:
                        last.then_inc(q_ready[j // 4], 1)
                for j in range(J):
                    if j % 4 == 0:
                        pe.wait_ge(q_copied[j // 4], b + 1)
                    last = mm(hv(banks[2 + j // 4])[:, j % 4, :], qT[:, j, :], by_key(keysT, j), start=True, stop=True)
                    if j % 4 == 3:
                        last.then_inc(s_ready[j // 4], 1)

            def pairs(b):
                pe.wait_ge(ld["const"], 32)
                pe.wait_ge(e["topk_done"], b + 1)
                for i in range(3):
                    last = tp(hv(banks[6])[:, i, :], picked[:, i, :], ident[:, :])
                last.then_inc(e["pair_ready"], 1)

            for j in range(J):
                last = tp(hv(banks[2 + j // 4])[:, j % 4, :], by_key(keys, j), ident[:, :])
                if j % 4 == 3:
                    last.then_inc(e["keysT_ready"], 1)
            project(0)
            pe.wait_ge(e["keysT_done"], 4)
            front(0)
            with pe.Fori(0, gathered) as b:
                pe.wait_ge(e["sub_copied"], 4 * b + 4)
                front(b + 1)
            with pe.Fori(gathered, NB - 2) as b:
                pe.wait_ge(e["sub_copied"], 4 * b + 4)
                front(b + 1)
                pairs(b)
            pe.wait_ge(e["sub_copied"], 4 * (NB - 2) + 4)
            front(NB - 1, more=False)
            pairs(NB - 2)
            pairs(NB - 1)

        @block.vector
        def _(dve):
            V = nc.vector

            def residual(b):
                dve.wait_ge(e["out_ready"], b + 1)
                dve.wait_ge(ld["x"], 16 * b + 16)
                V.tensor_tensor(xin[:, 0:512], banks[0][:, :], xin[:, 0:512], ALU.add)
                V.tensor_tensor(xin[:, 512:1024], banks[1][:, :], xin[:, 512:1024], ALU.add).then_inc(e["x1_done"], 1)

            def norm(b):
                dve.wait_ge(e["ss_done"], b + 1)
                V.tensor_scalar(ss[:, 1:2], ss[:, 0:1], 1.0 / D, EPS, ALU.mult, ALU.add).then_inc(e["eps_done"], 1)
                dve.wait_ge(e["rstd_done"], b + 1)
                if not (isinstance(b, int) and b == 0):
                    dve.wait_ge(ld["xn"], 16 * b)
                    dve.wait_ge(e["xT_ready"], b)
                V.scalar_tensor_tensor(xh[:, :], xin[:, :], ss[:, 3:4], g2[:, :], ALU.mult, ALU.mult).then_inc(
                    e["xh_done"], 1)

            def top16(step, lists):
                for values, scratch, out, index in lists:
                    last = V.max(out[:, 0:8], values)
                step(last)
                for values, scratch, out, index in lists:
                    V.max_index(index[:, 0:8], out[:, 0:8], values)
                    last = V.match_replace(scratch, out[:, 0:8], values, NEG)
                step(last)
                for values, scratch, out, index in lists:
                    last = V.max(out[:, 8:16], scratch)
                step(last)
                for values, scratch, out, index in lists:
                    last = V.max_index(index[:, 8:16], out[:, 8:16], scratch)
                step(last)

            halves, keys_f = [t[:, :, :].rearrange("p (h s) k -> p h s k", s=2) for t in (top, top_f)]

            def body(b, dense, next_dense, more=True, last=False):
                step = Chain(dve, e["dve_step"])
                dve.wait_ge(e["sub_copied"], 4 * b + 4)
                V.tensor_copy(spare[:, 0:1], iota[:, 0:1])
                for j0 in range(0, J, 8):
                    top16(step, [(by_key(sub, j), spare[:, (j - j0) * P:(j - j0 + 1) * P], top[:, j, :], top_i[:, j, :])
                                 for j in range(j0, j0 + 8)])
                if next_dense and not last:
                    dve.wait_ge(e["xT_hi"], b + 1 - (gathered - 1))
                    cols = bass.ds((b + 1 - gathered) * P, P)
                    V.tensor_tensor(xt_lo[:, :, cols], x2T[:, :, :], xt_hi[:, :, cols].bitcast(F32), ALU.subtract)
                if more:
                    residual(b + 2)
                for at, i, rows, width in ((0, 0, 1, 16), (16, 1, 3, 8), (40, 4, 4, 4), (56, 8, 8, 1)):
                    shape = [P, PEER_HEADS, rows, width]
                    last_op = V.tensor_tensor(
                        cand[:, :, at:at + rows * width].rearrange("p h (a c) -> p h a c", a=rows),
                        halves[:, :, 0, i:i + rows].unsqueeze(3).broadcast_to(shape),
                        halves[:, :, 1, 0:width].unsqueeze(2).broadcast_to(shape), ALU.add)
                step(last_op)
                if more:
                    norm(b + 2)
                top16(step, [(cand[:, h, :], spare[:, h * PAIRS:(h + 1) * PAIRS], best[:, h, :], flat[:, h, :])
                             for h in range(PEER_HEADS)])
                step(V.tensor_tensor(soft[:, 0, :, :], best[:, :, :],
                                     best[:, :, 0:1].broadcast_to([P, PEER_HEADS, TOPK]), ALU.subtract))
                V.tensor_copy(top_f[:, :, :], top_i[:, :, :]).then_inc(e["best_done"], 1)
                dve.wait_ge(e["best_done"], b + 1)
                fl = flat[:, :, :].rearrange("p h k -> p (h k)")
                row, other = digit_f[:, 0, :], digit_f[:, 1, :]
                V.tensor_scalar(digit[:, 0, :], fl, 3, None, ALU.logical_shift_right)
                step(V.tensor_scalar(digit[:, 1, :], fl, 2, None, ALU.logical_shift_right))
                V.tensor_copy(digit_f[:, :, :], digit)
                step(V.tensor_copy(place, fl))
                step(V.tensor_scalar(row, row, -1.0, 0.0, ALU.add, ALU.max))
                step(V.scalar_tensor_tensor(other, other, -6.0, row, ALU.add, ALU.max))
                step(V.scalar_tensor_tensor(row, place, -48.0, other, ALU.add, ALU.max))
                V.tensor_scalar(start, row, 4.0, 24.0, ALU.mult, ALU.add)
                step(V.tensor_scalar(other, row, 8.0, 8.0, ALU.mult, ALU.add))
                step(V.scalar_tensor_tensor(other, row, 16.0, other, ALU.mult, ALU.min))
                step(V.scalar_tensor_tensor(other, row, 48.0, other, ALU.add, ALU.min))
                step(V.tensor_tensor(other, other, start, ALU.min))
                step(V.tensor_tensor(other, place, other, ALU.subtract))
                if dense:
                    dve.wait_ge(e["pair_copied"], b - gathered + 1)
                for s in range(2):
                    step(V.tensor_tensor(hit[:, :, :], digit_f[:, s, :].unsqueeze(2).broadcast_to([P, N, TOPK]),
                                         iota[:, :].unsqueeze(1).broadcast_to([P, N, TOPK]), ALU.is_equal))
                    by_head_hit = hit[:, :, :].rearrange("p (h k) a -> p h k a", h=PEER_HEADS)
                    step(V.tensor_tensor(by_head_hit, by_head_hit, keys_f[:, :, s, :].unsqueeze(2).broadcast_to(
                        [P, PEER_HEADS, TOPK, TOPK]), ALU.mult))
                    step(V.tensor_reduce(picked[:, s, :], hit[:, :, :], AX, ALU.add))
                dve.wait_ge(e["exp_done"], b + 1)
                step(V.tensor_reduce(sums[:, 0, :], soft[:, 1, :, :], AX, ALU.add))
                step(V.reciprocal(sums[:, 1, :], sums[:, 0, :]))
                share = sums[:, 1, :].unsqueeze(2).broadcast_to([P, PEER_HEADS, TOPK])
                by_head = lambda t: t.rearrange("p (h k) -> p h k", h=PEER_HEADS)
                if dense:
                    V.tensor_tensor(by_head(picked[:, 2, :]), soft[:, 1, :, :], share, ALU.mult).then_inc(
                        e["topk_done"], 1)
                    dve.wait_ge(e["pair_ready"], b - gathered + 1)
                    V.tensor_copy(pair_t[:, :, bass.ds((b - gathered) * P, P)], hv(banks[6])[:, 0:3, :]).then_inc(
                        e["pair_copied"], 1)
                else:
                    step(V.tensor_tensor(by_head(gate[:, bass.ds(b * N, N)]), soft[:, 1, :, :], share, ALU.mult))
                    step(V.scalar_tensor_tensor(row_f, picked[:, 0, :], float(P), picked[:, 1, :], ALU.mult,
                                                ALU.add))
                    V.tensor_copy(expert[:, bass.ds(b * N, N)], row_f).then_inc(e["topk_done"], 1)

            dve.wait_ge(ld["const"], 32)
            V.memset(expert[:, gathered * N:], 0).then_inc(e["pair_copied"], 1)
            for b in range(2):
                residual(b)
                norm(b)
            with dve.Fori(0, gathered - 1) as b:
                body(b, False, False)
            body(gathered - 1, False, True)
            with dve.Fori(gathered, NB - 2) as b:
                body(b, True, True)
            body(NB - 2, True, True, more=False)
            body(NB - 1, True, True, more=False, last=True)


def pair_stage(nc, io, g_dram, pair_t, blocks):
    GROUP, SLOTS = 4, 8
    PER = SLOTS
    held = []
    with ExitStack() as ctx:
        ctx.callback(clear_semaphores, nc, held)

        def sb(name, shape, dt=F32):
            return ctx.enter_context(nc.sbuf_tensor(name, shape, dt))

        def sem(name):
            held.append(nc.alloc_semaphore(name))
            return held[-1]

        first = [sb(f"first{i}", [P, P]) for i in range(SLOTS)]
        second = sb("second", [P, SLOTS, P])
        key = sb("key", [P, 2])
        iota = sb("iota2", [P, P])
        whole = [sb(f"whole{i}", [P, P, P]) for i in range(2)]
        banks = [ctx.enter_context(nc.psum_tensor(f"gb{i}", [P, 512], F32)) for i in range(2)]
        iota_in, stored = sem("g_iota_in"), [sem(f"g_stored{i}") for i in range(2)]
        hot = [sem(f"g_hot{i}") for i in range(2)]
        hot2 = [sem(f"g_hot2{i}") for i in range(2)]
        key_set = sem("g_key_set")
        used = [Count(sem(f"g_used{i}"), 1) for i in range(2)]
        copied = [Count(sem(f"g_copied{i}"), 1) for i in range(2)]
        block = ctx.enter_context(nc.Block())
        LOOPS = P // PER

        @block.sync
        def _(sp):
            sp.dma_start(iota[:, :], io["iota"]).then_inc(iota_in, 16)
            for b in range(blocks):
                for i in range(2):
                    copied[i].wait(sp, (b + 1) * LOOPS)
                sp.dma_start(g_dram[:, :, b * P:(b + 1) * P].rearrange("a c t -> c a t"),
                             whole[b % 2][:, :, :]).then_inc(stored[b % 2], 16)
            for i in range(2):
                sp.wait_ge(stored[i], 16 * ((blocks + 1 - i) // 2))

        @block.vector
        def _(dve):
            dve.wait_ge(iota_in, 16)
            with dve.Fori(0, blocks * LOOPS) as n:
                for i in range(2):
                    used[i].wait(dve, n)
                    for t in range(GROUP):
                        at = bass.ds(n * PER + (i * GROUP + t), 1)
                        slot = i * GROUP + t
                        nc.vector.tensor_scalar(first[slot][:, :], iota[:, :], pair_t[:, 0, at], pair_t[:, 2, at],
                                                ALU.is_equal, ALU.mult)
                    at = bass.ds(n * PER + i * GROUP, GROUP - 1)
                    nc.vector.tensor_tensor(
                        second[:, i * GROUP:i * GROUP + GROUP - 1, :],
                        iota[:, :].unsqueeze(1).broadcast_to([P, GROUP - 1, P]),
                        pair_t[:, 1, at].unsqueeze(2).broadcast_to([P, GROUP - 1, P]), ALU.is_equal).then_inc(hot[i], 1)

        @block.gpsimd
        def _(pool):
            pool.wait_ge(iota_in, 16)
            with pool.Fori(0, blocks * LOOPS) as n:
                step = Chain(pool, key_set)
                for i in range(2):
                    used[i].wait(pool, n)
                    at = bass.ds(n * PER + i * GROUP + GROUP - 1, 1)
                    step(nc.gpsimd.tensor_copy(key[:, i:i + 1], pair_t[:, 1, at]))
                    nc.gpsimd.tensor_scalar(second[:, i * GROUP + GROUP - 1, :], iota[:, :], key[:, i:i + 1], None,
                                            ALU.is_equal).then_inc(hot2[i], 1)

        @block.tensor
        def _(pe):
            for i in range(2):
                used[i].give(pe)
            with pe.Fori(0, blocks * LOOPS) as n:
                for i in range(2):
                    pe.wait_ge(hot[i], n + 1)
                    pe.wait_ge(hot2[i], n + 1)
                    copied[i].wait(pe, n)
                    for t in range(GROUP):
                        slot = i * GROUP + t
                        last = nc.tensor.matmul(banks[i][:, t * P:(t + 1) * P], second[:, slot, :], first[slot][:, :],
                                                start=True, stop=True)
                    last.then_inc(used[i].sem, 1)

        @block.scalar
        def _(act):
            for i in range(2):
                copied[i].give(act)
            for b in range(blocks):
                if b >= 2:
                    act.wait_ge(stored[b % 2], 16 * (b // 2))
                with act.Fori(0, LOOPS) as n:
                    for i in range(2):
                        used[i].wait(act, n + (b * LOOPS + 1))
                        nc.scalar.copy(whole[b % 2][:, :, bass.ds(n * PER + i * GROUP, GROUP)],
                                       banks[i][:, :].rearrange("p (t a) -> p a t", t=GROUP)).then_inc(copied[i].sem, 1)


def expert_stage(nc, io, ident, x1_dram, xn_dram, g_dram, xt_hi, xt_lo, expert, gate, blocks, out):
    T, D = io["x"].shape
    NB = T // P
    KC = D // P
    NH = PEER_HEADS
    DENSE = NB - blocks
    TD = DENSE * P
    WINDOWS = io["peer_down"].shape[0] // P // 2
    HALF = 5
    FIRST = (0, 13, 26, 39, 52, 64)
    BODIES = blocks * NH // 4
    ALONE = WINDOWS - BODIES * 2 * HALF
    assert NH % 4 == 0 and ALONE >= 0 and ALONE % 2 == 0 and TD // 2 <= 512
    held = []
    with ExitStack() as ctx:
        ctx.callback(clear_semaphores, nc, held)

        def sb(name, shape, dt=F32):
            return ctx.enter_context(nc.sbuf_tensor(name, shape, dt))

        def sem(name):
            held.append(nc.alloc_semaphore(name))
            return held[-1]

        ring = [sb(f"ring{i}", [P, D]) for i in range(RING)]
        fg = sb("fg", [P, D])
        xg = sb("xg", [P, D])
        done = sb("done", [P, D])
        xng = sb("xng", [P, D])
        rows = [sb(f"rows{i}", [P, TOPK], U32) for i in range(2)]
        act_in = sb("act_in", [P, TOPK])
        act_out = sb("act_out", [P, TOPK])
        weight = sb("weight", [P, TOPK])
        ss = sb("ss3", [P, 4])
        ssd = sb("ssd", [P, 4, DENSE])
        raw = [sb(f"raw{j}", [P, D]) for j in range(2)]
        dt_hi = [sb(f"dt_hi{j}", [P, KC, P], F32R) for j in range(2)]
        dt_lo = [sb(f"dt_lo{j}", [P, KC, P], F32R) for j in range(2)]
        upr = [sb(f"upr{j}", [P, D]) for j in range(2)]
        up_hi = [[sb(f"up_hi{w}{j}", [P, D], F32R) for j in range(2)] for w in range(2)]
        up_lo = [[sb(f"up_lo{w}{j}", [P, D], F32R) for j in range(2)] for w in range(2)]
        gw = [sb(f"gw{j}", [P, TD]) for j in range(2)]
        pr = [sb(f"pr{j}", [P, TD]) for j in range(2)]
        s_hi = [[sb(f"s_hi{w}{j}", [P, TD], F32R) for j in range(2)] for w in range(2)]
        s_lo = [[sb(f"s_lo{w}{j}", [P, TD], F32R) for j in range(2)] for w in range(2)]
        xo = sb("xo", [P, DENSE, D])
        TR = [ctx.enter_context(nc.psum_tensor(f"tr{i}", [P, 512], F32)) for i in range(2)]
        PB = [ctx.enter_context(nc.psum_tensor(f"pj{i}", [P, 512], F32)) for i in range(2)]
        OB = [ctx.enter_context(nc.psum_tensor(f"ob{i}", [P, 512], F32)) for i in range(4)]
        hv = lambda t: t[:, :].rearrange("p (h d) -> p h d", d=P)

        row_in = [sem(f"x_row_in{i}") for i in range(RING)]
        names = ("rows_set gelu_g weighed ss_done eps_done ln_done rstd_done out_done fg_in "
                 "xg_in xng_in xo_in u_ready cleared norm_start").split()
        e = {n: sem("x_" + n) for n in names}
        read = Count(sem("x_read"), RING)
        adds, stored = Count(sem("x_adds"), 2), Count(sem("x_stored"), 1)
        two = lambda name: [sem(f"x_{name}{j}") for j in range(2)]
        free = lambda name: [Count(sem(f"x_{name}{j}"), 1) for j in range(2)]
        raw_in, upr_in, gw_in = two("raw_in"), two("upr_in"), two("gw_in")
        t_done, hi_done, p_ready = free("t_done"), two("hi_done"), two("p_ready")
        gelu_d, shi_done, uphi_done = free("gelu_d"), two("shi_done"), two("uphi_done")
        lo_done, pg_done, slo_done, uplo_done = free("lo_done"), free("pg_done"), free("slo_done"), free("uplo_done")
        block = ctx.enter_context(nc.Block())
        down_rows, up_rows = io["peer_down"], io["peer_up"]

        @block.sync
        def _(sp):
            def fetch_down(w, j, chunk):
                t_done[j].wait(sp, w)
                sp.dma_start(raw[j][:, :], down_rows[bass.ts(chunk, P), :]).then_inc(raw_in[j], 16)

            def fetch(w, j, chunk):
                pg_done[j].wait(sp, w)
                sp.dma_start(gw[j][:, :], g_dram[bass.ds(chunk, 1), :, :].rearrange("a c t -> c (a t)")).then_inc(
                    gw_in[j], 16)
                uplo_done[j].wait(sp, w)
                sp.dma_start(upr[j][:, :], up_rows[bass.ts(chunk, P), :]).then_inc(upr_in[j], 16)

            for j in range(2):
                fetch_down(0, j, j)
            for j in range(2):
                fetch(0, j, j)
            sp.dma_start(xo[:, :, :], x1_dram[blocks * P:, :].rearrange("(b p) d -> p b d", p=P)).then_inc(
                e["xo_in"], 16)
            sp.dma_start(fg[:, :], io["final_g"].partition_broadcast(P)).then_inc(e["fg_in"], 16)
            with sp.Fori(1, WINDOWS) as w:
                for j in range(2):
                    fetch_down(w, j, w * 2 + j)
                    fetch(w, j, w * 2 + j)
            t_done[0].wait(sp, WINDOWS)
            sp.dma_start(raw[0][:, :], down_rows[0:P, :]).then_inc(raw_in[0], 16)

        @block.gpsimd
        def _(pool):
            turns = pool.alloc_register("turns")

            def counted(count, n):
                pool.reg_mov(turns, n + count.credit)
                pool.wait_ge(e["rows_set"], 1)
                pool.wait_ge(count.sem, turns)

            def gather(table, buf, index, arrived):
                nc.gpsimd.indirect_dma_start(
                    buf[:, :], None, table, bass.IndirectOffsetOnAxis(ap=index, axis=0)).then_inc(arrived, 16)

            def low_part(w, turn, j):
                pool.wait_ge(uphi_done[j], w + 1)
                nc.gpsimd.tensor_tensor(up_lo[turn][j][:, :], upr[j][:, :], up_hi[turn][j][:, :].bitcast(F32),
                                        ALU.subtract).then_inc(uplo_done[j].sem, 1)

            def low_scores(w, turn, j):
                pool.wait_ge(shi_done[j], w + 1)
                nc.gpsimd.tensor_tensor(s_lo[turn][j][:, :], pr[j][:, :], s_hi[turn][j][:, :].bitcast(F32),
                                        ALU.subtract).then_inc(slo_done[j].sem, 1)

            for j in range(2):
                uplo_done[j].give(pool)
                slo_done[j].give(pool)
            with pool.Fori(0, BODIES) as body:
                for half in range(2):
                    for row in range(4 * TOPK):
                        head, k = row // (2 * TOPK), row % (2 * TOPK)
                        g = body * 4 + (half * 2 + head)
                        if k == 0:
                            counted(Count(e["rows_set"]), g + 1)
                        counted(read, g * (2 * TOPK) + (k - RING + 1))
                        gather(down_rows if k < TOPK else up_rows, ring[k % RING],
                               rows[head][:, k % TOPK:k % TOPK + 1], row_in[k % RING])
                        for i in range(HALF):
                            at = half * HALF + i
                            w = body * (2 * HALF) + at
                            if row - FIRST[i] in (9, 10):
                                low_part(w, at % 2, int(row - FIRST[i] == 10))
                            if row == FIRST[i] + 11:
                                low_scores(w, at % 2, 0)
                            if row == FIRST[i + 1] - 1:
                                low_scores(w, at % 2, 1)
            with pool.Fori(BODIES * HALF, WINDOWS // 2) as pair:
                for turn in range(2):
                    for j in range(2):
                        low_part(pair * 2 + turn, turn, j)
                    for j in range(2):
                        low_scores(pair * 2 + turn, turn, j)

        @block.tensor
        def _(pe):
            mm, tp = nc.tensor.matmul, nc.tensor.transpose

            def turn_down(w, j, n_before):
                pe.wait_ge(raw_in[j], w * 16 + 16)
                lo_done[1 - j].wait(pe, n_before)
                for k in range(KC):
                    last = tp(hv(TR[k // 4])[:, k % 4, :], raw[j][:, k * P:(k + 1) * P], ident[:, :])
                last.then_inc(t_done[j].sem, 1)

            def activations(w, j):
                lo_done[j].wait(pe, w + 1)
                gelu_d[1 - j].wait(pe, w + j)
                parts = ((dt_hi, xt_hi), (dt_lo, xt_hi), (dt_hi, xt_lo))
                for k in range(KC):
                    for n, (a, x) in enumerate(parts):
                        for i in range(2):
                            last = mm(PB[i][:, 0:TD // 2], a[j][:, k, :], x[:, k, i * TD // 2:(i + 1) * TD // 2],
                                      start=(k == 0 and n == 0), stop=(k == KC - 1 and n == 2))
                last.then_inc(p_ready[j], 1)

            def outputs(v, turn):
                par = 1 - turn
                for j in range(2):
                    slo_done[j].wait(pe, v)
                    uplo_done[j].wait(pe, v)
                for tb in range(DENSE):
                    adds.wait(pe, v * DENSE + (tb - 1))
                    tok = slice(tb * P, (tb + 1) * P)
                    for half in range(2):
                        d = slice(half * 512, half * 512 + 512)
                        n = 0
                        for j in range(2):
                            for a, u in ((s_hi, up_hi), (s_lo, up_hi), (s_hi, up_lo)):
                                last = mm(OB[(par + tb) % 2 * 2 + half][:, :], a[turn][j][:, tok], u[turn][j][:, d],
                                          start=(n == 0), stop=(n == 5))
                                n += 1
                    last.then_inc(e["u_ready"], 1)

            for j in range(2):
                t_done[j].give(pe)
            pe.wait_ge(e["cleared"], 8)
            turn_down(0, 0, 0)
            with pe.Fori(0, WINDOWS // 2) as pair:
                for turn in range(2):
                    w = pair * 2 + turn
                    turn_down(w, 1, w + 1)
                    activations(w, 0)
                    turn_down(w + 1, 0, w + 1)
                    activations(w, 1)
                    outputs(w, 1 - turn)
            outputs(WINDOWS, 1)

        @block.scalar
        def _(act):
            A = nc.scalar

            def split_down(w, j):
                t_done[j].wait(act, w + 1)
                A.copy(dt_hi[j][:, 0:4, :], hv(TR[0]))
                A.copy(dt_hi[j][:, 4:8, :], hv(TR[1])).then_inc(hi_done[j], 1)

            def gelu(w, j):
                act.wait_ge(p_ready[j], w + 1)
                slo_done[j].wait(act, w)
                for i in range(2):
                    last = A.activation(pr[j][:, i * TD // 2:(i + 1) * TD // 2], PB[i][:, 0:TD // 2], ACT.Gelu)
                last.then_inc(gelu_d[j].sem, 1)

            def split_up(w, turn, j):
                act.wait_ge(upr_in[j], w * 16 + 16)
                A.copy(up_hi[turn][j][:, :], upr[j][:, :]).then_inc(uphi_done[j], 1)

            def split_s(w, turn, j):
                pg_done[j].wait(act, w + 1)
                A.copy(s_hi[turn][j][:, :], pr[j][:, :]).then_inc(shi_done[j], 1)

            def window(w, turn, dots_end=None, g=None):
                split_down(w, 1)
                split_up(w, turn, 0)
                split_up(w, turn, 1)
                if dots_end == "early":
                    gelu_gathered(g)
                gelu(w, 0)
                split_down(w + 1, 0)
                split_s(w, turn, 0)
                gelu(w, 1)
                if dots_end == "late":
                    gelu_gathered(g)
                split_s(w, turn, 1)

            def gelu_gathered(g):
                read.wait(act, g * (2 * TOPK) + TOPK)
                A.activation(act_out[:, :], act_in[:, :], ACT.Gelu).then_inc(e["gelu_g"], 1)

            def root(n):
                act.wait_ge(e["eps_done"], n)
                A.activation(ss[:, 2:3], ss[:, 1:2], ACT.Ln).then_inc(e["ln_done"], 1)
                act.wait_ge(e["ln_done"], n)
                A.activation(ss[:, 3:4], ss[:, 2:3], ACT.Exp, scale=-0.5).then_inc(e["rstd_done"], 1)

            def load_normed(b):
                act.dma_start(xng[:, :], xn_dram[bass.ts(b, P), :]).then_inc(e["xng_in"], 16)

            def load(b):
                act.dma_start(xg[:, :], x1_dram[bass.ts(b, P), :]).then_inc(e["xg_in"], 16)

            for j in range(2):
                gelu_d[j].give(act)
            stored.give(act)
            split_down(0, 0)
            load_normed(0)
            load(0)
            with act.Fori(0, blocks) as b:
                with act.Fori(0, NH // 4) as part:
                    for i in range(2 * HALF):
                        body = b * (NH // 4) + part
                        g = body * 4 + i // HALF * 2
                        window(body * (2 * HALF) + i, i % 2, {1: "early", 3: "late"}.get(i % HALF), g + i % HALF // 3)
                act.wait_ge(e["norm_start"], b + 1)
                load_normed(b + 1)
                stored.wait(act, b * 16)
                A.activation(done[:, :], xg[:, :], ACT.Square, accum_out=ss[:, 0:1]).then_inc(e["ss_done"], 1)
                root(b + 1)
                act.wait_ge(e["out_done"], b + 1)
                load(b + 1)
                act.dma_start(out[bass.ts(b, P), :], done[:, :]).then_inc(stored.sem, 16)
            with act.Fori(BODIES * HALF, WINDOWS // 2) as pair:
                for turn in range(2):
                    window(pair * 2 + turn, turn)
            act.wait_ge(e["xng_in"], blocks * 16 + 16)
            act.wait_ge(e["xg_in"], blocks * 16 + 16)
            for t in range(DENSE):
                adds.wait(act, DENSE * WINDOWS + t + 1)
                last = A.activation(ring[t][:, :], xo[:, t, :], ACT.Square, accum_out=ssd[:, 0, t:t + 1])
            last.then_inc(e["ss_done"], 1)
            act.wait_ge(e["eps_done"], blocks + 1)
            A.activation(ssd[:, 2, :], ssd[:, 1, :], ACT.Ln).then_inc(e["ln_done"], 1)
            act.wait_ge(e["ln_done"], blocks + 1)
            A.activation(ssd[:, 3, :], ssd[:, 2, :], ACT.Exp, scale=-0.5).then_inc(e["rstd_done"], 1)
            for t in range(DENSE):
                act.wait_ge(e["out_done"], blocks + t + 1)
                act.dma_start(out[(blocks + t) * P:(blocks + t + 1) * P, :], xo[:, t, :]).then_inc(stored.sem, 16)
            stored.wait(act, NB * 16)

        @block.vector
        def _(dve):
            V = nc.vector

            def set_rows(g, turn):
                V.tensor_copy(rows[turn][:, :], expert[:, bass.ds(g * TOPK, TOPK)]).then_inc(e["rows_set"], 1)

            def arrived(g, n):
                dve.wait_ge(row_in[n % RING], g * (16 * 2 * TOPK // RING) + (16 * (n // RING) + 16))
                return ring[n % RING][:, :]

            def dot(g, k):
                slot = arrived(g, k)
                V.scalar_tensor_tensor(slot, slot, 1.0, xng[:, :], ALU.mult, ALU.mult,
                                       accum_out=act_in[:, k:k + 1]).then_inc(read.sem, 1)

            def add_row(g, k):
                slot = arrived(g, TOPK + k)
                if k > 0:
                    read.wait(dve, g * (2 * TOPK) + (TOPK + k))
                V.scalar_tensor_tensor(xg[:, :], slot, weight[:, k:k + 1], xg[:, :], ALU.mult, ALU.add).then_inc(
                    read.sem, 1)

            def split_down(w, j):
                dve.wait_ge(hi_done[j], w + 1)
                for i in range(2):
                    last = V.tensor_tensor(dt_lo[j][:, 4 * i:4 * i + 4, :], hv(TR[i]),
                                           dt_hi[j][:, 4 * i:4 * i + 4, :].bitcast(F32), ALU.subtract)
                last.then_inc(lo_done[j].sem, 1)

            def by_gate(w, j):
                dve.wait_ge(gw_in[j], w * 16 + 16)
                gelu_d[j].wait(dve, w + 1)
                V.tensor_tensor(pr[j][:, :], pr[j][:, :], gw[j][:, :], ALU.mult).then_inc(pg_done[j].sem, 1)

            def add_out(v, tb, par):
                if tb == 0:
                    dve.wait_ge(e["xo_in"], 16)
                dve.wait_ge(e["u_ready"], v * DENSE + (tb + 1))
                for half in range(2):
                    d = slice(half * 512, half * 512 + 512)
                    last = V.tensor_tensor(xo[:, tb, d], OB[(par + tb) % 2 * 2 + half][:, :], xo[:, tb, d], ALU.add)
                last.then_inc(adds.sem, 1)

            def window(w, turn, rows=()):
                rows = list(rows)

                def some(n):
                    for row in rows[:n]:
                        row()
                    del rows[:n]

                split_down(w, 1)
                some(6)
                split_down(w + 1, 0)
                by_gate(w, 0)
                some(3)
                by_gate(w, 1)
                some(1)
                for tb in range(DENSE):
                    add_out(w, tb, turn)
                    some(1)

            def gathered_row(b, g, head, k):
                if k == 0:
                    dve.wait_ge(e["xng_in"], b * 16 + 16)
                if k < TOPK:
                    dot(g, k)
                    return
                k -= TOPK
                if k == 0:
                    dve.wait_ge(e["gelu_g"], g + 1)
                    V.tensor_tensor(weight[:, :], act_out[:, :], gate[:, bass.ds(g * TOPK, TOPK)],
                                    ALU.mult).then_inc(e["weighed"], 1)
                    dve.wait_ge(e["xg_in"], b * 16 + 16)
                    dve.wait_ge(e["weighed"], g + 1)
                add_row(g, k)
                if k == TOPK - 1:
                    read.wait(dve, g * (2 * TOPK) + 2 * TOPK)
                    set_rows(g + 2, head)

            def finish(n):
                dve.wait_ge(e["ss_done"], n)
                V.tensor_scalar(ss[:, 1:2], ss[:, 0:1], 1.0 / D, EPS, ALU.mult, ALU.add).then_inc(e["eps_done"], 1)
                dve.wait_ge(e["rstd_done"], n)
                V.scalar_tensor_tensor(done[:, :], xg[:, :], ss[:, 3:4], fg[:, :], ALU.mult, ALU.mult).then_inc(
                    e["out_done"], 1)

            for j in range(2):
                for t in (s_hi[1][j], s_lo[1][j], up_hi[1][j], up_lo[1][j]):
                    V.memset(t[:, :].bitcast(F32), 0.0).then_inc(e["cleared"], 1)
            read.give(dve)
            adds.give(dve)
            for j in range(2):
                lo_done[j].give(dve)
                pg_done[j].give(dve)
            dve.wait_ge(e["fg_in"], 16)
            set_rows(0, 0)
            set_rows(1, 1)
            split_down(0, 0)
            with dve.Fori(0, blocks) as b:
                with dve.Fori(0, NH // 4) as part:
                    for i in range(2 * HALF):
                        body = b * (NH // 4) + part
                        g = body * 4 + i // HALF * 2
                        first, end = FIRST[i % HALF], FIRST[i % HALF + 1]
                        window(body * (2 * HALF) + i, i % 2, [
                            lambda n=n: gathered_row(b, g + n // (2 * TOPK), n // (2 * TOPK), n % (2 * TOPK))
                            for n in range(first, end)])
                V.tensor_copy(weight[:, 0:1], xg[:, 0:1]).then_inc(e["norm_start"], 1)
                finish(b + 1)
            with dve.Fori(BODIES * HALF, WINDOWS // 2) as pair:
                for turn in range(2):
                    window(pair * 2 + turn, turn)
            for tb in range(DENSE):
                add_out(WINDOWS, tb, 0)
            dve.wait_ge(e["ss_done"], blocks + 1)
            V.tensor_scalar(ssd[:, 1, :], ssd[:, 0, :], 1.0 / D, EPS, ALU.mult, ALU.add).then_inc(e["eps_done"], 1)
            dve.wait_ge(e["rstd_done"], blocks + 1)
            for t in range(DENSE):
                V.scalar_tensor_tensor(xo[:, t, :], xo[:, t, :], ssd[:, 3, t:t + 1], fg[:, :], ALU.mult,
                                       ALU.mult).then_inc(e["out_done"], 1)


def build(nc, io, out):
    T, D = io["x"].shape
    NB = T // P
    N = PEER_HEADS * TOPK
    gathered = 3
    dense = (NB - gathered) * P
    y_dram = nc.dram_tensor("y_scratch", (NB, P, D), F32, kind="Internal").ap()
    x1_dram = nc.dram_tensor("x1_scratch", (T, D), F32, kind="Internal").ap()
    xn_dram = nc.dram_tensor("xn_scratch", (T, D), F32, kind="Internal").ap()
    g_dram = nc.dram_tensor("gate_scratch", (P, P, dense), F32, kind="Internal").ap()
    with ExitStack() as ctx:
        ident = ctx.enter_context(nc.sbuf_tensor("ident", [P, P], F32))
        front = ctx.enter_context(ExitStack())
        weights = front.enter_context(nc.sbuf_tensor("weights", [P, D // P, io["w_in"].shape[1]], F32, side="right"))
        mix_stage(nc, io, y_dram, weights, ident)
        xt_hi = ctx.enter_context(nc.sbuf_tensor("xt_hi", [P, D // P, dense], F32R))
        xt_lo = ctx.enter_context(nc.sbuf_tensor("xt_lo", [P, D // P, dense], F32R))
        expert = ctx.enter_context(nc.sbuf_tensor("expert", [P, gathered * N + 2 * TOPK], U32))
        gate = ctx.enter_context(nc.sbuf_tensor("gate", [P, gathered * N], F32))
        with ExitStack() as inner:
            pair_t = inner.enter_context(nc.sbuf_tensor("pair_t", [P, 3, dense], F32))
            router_stage(nc, io, weights, ident, y_dram, x1_dram, xn_dram, gathered, xt_hi, xt_lo, expert, gate,
                         pair_t)
            front.close()
            pair_stage(nc, io, g_dram, pair_t, NB - gathered)
        expert_stage(nc, io, ident, x1_dram, xn_dram, g_dram, xt_hi, xt_lo, expert, gate, gathered, out)


def shape_constants(np, T):
    H, half_w = 4, 64
    gamma = 1.0 - 2.0 ** (-5.0 - np.arange(H, dtype=np.float64))
    inv = (np.float64(10000.0) ** (-np.arange(half_w, dtype=np.float64) / half_w)).astype(np.float32)
    angle = (np.arange(T, dtype=np.float32)[:, None] * inv[None, :]).astype(np.float64)
    place = np.arange(T) % P
    q_decay = gamma[None, :] ** (place[:, None] + 1.0)
    k_decay = gamma[None, :] ** (P - 1.0 - place[:, None]) * float(P) ** -0.5
    trig = np.stack([f(angle)[:, None, :] * d[:, :, None] for d in (q_decay, k_decay) for f in (np.cos, np.sin)], 1)
    l, m = np.arange(P)[None, :], np.arange(P)[:, None]
    same, past = l // 64 == m // 64, l // 64 > m // 64
    power = np.where(same, np.abs(l - m), l - m) - (l + 1.0) - (P - 1.0 - m)
    decay = np.where((same | past)[None], gamma[:, None, None] ** power[None], 0.0)
    one = np.float32
    return {
        "ident": np.eye(P, dtype=one),
        "iota": np.tile(np.arange(P, dtype=one), (P, 1)),
        "trig": trig.reshape(T, 4, H * half_w).astype(one),
        "decay_t": np.ascontiguousarray(decay.transpose(1, 0, 2)).astype(one),
        "select": np.ascontiguousarray(np.repeat(np.eye(H, dtype=one)[:, :, None], P, axis=2)),
        "reset": np.tile((np.arange(P) % 64 != 0).astype(one), (H, 1)),
        "half": np.stack([np.arange(P) < 64, np.arange(P) >= 64], 1).astype(one),
    }


_LAYER = ["norm1_g", "w_in", "ret_norm_g", "m_conv_w", "m_conv_b", "m_wq", "m_wk", "m_b_i", "m_b_f", "m_norm_g",
          "m_skip", "w_out", "norm2_g", "peer_wq", "peer_keys", "peer_down", "peer_up"]


def kernel(**inputs):
    import numpy as np
    import concourse.bacc as bacc
    from concourse.bass_utils import run_bass_kernel_spmd

    x = np.ascontiguousarray(inputs["x"])
    arrays = {"x": x[0], "final_g": np.ascontiguousarray(inputs["final_g"])}
    for name in _LAYER:
        arrays[name] = np.ascontiguousarray(inputs[name])[0]
    arrays.update(shape_constants(np, x.shape[1]))
    nc = bacc.Bacc("TRN2", target_bir_lowering=False, num_devices=1)
    io = {name: nc.dram_tensor(f"in_{name}", a.shape, mybir.dt.from_np(a.dtype), kind="ExternalInput").ap()
          for name, a in arrays.items()}
    out = nc.dram_tensor("out_x", x.shape[1:], F32, kind="ExternalOutput").ap()
    build(nc, io, out)
    r = run_bass_kernel_spmd(nc, [{f"in_{n}": a for n, a in arrays.items()}], core_ids=[0])
    return r.results[0]["out_x"].reshape(x.shape)
```
